# Optimizing a Trainium2 kernel written in Bass

```python
import jax
import jax.numpy as jnp
from jax import lax
import numpy as np

D_MODEL = 1024
BATCH = 1
SEQ = 512
DEPTH = 2

GRID_W = 64
CTX_LEN = 256
HEAD_DIM = 64
N_GROUPS = 4
GROUP_WIDTH = D_MODEL // N_GROUPS
MIX_WIDTH = N_GROUPS * GROUP_WIDTH
N_HEADS = GROUP_WIDTH // HEAD_DIM
N_KV_HEADS = N_HEADS // 2
KV_WIDTH = N_KV_HEADS * HEAD_DIM
WIN = 128
BLOCK = 128
NA_ROWS = 8
NA_COLS = 16
HGRN_CHUNK = 64
D_FF = 256 * ((8 * D_MODEL // 3 + 255) // 256)
CONV_W = 3
ROPE_BASE = 10000.0
ALPHA = (2 * DEPTH) ** 0.25
BETA = (8 * DEPTH) ** -0.25
EPS = 1e-6
IN_SPLIT = (GROUP_WIDTH, KV_WIDTH, KV_WIDTH,
            GROUP_WIDTH, KV_WIDTH, KV_WIDTH,
            GROUP_WIDTH, GROUP_WIDTH, GROUP_WIDTH, GROUP_WIDTH, GROUP_WIDTH,
            GROUP_WIDTH, GROUP_WIDTH, GROUP_WIDTH)
IN_WIDTH = sum(IN_SPLIT)

kernel_name = 'hybrid_parallel_groups_dit_block'

def _layer_norm(x, g, b):
    xf = x.astype(jnp.float32)
    mu = jnp.mean(xf, -1, keepdims=True)
    var = jnp.mean(jnp.square(xf - mu), -1, keepdims=True)
    return ((xf - mu) * lax.rsqrt(var + EPS) * g + b).astype(x.dtype)

def _rms_norm(x, g):
    xf = x.astype(jnp.float32)
    return (xf * lax.rsqrt(jnp.mean(jnp.square(xf), -1, keepdims=True) + EPS) * g).astype(x.dtype)

def _heads(a):
    return a.reshape(a.shape[0], a.shape[1], -1, HEAD_DIM)

def _split_cols(p):
    return jnp.split(p, np.cumsum(IN_SPLIT)[:-1].tolist(), axis=-1)

def _axial_rope_tables(n):
    t = jnp.arange(n)
    pos = jnp.stack([t // GRID_W, t % GRID_W], -1).astype(jnp.float32)
    n_freq = HEAD_DIM // 4
    inv = ROPE_BASE ** (-jnp.arange(n_freq, dtype=jnp.float32) / n_freq)
    ang = pos[:, :, None] * inv
    return jnp.cos(ang), jnp.sin(ang)

def _rope2d(x, cos, sin):
    B, S, H, D = x.shape
    xa = x.reshape(B, S, H, 2, 2, D // 4)
    x1, x2 = xa[..., 0, :], xa[..., 1, :]
    cs, sn = cos[:, None], sin[:, None]
    out = jnp.stack([x1 * cs - x2 * sn, x2 * cs + x1 * sn], axis=-2)
    return out.reshape(B, S, H, D).astype(x.dtype)

def _dense_attn(q, k, v, sink=None):
    B, T, H, dh = q.shape
    kvh = k.shape[2]
    g = H // kvh
    n_k = k.shape[1]
    s = jnp.einsum('btkgd,bskd->bkgts', q.reshape(B, T, kvh, g, dh), k).astype(jnp.float32) * dh ** -0.5
    if sink is not None:
        s = jnp.concatenate([s, jnp.broadcast_to(sink.astype(jnp.float32).reshape(1, kvh, g, 1, 1), (B, kvh, g, T, 1))], -1)
    p = jax.nn.softmax(s, -1)[..., :n_k].astype(v.dtype)
    return jnp.einsum('bkgts,bskd->btkgd', p, v).reshape(B, T, H * dh)

def _window_attn_latent(q, k, v, k_ctx, v_ctx, sink):
    B, S, H, dh = q.shape
    kvh = k.shape[2]
    g = H // kvh
    nb = S // BLOCK
    n_ctx = k_ctx.shape[1]
    qb = q.reshape(B, nb, BLOCK, kvh, g, dh)

    def band(a):
        ap = jnp.pad(a, ((0, 0), (WIN, WIN), (0, 0), (0, 0))).reshape(B, nb + 2, BLOCK, kvh, dh)
        return jnp.concatenate([ap[:, :-2], ap[:, 1:-1], ap[:, 2:]], axis=2)

    kb, vb = band(k), band(v)
    qpos = jnp.arange(nb)[:, None] * BLOCK + jnp.arange(BLOCK)[None]
    kpos = jnp.arange(nb)[:, None] * BLOCK - WIN + jnp.arange(3 * BLOCK)[None]
    kp = kpos[:, None, :]
    valid = (jnp.abs(qpos[:, :, None] - kp) <= WIN) & (kp >= 0) & (kp < S)
    scale = dh ** -0.5
    s_loc = jnp.einsum('bnqkgd,bnjkd->bkgnqj', qb, kb).astype(jnp.float32) * scale
    s_loc = jnp.where(valid, s_loc, -jnp.inf)
    s_ctx = jnp.einsum('bnqkgd,bckd->bkgnqc', qb, k_ctx).astype(jnp.float32) * scale
    s_sink = jnp.broadcast_to(sink.astype(jnp.float32).reshape(1, kvh, g, 1, 1, 1), (B, kvh, g, nb, BLOCK, 1))
    p = jax.nn.softmax(jnp.concatenate([s_loc, s_ctx, s_sink], -1), axis=-1).astype(v.dtype)
    n_loc = 3 * BLOCK
    o = (jnp.einsum('bkgnqj,bnjkd->bnqkgd', p[..., :n_loc], vb)
         + jnp.einsum('bkgnqc,bckd->bnqkgd', p[..., n_loc:n_loc + n_ctx], v_ctx))
    return o.reshape(B, S, H * dh)

def _global_attn_latent(q, k, v, k_ctx, v_ctx):
    B, S, H, dh = q.shape
    kvh = k.shape[2]
    g = H // kvh
    nb = S // BLOCK
    qb = q.reshape(B, nb, BLOCK, kvh, g, dh).transpose(1, 0, 2, 3, 4, 5)
    k_all = jnp.concatenate([k, k_ctx], 1)
    v_all = jnp.concatenate([v, v_ctx], 1)
    scale = dh ** -0.5

    def one_block(q_blk):
        s = jnp.einsum('bqkgd,bskd->bkgqs', q_blk, k_all).astype(jnp.float32) * scale
        p = jax.nn.softmax(s, -1).astype(v_all.dtype)
        return jnp.einsum('bkgqs,bskd->bqkgd', p, v_all)

    o = lax.map(one_block, qb)
    return o.transpose(1, 0, 2, 3, 4, 5).reshape(B, S, H * dh)

def _neigh_attn_latent(q, k, v, k_ctx, v_ctx, rpb):
    B, S, H, dh = q.shape
    rows = S // GRID_W
    kr = min(NA_ROWS, rows)
    qg = q.reshape(B, rows, GRID_W, H, dh)
    kg = k.reshape(B, rows, GRID_W, H, dh)
    vg = v.reshape(B, rows, GRID_W, H, dh)
    r = jnp.arange(rows)
    r0 = jnp.clip(r - kr // 2, 0, rows - kr)
    row_idx = r0[:, None] + jnp.arange(kr)[None]
    k_nb = kg[:, row_idx]
    v_nb = vg[:, row_idx]
    col = jnp.arange(GRID_W)
    c0 = jnp.clip(col - NA_COLS // 2, 0, GRID_W - NA_COLS)
    col_ok = (col[None] >= c0[:, None]) & (col[None] < c0[:, None] + NA_COLS)
    roff = row_idx - r[:, None] + (NA_ROWS - 1)
    coff = jnp.clip(col[None] - col[:, None], -(NA_COLS - 1), NA_COLS - 1) + (NA_COLS - 1)
    bias = rpb[:, roff[:, None, :, None], coff[None, :, None, :]]
    scale = dh ** -0.5
    s_loc = jnp.einsum('brqhd,brjchd->bhrqjc', qg, k_nb).astype(jnp.float32) * scale + bias.astype(jnp.float32)
    s_loc = jnp.where(col_ok[:, None, :], s_loc, -jnp.inf).reshape(B, H, rows, GRID_W, kr * GRID_W)
    s_ctx = jnp.einsum('brqhd,bthd->bhrqt', qg, k_ctx).astype(jnp.float32) * scale
    p = jax.nn.softmax(jnp.concatenate([s_loc, s_ctx], -1), axis=-1).astype(v.dtype)
    n_loc = kr * GRID_W
    p_loc = p[..., :n_loc].reshape(B, H, rows, GRID_W, kr, GRID_W)
    o = (jnp.einsum('bhrqjc,brjchd->brqhd', p_loc, v_nb)
         + jnp.einsum('bhrqt,bthd->brqhd', p[..., n_loc:], v_ctx))
    return o.reshape(B, S, H * dh)

def _hgrn_scan(q, k, v, logf, s0, with_output):
    B, T, H, DK = q.shape
    DV = v.shape[-1]
    L = HGRN_CHUNK
    n = T // L
    tril = jnp.tril(jnp.ones((L, L), dtype=bool))[None, :, :, None, None]

    def chunks(a):
        return a.reshape(B, n, L, H, a.shape[-1]).swapaxes(0, 1)

    def step(s, inp):
        qc, kc, vc, gc = inp
        b = jnp.cumsum(gc, axis=1)
        b_last = b[:, -1]
        s_new = jnp.exp(b_last)[..., None] * s + jnp.einsum('blhk,blhv->bhkv', kc * jnp.exp(b_last[:, None] - b), vc)
        if not with_output:
            return s_new, None
        o_inter = jnp.einsum('blhk,bhkv->blhv', qc * jnp.exp(b), s)
        diff = b[:, :, None] - b[:, None, :]
        dec = jnp.where(tril, jnp.exp(jnp.where(tril, diff, 0.0)), 0.0)
        a = jnp.sum(qc[:, :, None] * kc[:, None, :] * dec, axis=-1)
        o_intra = jnp.einsum('btsh,bshv->bthv', a, vc)
        return s_new, o_inter + o_intra

    s_fin, o = lax.scan(step, s0, (chunks(q), chunks(k), chunks(v), chunks(logf)))
    if with_output:
        o = o.swapaxes(0, 1).reshape(B, T, H, DV)
    return s_fin, o

def _hgrn_mixer(xs, cs, lb, onorm, need_ctx):
    q_x, i_x, zf_fx, zf_bx, g_x = xs
    q_c, i_c, zf_fc, zf_bc, g_c = cs
    B = q_x.shape[0]
    f32 = jnp.float32
    qh_x, ih_x = _heads(jax.nn.silu(q_x.astype(f32))), _heads(i_x.astype(f32))
    qh_c, ih_c = _heads(jax.nn.silu(q_c.astype(f32))), _heads(i_c.astype(f32))

    def gates(zf, lbd):
        f = lbd + (1.0 - lbd) * jax.nn.sigmoid(zf.astype(f32))
        return _heads(1.0 - f), _heads(jnp.log(f))

    outs_x, outs_c = [], []
    for d, (zf_x, zf_c) in enumerate(((zf_fx, zf_fc), (zf_bx, zf_bc))):
        k_x, lf_x = gates(zf_x, lb[d])
        k_c, lf_c = gates(zf_c, lb[d])
        lat = (qh_x, k_x, ih_x, lf_x)
        con = (qh_c, k_c, ih_c, lf_c)
        if d == 1:
            lat = tuple(a[:, ::-1] for a in lat)
            con = tuple(a[:, ::-1] for a in con)
        s0 = jnp.zeros((B, N_HEADS, HEAD_DIM, HEAD_DIM), f32)
        s_ctx, o_ctx = _hgrn_scan(*con, s0, need_ctx)
        _, o_lat = _hgrn_scan(*lat, s_ctx, True)
        if d == 1:
            o_lat = o_lat[:, ::-1]
            if need_ctx:
                o_ctx = o_ctx[:, ::-1]
        outs_x.append(o_lat)
        outs_c.append(o_ctx)

    def readout(o, gate):
        y = _rms_norm(o, onorm.reshape(N_HEADS, HEAD_DIM).astype(f32))
        y = y.reshape(o.shape[0], o.shape[1], GROUP_WIDTH) * jax.nn.silu(gate.astype(f32))
        return y.astype(gate.dtype)

    out_x = readout(outs_x[0] + outs_x[1], g_x)
    out_c = readout(outs_c[0] + outs_c[1], g_c) if need_ctx else None
    return out_x, out_c

def _token_mixers(px, pc, cos, sin, sink, qk_gain, lb, onorm, rpb, need_ctx):
    (qa, ka, va, qb, kb, vb, qc, ic, fcf, fcb, gc, qd, kd, vd) = _split_cols(px)
    (qa_c, ka_c, va_c, qb_c, kb_c, vb_c, qc_c, ic_c, fcf_c, fcb_c, gc_c, qd_c, kd_c, vd_c) = _split_cols(pc)
    ka_c, va_c = _heads(ka_c), _heads(va_c)
    o_a = _window_attn_latent(_rope2d(_heads(qa), cos, sin), _rope2d(_heads(ka), cos, sin), _heads(va), ka_c, va_c, sink)
    nq = lambda a: _rms_norm(_heads(a), qk_gain[0])
    nk = lambda a: _rms_norm(_heads(a), qk_gain[1])
    kb_c, vb_c = nk(kb_c), _heads(vb_c)
    o_b = _global_attn_latent(_rope2d(nq(qb), cos, sin), _rope2d(nk(kb), cos, sin), _heads(vb), kb_c, vb_c)
    o_c, oc_ctx = _hgrn_mixer((qc, ic, fcf, fcb, gc), (qc_c, ic_c, fcf_c, fcb_c, gc_c), lb, onorm, need_ctx)
    kd_c, vd_c = _heads(kd_c), _heads(vd_c)
    o_d = _neigh_attn_latent(_heads(qd), _heads(kd), _heads(vd), kd_c, vd_c, rpb)
    mix_x = jnp.concatenate([o_a, o_b, o_c, o_d], -1)
    mix_c = None
    if need_ctx:
        mix_c = jnp.concatenate([
            _dense_attn(_heads(qa_c), ka_c, va_c, sink),
            _dense_attn(nq(qb_c), kb_c, vb_c),
            oc_ctx,
            _dense_attn(_heads(qd_c), kd_c, vd_c)], -1)
    return mix_x, mix_c

def _conv_ffn(h, w_up, conv_w, conv_b, w_down):
    u = h @ w_up
    up = jnp.pad(u, ((0, 0), (1, 1), (0, 0)))
    u = up[:, :-2] * conv_w[0] + up[:, 1:-1] * conv_w[1] + up[:, 2:] * conv_w[2] + conv_b
    a, v = jnp.split(u, 2, axis=-1)
    return (jax.nn.silu(a) * v) @ w_down

def setup_inputs(seed: int = 0) -> dict:
    key = jax.random.key(seed)
    ks = jax.random.split(key, 19)
    f32 = jnp.float32
    nrm = lambda k, shape, s: jax.random.normal(k, shape, f32) * s
    return {
        'x': nrm(ks[0], (BATCH, SEQ, D_MODEL), 1.0),
        'c': nrm(ks[1], (BATCH, D_MODEL), 1.0),
        'ctx': nrm(ks[2], (BATCH, CTX_LEN, D_MODEL), 1.0),
        'c_ctx': nrm(ks[3], (D_MODEL,), 1.0),
        'w_mod': nrm(ks[4], (DEPTH, D_MODEL, 6 * D_MODEL), 0.5 * D_MODEL ** -0.5),
        'b_mod': nrm(ks[5], (DEPTH, 6 * D_MODEL), 0.02),
        'w_in': nrm(ks[6], (DEPTH, D_MODEL, IN_WIDTH), D_MODEL ** -0.5),
        'w_out': nrm(ks[7], (DEPTH, MIX_WIDTH, D_MODEL), BETA * MIX_WIDTH ** -0.5),
        'ln_g': 1.0 + nrm(ks[8], (DEPTH, 2, D_MODEL), 0.02),
        'ln_b': nrm(ks[9], (DEPTH, 2, D_MODEL), 0.02),
        'attn_sink': nrm(ks[10], (DEPTH, N_HEADS), 1.0),
        'qk_norm': 1.0 + nrm(ks[11], (DEPTH, 2, HEAD_DIM), 0.02),
        'hgrn_lb_logits': nrm(ks[12], (2, DEPTH, GROUP_WIDTH), 1.0),
        'hgrn_onorm': 1.0 + nrm(ks[13], (DEPTH, GROUP_WIDTH), 0.02),
        'na_rpb': nrm(ks[14], (DEPTH, N_HEADS, 2 * NA_ROWS - 1, 2 * NA_COLS - 1), 0.1),
        'ffn_w_up': nrm(ks[15], (DEPTH, D_MODEL, 2 * D_FF), D_MODEL ** -0.5),
        'ffn_conv_w': nrm(ks[16], (DEPTH, CONV_W, 2 * D_FF), CONV_W ** -0.5),
        'ffn_conv_b': nrm(ks[17], (DEPTH, 2 * D_FF), 0.02),
        'ffn_w_down': nrm(ks[18], (DEPTH, D_FF, D_MODEL), BETA * D_FF ** -0.5),
    }

def reference(x, c, ctx, c_ctx, w_mod, b_mod, w_in, w_out, ln_g, ln_b, attn_sink, qk_norm,
              hgrn_lb_logits, hgrn_onorm, na_rpb, ffn_w_up, ffn_conv_w, ffn_conv_b, ffn_w_down):
    cos, sin = _axial_rope_tables(x.shape[1])
    p_lb = jax.nn.softmax(hgrn_lb_logits.astype(jnp.float32), axis=1)
    lb_all = jnp.cumsum(p_lb, axis=1) - p_lb[:, :1]
    s_c = jax.nn.silu(c)
    s_cc = jax.nn.silu(c_ctx)
    h_x, h_c = x, ctx
    for l in range(DEPTH):
        need_ctx = l < DEPTH - 1
        mod_x = (s_c @ w_mod[l] + b_mod[l])[:, None, :]
        mod_c = s_cc @ w_mod[l] + b_mod[l]
        sa_x, ca_x, ga_x, sf_x, cf_x, gf_x = jnp.split(mod_x, 6, axis=-1)
        sa_c, ca_c, ga_c, sf_c, cf_c, gf_c = jnp.split(mod_c, 6, axis=-1)
        px = (h_x * (1.0 + ca_x) + sa_x) @ w_in[l]
        pc = (h_c * (1.0 + ca_c) + sa_c) @ w_in[l]
        mix_x, mix_c = _token_mixers(px, pc, cos, sin, attn_sink[l], qk_norm[l], lb_all[:, l],
                                     hgrn_onorm[l], na_rpb[l], need_ctx)
        h_x = _layer_norm(ALPHA * h_x + ga_x * (mix_x @ w_out[l]), ln_g[l, 0], ln_b[l, 0])
        f_x = _conv_ffn(h_x * (1.0 + cf_x) + sf_x, ffn_w_up[l], ffn_conv_w[l], ffn_conv_b[l], ffn_w_down[l])
        h_x = _layer_norm(ALPHA * h_x + gf_x * f_x, ln_g[l, 1], ln_b[l, 1])
        if need_ctx:
            h_c = _layer_norm(ALPHA * h_c + ga_c * (mix_c @ w_out[l]), ln_g[l, 0], ln_b[l, 0])
            f_c = _conv_ffn(h_c * (1.0 + cf_c) + sf_c, ffn_w_up[l], ffn_conv_w[l], ffn_conv_b[l], ffn_w_down[l])
            h_c = _layer_norm(ALPHA * h_c + gf_c * f_c, ln_g[l, 1], ln_b[l, 1])
    return h_x


_drawn_inputs = setup_inputs


def setup_inputs(seed=0):
    import zlib

    import numpy as np

    out = dict(_drawn_inputs(seed))
    spreads = {}
    factors = {'ctx': 6.257,
     'c_ctx': 2.754,
     'b_mod': 5.721,
     'attn_sink': 64.0,
     'qk_norm': 8.0,
     'hgrn_lb_logits': 8.0,
     'hgrn_onorm': 47.695,
     'na_rpb': 64.0,
     'ffn_conv_b': 8.0}
    for name, (base, spread) in spreads.items():
        noise = np.random.default_rng([zlib.crc32(name.encode()), seed]).standard_normal(out[name].shape)
        drawn = base * np.exp(spread * noise) if base else spread * noise
        out[name] = jnp.asarray(drawn.astype(out[name].dtype))
    for name, factor in factors.items():
        out[name] = (out[name] * factor).astype(out[name].dtype)
    return out
```

```python
import concourse.bass as bass
from concourse import mybir
from contextlib import ExitStack
import math

D_MODEL, SEQ, CTX, DEPTH = 1024, 512, 256, 2
P = 128
KT = D_MODEL // P
TOK = SEQ + CTX
NLT, NCT = SEQ // P, CTX // P
NT = NLT + NCT
HEADS, HD = 4, 64
D_FF = 256 * ((8 * D_MODEL // 3 + 255) // 256)
FT = D_FF // P
ALPHA = (2 * DEPTH) ** 0.25
EPS = 1e-6
SCALE = HD ** -0.5
NEG = -1e30
LEVELS = 7
GRID_W, NA_ROWS, NA_COLS = 64, 8, 16
BIAS_ROWS = 2 * NA_ROWS - 2

SLOT = 2048
RING = 4
KDN = 4
DN_GROUPS = -(-FT // KDN)
QA, KVA, QB, KVB, QC, IC, FCF, FCB, GC, QD, KD, VD = range(12)
IN_ORDER = (QC, GC, IC, FCF, FCB, QA, KVA, QB, KVB, QD, KD, VD)
FEATURE = (QC, FCF, FCB, QD, KD)
LATENT_ONLY = (QA, QB, QC, GC, QD)
MOD_FIRST = 8


def weight_stream():
    s = [("mod", 0, i, 0) for i in range(MOD_FIRST)]
    for l in range(DEPTH):
        extra = list(range(MOD_FIRST, 24)) if l == 0 else []
        for n, i in enumerate(IN_ORDER):
            s.append(("in", l, i, 0))
            for _ in range(2 if n < 4 else 1):
                if extra:
                    s.append(("mod", 0, extra.pop(0), 0))
        assert not extra
        s += [("out", l, n, g) for n in range(2) for g in range(KT // KDN)]
        nxt = list(range(24)) if l + 1 < DEPTH else []
        for j in range(FT):
            s.append(("up", l, j, 0))
            for _ in range(2 if j < 2 else 1):
                if nxt:
                    s.append(("mod", l + 1, nxt.pop(0), 0))
        assert not nxt
        s += [("down", l, n, g) for n in range(2) for g in range(DN_GROUPS)]
    return s


STREAM = weight_stream()
SLOT_AT = {key: n for n, key in enumerate(STREAM)}


def hybrid_backbone(nc, weights, x, ctx_in, consts, masks, params, bias_d, ln_rows, out):
    f32, u8 = mybir.dt.float32, mybir.dt.uint8
    ALU, ACT, AX = mybir.AluOpType, mybir.ActivationFunctionType, mybir.AxisListType.X
    stack = ExitStack()

    def sb(name, cols, dt=f32):
        return stack.enter_context(nc.sbuf_tensor(name, [P, cols], dt))

    def sem(name):
        return stack.enter_context(nc.semaphore(name))

    with stack:
        H = sb("H", NT * D_MODEL)
        X = sb("X", KT * TOK)
        U = sb("U", 18432)
        W = sb("W", 10240)
        WR = sb("WR", RING * SLOT)
        CN = sb("CN", 1024)
        MK = sb("MK", 2 * 8 * P, u8)
        PR = sb("PR", 1312)
        MOD = sb("MOD", DEPTH * 96)
        SC = sb("SC", 16 + 8 + 8 + 16 + 64)
        ST = sb("ST", 4 * 32 + 64 + 64)
        PS = [stack.enter_context(nc.psum_tensor(f"PS{i}", [P, 1024], f32)) for i in range(4)]

        def bank(n, cols=512):
            return PS[n // 2][:, (n % 2) * 512:(n % 2) * 512 + cols]

        h3 = H[:, :].rearrange("p (t d) -> p t d", t=NT)
        x3 = X[:, :].rearrange("p (k t) -> p k t", k=KT)

        def uview(at, blocks, cols):
            return U[:, at:at + blocks * cols].rearrange("p (b c) -> p b c", b=blocks)

        cq, ci = uview(0, 2, TOK), uview(1536, NT, 256)
        cz = [uview(4608, 2, TOK), uview(3072, 2, TOK)]
        cg = uview(6144, NT, 256)
        qkT = {"A": uview(7680, 3, TOK), "B": uview(10752, 3, TOK)}
        vv = {"A": uview(9984, NT, 128), "B": uview(13056, NT, 128), "D": uview(16896, NT, 256)}
        dqk = uview(13824, 4, TOK)
        biasv = U[:, 0:HEADS * BIAS_ROWS * 64].rearrange("p (h e) -> p h e", h=HEADS)
        g3 = uview(0, FT, TOK)

        ident = CN[:, 0:128]
        cosv = CN[:, 128:384].rearrange("p (t d) -> p t d", t=NLT)
        sinv = CN[:, 384:640].rearrange("p (t d) -> p t d", t=NLT)
        amask = CN[:, 640:1024]
        mk4 = MK[:, :].rearrange("p (d m t) -> p d m t", d=2, m=8)
        cvec = PR[:, 0:16]
        bmod = PR[:, 16:112].rearrange("p (l j) -> p l j", l=DEPTH)
        convp = PR[:, 112:464].rearrange("p (l w j) -> p l w j", l=DEPTH, w=4)
        lbl = PR[:, 464:472].rearrange("p (l e) -> p l e", l=DEPTH)
        qkn = PR[:, 472:728].rearrange("p (l w d) -> p l w d", l=DEPTH, w=2)
        onorm = PR[:, 728:1240].rearrange("p (l c) -> p l c", l=DEPTH)
        sinkv = PR[:, 1240:1248].rearrange("p (l h) -> p l h", l=DEPTH)
        scv = SC[:, 0:16].rearrange("p (k v) -> p k v", k=KT)
        lb4 = SC[:, 16:24].rearrange("p (l e) -> p l e", l=DEPTH)
        oml4 = SC[:, 24:32].rearrange("p (l e) -> p l e", l=DEPTH)
        lbt = SC[:, 32:48].rearrange("p (a e) -> p a e", a=4)
        cexp = SC[:, 48:64]
        mhalf = SC[:, 64:64 + 32]
        mod3 = MOD[:, :].rearrange("p (l j v) -> p l j v", l=DEPTH, j=48)
        ring = WR[:, :].rearrange("p (r c) -> p r c", r=RING)

        raw = W[:, 0:1536].rearrange("p (r c) -> p r c", r=3)
        rot = W[:, 1536:3072].rearrange("p (r c) -> p r c", r=3)
        ra = W[:, 3072:3584]
        rb = W[:, 3584:4096]
        rss = W[:, 4096:4112]
        gt = W[:, 4608:5120]
        EX = [W[:, i * 1152:(i + 1) * 1152].rearrange("p (e t) -> p e t", e=9) for i in range(2)]
        QE = [W[:, 2304 + i * 1024:2304 + (i + 1) * 1024].rearrange("p (e t) -> p e t", e=8) for i in range(2)]
        KE = [W[:, 4352 + i * 1024:4352 + (i + 1) * 1024].rearrange("p (e t) -> p e t", e=8) for i in range(2)]
        YB = [W[:, 6400 + i * 256:6400 + (i + 1) * 256] for i in range(2)]
        LN = [W[:, 6912 + i * 256:6912 + (i + 1) * 256] for i in range(2)]
        KB = [W[:, 7424 + i * 128:7424 + (i + 1) * 128] for i in range(4)]
        CB = [W[:, 7936 + i * 128:7936 + (i + 1) * 128] for i in range(2)]
        AT = [[W[:, 8192 + (2 * d + i) * 256:8192 + (2 * d + i + 1) * 256].rearrange("p (h t) -> p h t", h=2)
               for i in range(2)] for d in range(2)]
        SS = W[:, 9216:9728].rearrange("p (d b v) -> p d b v", d=2, b=2)
        KDT = [W[:, 9728 + i * 128:9728 + (i + 1) * 128] for i in range(2)]
        osq = W[:, 0:1536]
        PB = [W[:, i * 768:(i + 1) * 768] for i in range(2)]
        PT = [W[:, 1536 + i * 768:1536 + (i + 1) * 768] for i in range(2)]
        OB = [W[:, 3072 + i * 256:3072 + (i + 1) * 256] for i in range(2)]
        stat = ST[:, 0:128].rearrange("p (q s h) -> p q s h", q=4, s=8)
        lnp = W[:, 0:2048]
        gav = W[:, 2048:4096].rearrange("p (v c) -> p v c", v=2)
        gtmp = W[:, 4096:5120].rearrange("p (r c) -> p r c", r=2)
        bnb = ST[:, 128:128 + 48].rearrange("p (r c) -> p r c", r=3)
        ross = ST[:, 192:192 + 24]
        DEC = ST[:, 216:220]
        at = [W[:, i * 768:(i + 1) * 768] for i in range(2)]
        vt = [W[:, 1536 + i * 768:1536 + (i + 1) * 768] for i in range(2)]
        sl = [W[:, 3072 + i * 768:3072 + (i + 1) * 768] for i in range(2)]

        w_arrived = [sem(f"w_arrived{r}") for r in range(RING)]
        slot_read = sem("slot_read")
        consts_in = sem("consts_in")
        h_in = sem("h_in")
        sc_ready = sem("sc_ready")
        e_lb = sem("e_lb")
        halves = sem("halves")
        bias_in = sem("bias_in")
        ln_in = sem("ln_in")
        out_stored = sem("out_stored")
        dve_step = sem("dve_step")
        pool_step = sem("pool_step")
        act_step = sem("act_step")
        mod_sum = sem("mod_sum")
        mod_done = sem("mod_done")
        tp_lat = sem("tp_lat")
        tp_ctx = sem("tp_ctx")
        x_lat = sem("x_lat")
        x_ctx = sem("x_ctx")
        job_sum = sem("job_sum")
        job_act = sem("job_act")
        roped = sem("roped")
        rot_tp = sem("rot_tp")
        qk_in = sem("qk_in")
        ss_ready = sem("ss_ready")
        root_ready = sem("root_ready")
        e_in = sem("e_in")
        yk = sem("yk")
        lnr = sem("lnr")
        subs = sem("subs")
        expd = sem("expd")
        qe = sem("qe")
        ke = sem("ke")
        maps = sem("maps")
        kdt = sem("kdt")
        kd_in = sem("kd_in")
        atd = sem("atd")
        o_sum = sem("o_sum")
        kv_sum = sem("kv_sum")
        o_out = sem("o_out")
        s_new = sem("s_new")
        ro_sq = sem("ro_sq")
        ro_rstd = sem("ro_rstd")
        ro_out = sem("ro_out")
        ro_tp = sem("ro_tp")
        ro_in = sem("ro_in")
        sc_sum = sem("sc_sum")
        mx = sem("mx")
        ex = sem("ex")
        p_tp = sem("p_tp")
        pt_act = sem("pt_act")
        pt_dve = sem("pt_dve")
        o_pv = sem("o_pv")
        o_norm = sem("o_norm")
        ga_sum = sem("ga_sum")
        ga_in = sem("ga_in")
        acc_sum = sem("acc_sum")
        acc_read = sem("acc_read")
        bn_ready = sem("bn_ready")
        rstd_ready = sem("rstd_ready")
        ln_norm = sem("ln_norm")
        ln_done = sem("ln_done")
        up_sum = sem("up_sum")
        base_ready = sem("base_ready")
        conv_done = sem("conv_done")
        gate_ready = sem("gate_ready")
        hid_ready = sem("hid_ready")
        zeroed = sem("zeroed")

        def has_ctx(l):
            return l + 1 < DEPTH

        def tiles(l):
            return NT if has_ctx(l) else NLT

        class Job:
            pass

        jobs = []
        for l in range(DEPTH):
            order = [k for k in STREAM if (k[0] == "in" and k[1] == l)
                     or (k[0] == "mod" and l == 0 and k[2] >= MOD_FIRST and k[1] == 0)]
            for key in order:
                kind, _, s, _ = key
                parts = []
                if kind == "mod":
                    parts = [("mod", s, 0)]
                else:
                    with_ctx = has_ctx(l) or s not in LATENT_ONLY
                    if s in FEATURE:
                        parts = [("feat", b, w) for b in range(2) for w in range(1 + with_ctx)]
                    else:
                        parts = [("tok", p, 0) for p in range(2 + with_ctx)]
                for n, (kind, a, b) in enumerate(parts):
                    j = Job()
                    j.l, j.slot, j.kind, j.a, j.b, j.key = l, s, kind, a, b, key
                    j.first, j.last = n == 0, n == len(parts) - 1
                    j.rope = kind == "tok" and s in (QA, KVA, QB, KVB)
                    jobs.append(j)
        n_act = n_rope = n_e = 0
        n_dve = MOD_FIRST
        for j in jobs:
            if j.kind == "mod":
                n_dve += 1
            else:
                n_act += 1
            j.after = (n_act, n_dve)
            if j.rope:
                j.r = n_rope
                n_rope += 1
            j.is_e = j.slot in (FCF, FCB) and j.kind == "feat"
            if j.is_e:
                n_e += 1
                j.e = n_e
        jobs_of = [[j for j in jobs if j.l == l] for l in range(DEPTH)]
        JBANKS = 6
        for l in range(DEPTH):
            js = jobs_of[l]
            for n, j in enumerate(js):
                j.bank = n % JBANKS
                j.freed = js[n - JBANKS].after if n >= JBANKS else None
                j.turns = [js[n - 2]] if n >= 2 and js[n - 2].rope else []
                if n == len(js) - 1:
                    j.turns += [q for q in js[n - 1:] if q.rope]

        units = []
        n_out = n_st = n_u = 0
        for l in range(DEPTH):
            for d in range(2):
                order = [NLT + c for c in range(NCT)][::1 - 2 * d] + list(range(NLT))[::1 - 2 * d]
                for step, t in enumerate(order):
                    for b in range(2):
                        u = Job()
                        u.l, u.d, u.t, u.b, u.step, u.g = l, d, t, b, step, n_u
                        n_u += 1
                        u.out = t < NLT or has_ctx(l)
                        u.state = step < NT - 1
                        u.no, u.ns = n_out, n_st
                        n_out += u.out
                        n_st += u.state
                        units.append(u)
        units_of = [[u for u in units if u.l == l] for l in range(DEPTH)]

        atts = []
        for l in range(DEPTH):
            for g in "ABD":
                for t in range(tiles(l)):
                    for hd in range(HEADS):
                        a = Job()
                        a.l, a.grp, a.t, a.h, a.g, a.quad = l, g, t, hd, len(atts), len(atts) // HEADS
                        if t >= NLT:
                            a.lo, a.hi = 0, 0
                        elif g == "A":
                            a.lo, a.hi = max(0, t - 1), min(NLT, t + 2)
                        else:
                            a.lo, a.hi = 0, NLT
                        a.p_items = []
                        a.keys = list(range(a.lo, a.hi)) + [NLT + c for c in range(NCT)]
                        atts.append(a)
        atts_of = [[a for a in atts if a.l == l] for l in range(DEPTH)]
        n_pa = n_pd = 0
        items_at = {}
        flat = []
        for l in range(DEPTH):
            au = atts_of[l]
            first_item = len(flat)
            for i in range(len(au) + 4):
                its = []
                if 1 <= i <= len(au):
                    a = au[i - 1]
                    cuts = [0, min(3, len(a.keys)), len(a.keys)]
                    for n in range(2):
                        if cuts[n + 1] > cuts[n]:
                            its.append(("p", a, cuts[n], cuts[n + 1], "act" if n == 0 else "dve"))
                if 3 <= i < len(au) + 3 and au[i - 3].h == HEADS - 1:
                    its.append(("o", au[i - 3], 0, 2, "act"))
                made = []
                for it in its:
                    o = Job()
                    o.kind, o.a, o.lo, o.hi, o.eng = it
                    if o.eng == "act":
                        n_pa += 1
                    else:
                        n_pd += 1
                    o.done = (n_pa, n_pd)
                    o.n = len(flat) - first_item
                    o.index = len(flat)
                    o.prev = flat[-2].done if o.n >= 2 else None
                    flat.append(o)
                    made.append(o)
                items_at[l, i] = made
        quads = []
        for o in flat:
            if o.kind == "p":
                o.a.p_items.append(o)
            else:
                quads.append(o)

        ups = []
        n_c = n_m = 0
        for key in STREAM:
            if key[0] == "up":
                for half in range(2):
                    u = Job()
                    u.kind, u.l, u.j, u.half, u.key = "up", key[1], key[2], half, key
                    u.c = n_c
                    n_c += 1
                    ups.append(u)
            elif key[0] == "mod" and key[1] > 0:
                u = Job()
                u.kind, u.l, u.j, u.key = "mod", key[1] - 1, key[2], key
                ups.append(u)
        n_m = 24
        c = 0
        for u in ups:
            if u.kind == "mod":
                n_m += 1
            else:
                c += 1
            u.done = (c, n_m)
        ups_of = [[u for u in ups if u.l == l] for l in range(DEPTH)]
        for l in range(DEPTH):
            for n, u in enumerate(ups_of[l]):
                u.pos = n % 4
                u.freed = ups_of[l][n - 4].done if n >= 4 else None

        stages = [(0, 0, True), (0, 24, True), (1, 0, True), (1, 24, False)]
        ctx_before = [KT * sum(s[2] for s in stages[:m]) for m in range(5)]
        res = [(l, i) for l in range(DEPTH) for i in range(2)]
        tiles_before = [sum(tiles(l) for l, _ in res[:m]) for m in range(5)]
        e_end = [sum(j.is_e for j in jobs if j.l <= l) for l in range(DEPTH)]

        def ga_before(m):
            return sum(4 if has_ctx(l) else 2 for l, _ in res[:m])

        def ro_parts(n):
            return sum(4 if has_ctx(l) else 2 for l in range(n))

        def flat_end(l):
            return [o for o in flat if o.a.l <= l][-1].done

        release = {}
        for n, j in enumerate(jobs):
            release[j.key] = (job_sum, n + 1)
        for i in range(MOD_FIRST):
            release["mod", 0, i, 0] = (mod_sum, i + 1)
        n_up_mod = MOD_FIRST
        for u in ups:
            if u.kind == "mod":
                n_up_mod += 1
                u.sum = n_up_mod
                release[u.key] = (mod_sum, u.sum)
            else:
                release[u.key] = (up_sum, u.c + 1)
        n_read = 0
        for m, (l, i) in enumerate(res):
            groups = KT // KDN if i == 0 else DN_GROUPS
            for n in range(2):
                for g in range(groups):
                    if g < groups - 1:
                        n_read += 1
                        release["down" if i else "out", l, n, g] = (slot_read, n_read)
                    else:
                        release["down" if i else "out", l, n, g] = (
                            acc_sum, 2 * tiles_before[m] + (n + 1) * tiles(l))

        def wait_all(eng, *pairs):
            for s, v in pairs:
                if v > 0:
                    eng.wait_ge(s, v)

        def att_end(l):
            return len([a for a in atts if a.l <= l])

        def unit_end(l):
            us = [u for u in units if u.l <= l]
            return len(us), sum(u.out for u in us), sum(u.state for u in us)

        def mods_done(l):
            return 24 * (l + 1)

        block = stack.enter_context(nc.Block())

        @block.sync
        def _(sp):
            for dst, src in ((PR[:, 0:1248], params), (CN[:, :], consts), (W[:, 0:2 * 8 * P], masks)):
                sp.dma_start(dst, src).then_inc(consts_in, 16)
            sp.dma_start(h3[:, 0:NLT, :], x.rearrange("(t p) d -> p t d", p=P)).then_inc(h_in, 16)
            sp.dma_start(h3[:, NLT:NT, :], ctx_in.rearrange("(t p) d -> p t d", p=P)).then_inc(h_in, 16)
            for n, key in enumerate(STREAM):
                if n >= RING:
                    sp.wait_ge(*release[STREAM[n - RING]])
                half = key[0] == "down" and key[3] == DN_GROUPS - 1 and FT % KDN
                cols = (FT % KDN) * 512 if half else SLOT
                sp.dma_start(ring[:, n % RING, 0:cols], weights[n, :, 0:cols]).then_inc(w_arrived[n % RING], 16)

        @block.tensor
        def _(pe):
            def slot(key):
                n = SLOT_AT[key]
                pe.wait_ge(w_arrived[n % RING], 16 * (n // RING + 1))
                return ring[:, n % RING, :]

            def mod_products(wk, b):
                for jj in range(2):
                    for k in range(KT):
                        mm = pe.matmul(bank(b)[:, 2 * jj:2 * jj + 2], wk[:, k, jj * P:(jj + 1) * P], scv[:, k, :],
                                       start=(k == 0), stop=(k == KT - 1))
                return mm

            pe.wait_ge(consts_in, 48)
            pe.wait_ge(sc_ready, 1)
            for i in range(MOD_FIRST):
                wk = slot(("mod", 0, i, 0)).rearrange("p (k c) -> p k c", k=KT)
                mm = mod_products(wk, i)
                mm.then_inc(mod_sum, 1)

            def transposes(m):
                l, _, with_ctx = stages[m]
                if m == 0:
                    pe.wait_ge(h_in, 32)
                    pe.wait_ge(mod_done, MOD_FIRST)
                for k in range(KT):
                    a = KT * m + k
                    if k >= 2:
                        pe.wait_ge(x_lat, a - 1)
                    for t in range(NLT):
                        if m > 0 and k == 0:
                            pe.wait_ge(ln_done, tiles_before[m - 1] + t + 1)
                        mm = pe.transpose(bank(k % 2)[:, t * P:(t + 1) * P], h3[:, t, k * P:(k + 1) * P], ident)
                    mm.then_inc(tp_lat, 1)
                    if with_ctx:
                        c = ctx_before[m] + k
                        if k >= 2:
                            pe.wait_ge(x_ctx, c - 1)
                        if m > 0 and k == 0:
                            pe.wait_ge(ln_done, tiles_before[m])
                        for t in range(NCT):
                            mm = pe.transpose(bank(2 + k % 2)[:, t * P:(t + 1) * P],
                                              h3[:, NLT + t, k * P:(k + 1) * P], ident)
                        mm.then_inc(tp_ctx, 1)
                pe.wait_ge(x_lat, KT * (m + 1))
                if with_ctx:
                    pe.wait_ge(x_ctx, ctx_before[m + 1])

            def projections(l):
                for j in jobs_of[l]:
                    if j.first:
                        ws = slot(j.key)
                    wk = ws.rearrange("p (k c) -> p k c", k=KT)
                    if j.freed:
                        wait_all(pe, (job_act, j.freed[0]), (mod_done, j.freed[1]))
                    if j.kind == "mod":
                        mm = mod_products(wk, j.bank)
                    elif j.kind == "feat":
                        lo, hi = (0, SEQ) if j.b == 0 else (SEQ, TOK)
                        for k in range(KT):
                            mm = pe.matmul(bank(j.bank)[:, 0:hi - lo], wk[:, k, j.a * P:(j.a + 1) * P],
                                           x3[:, k, lo:hi], start=(k == 0), stop=(k == KT - 1))
                    else:
                        for i in range(2):
                            t = 2 * j.a + i
                            for k in range(KT):
                                mm = pe.matmul(bank(j.bank)[:, i * 256:(i + 1) * 256], x3[:, k, t * P:(t + 1) * P],
                                               wk[:, k, :], start=(k == 0), stop=(k == KT - 1))
                    mm.then_inc(job_sum, 1)
                    for q in j.turns:
                        pe.wait_ge(roped, q.r + 1)
                        if q.r >= 2:
                            pe.wait_ge(qk_in, q.r - 1)
                        tb = bank(6 + q.r % 2)
                        r3 = rot[:, q.r % 3, :].rearrange("p (i c) -> p i c", i=2)
                        if q.slot in (QA, QB):
                            for g in range(2):
                                for i in range(2):
                                    mm = pe.transpose(tb[:, g * 256 + i * P:g * 256 + (i + 1) * P],
                                                      r3[:, i, g * P:(g + 1) * P], ident)
                        else:
                            for i in range(2):
                                mm = pe.transpose(tb[:, i * P:(i + 1) * P], r3[:, i, 0:P], ident)
                        mm.then_inc(rot_tp, 1)

            def hgrn(l):
                us = units_of[l]
                wait_all(pe, (job_act, jobs_of[l][-1].after[0]), (mod_done, jobs_of[l][-1].after[1]),
                         (qk_in, max(j.r for j in jobs_of[l] if j.rope) + 1))

                def score_maps(u):
                    par = u.g % 2
                    pe.wait_ge(qe, u.no + 1)
                    pe.wait_ge(ke, u.g + 1)
                    pe.wait_ge(yk, u.g + 1)
                    for half in range(2):
                        if u.no >= 1:
                            pe.wait_ge(atd, 2 * (u.no - 1) + half + 1)
                        for m in range(4 * half, 4 * half + 4):
                            for hh in range(2):
                                rows = slice(64 * hh, 64 * hh + 64)
                                if m < LEVELS:
                                    lhs, rhs = KE[par][rows, m, :], QE[par][rows, 1 + m, :]
                                else:
                                    lhs, rhs = KB[u.g % 4][rows, :], cq[rows, u.b, u.t * P:(u.t + 1) * P]
                                mm = pe.matmul(bank(2 * half + hh)[:, (m % 4) * P:(m % 4 + 1) * P], lhs, rhs,
                                               start=True, stop=True)
                        mm.then_inc(maps, 1)

                def turn_keys(u):
                    pe.wait_ge(ke, u.g + 1)
                    if u.ns >= 1:
                        pe.wait_ge(kd_in, u.ns)
                    pe.transpose(bank(4)[:, 0:P], KE[u.g % 2][:, 7, :], ident).then_inc(kdt, 1)

                def outputs(u):
                    vslice = ci[:, u.t, u.b * P:(u.b + 1) * P]
                    if u.out:
                        ob = bank(6 + u.no % 2)
                        pe.wait_ge(atd, 2 * u.no + 2)
                        if u.no >= 2:
                            pe.wait_ge(o_out, u.no - 1)
                        if u.step >= 1:
                            prev = [w for w in us if w.d == u.d and w.b == u.b and w.step == u.step - 1][0]
                            pe.wait_ge(s_new, prev.ns + 1)
                        pe.wait_ge(zeroed, l + 1)
                        for hh in range(2):
                            oh = ob[:, hh * 64:(hh + 1) * 64]
                            pe.matmul(oh, QE[u.g % 2][:, 0, :], SS[:, u.d, u.b, hh * 64:(hh + 1) * 64],
                                      start=True, stop=False)
                            mm = pe.matmul(oh, AT[u.d][u.no % 2][:, hh, :], vslice[:, hh * 64:(hh + 1) * 64],
                                           start=False, stop=True)
                        mm.then_inc(o_sum, 1)
                    if u.state:
                        pe.wait_ge(kd_in, u.ns + 1)
                        if u.ns >= 1:
                            pe.wait_ge(s_new, u.ns)
                        pe.matmul(bank(5)[:, 0:P], KDT[u.ns % 2], vslice, start=True, stop=True).then_inc(kv_sum, 1)

                for i in range(len(us) + 1):
                    if i < len(us):
                        if us[i].out:
                            score_maps(us[i])
                        if us[i].state:
                            turn_keys(us[i])
                    if i >= 1:
                        outputs(us[i - 1])
                pe.wait_ge(ro_out, l + 1)
                n = 0
                for b in range(2):
                    for lo, hi in ((0, NLT), (NLT, tiles(l))):
                        if hi > lo:
                            for t in range(lo, hi):
                                mm = pe.transpose(bank(n)[:, (t - lo) * P:(t - lo + 1) * P],
                                                  cz[0][:, b, t * P:(t + 1) * P], ident)
                            mm.then_inc(ro_tp, 1)
                            n += 1

            def attention(l):
                au = atts_of[l]
                pe.wait_ge(ro_in, ro_parts(l + 1))
                pe.wait_ge(s_new, unit_end(l)[2])
                pe.wait_ge(o_out, unit_end(l)[1])

                def scores(a):
                    n = a.g
                    sbk = PS[n % 2]
                    if n - atts_of[l][0].g >= 2:
                        pe.wait_ge(ex, n - 1)
                    if a.grp == "D":
                        rows = slice(64 * (a.h % 2), 64 * (a.h % 2) + 64)
                        q, kk = dqk[rows, a.h // 2, :], dqk[rows, 2 + a.h // 2, :]
                    else:
                        rows = slice(64 * (a.h // 2), 64 * (a.h // 2) + 64)
                        q, kk = qkT[a.grp][rows, a.h % 2, :], qkT[a.grp][rows, 2, :]
                    q = q[:, a.t * P:(a.t + 1) * P]
                    if a.hi > a.lo:
                        pe.matmul(sbk[:, 0:(a.hi - a.lo) * P], q, kk[:, a.lo * P:a.hi * P], start=True, stop=True)
                    pe.matmul(sbk[:, 512:512 + CTX], q, kk[:, SEQ:TOK], start=True, stop=True).then_inc(sc_sum, 1)

                def turn(o):
                    if o.prev:
                        wait_all(pe, (pt_act, o.prev[0]), (pt_dve, o.prev[1]))
                    tb = bank(4 + o.n % 2)
                    if o.kind == "p":
                        pe.wait_ge(ex, o.a.g + 1)
                        for i in range(o.lo, o.hi):
                            mm = pe.transpose(tb[:, (i - o.lo) * P:(i - o.lo + 1) * P],
                                              PB[o.a.g % 2][:, i * P:(i + 1) * P], ident)
                    else:
                        pe.wait_ge(o_norm, o.a.quad + 1)
                        for i in range(2):
                            mm = pe.transpose(tb[:, i * P:(i + 1) * P], OB[o.a.quad % 2][:, i * P:(i + 1) * P], ident)
                    mm.then_inc(p_tp, 1)

                def values(a):
                    if a.h == 0 and a.quad - atts_of[l][0].quad >= 2:
                        pe.wait_ge(o_norm, a.quad - 1)
                    last = a.p_items[-1]
                    wait_all(pe, (pt_act, last.done[0]), (pt_dve, last.done[1]))
                    ob = bank(6 + a.quad % 2)[:, a.h * 64:(a.h + 1) * 64]
                    vc = slice(a.h * 64, a.h * 64 + 64) if a.grp == "D" else slice((a.h // 2) * 64, (a.h // 2) * 64 + 64)
                    for i, kt in enumerate(a.keys):
                        mm = pe.matmul(ob, PT[a.g % 2][:, i * P:(i + 1) * P], vv[a.grp][:, kt, vc],
                                       start=(i == 0), stop=(i == len(a.keys) - 1))
                    mm.then_inc(o_pv, 1)

                for i in range(len(au) + 4):
                    if i < len(au):
                        scores(au[i])
                    for o in items_at[l, i]:
                        if o.kind == "p":
                            turn(o)
                    if 2 <= i < len(au) + 2:
                        values(au[i - 2])
                    for o in items_at[l, i]:
                        if o.kind == "o":
                            turn(o)

            def spread_gates(m):
                l, i = res[m]
                if i == 0:
                    wait_all(pe, (pt_act, flat_end(l)[0]), (pt_dve, flat_end(l)[1]), (o_norm, att_end(l) // HEADS))
                    pe.wait_ge(mod_done, mods_done(l))
                else:
                    wait_all(pe, (conv_done, ups_of[l][-1].done[0]), (mod_done, ups_of[l][-1].done[1]))
                    pe.wait_ge(hid_ready, FT * (l + 1))
                for v in range(2 if has_ctx(l) else 1):
                    for hf in range(2):
                        for k in range(4):
                            col = mod3[:, l, (16 if i == 0 else 40) + hf * 4 + k, v:v + 1]
                            mm = pe.matmul(bank(2 * v + hf)[:, k * P:(k + 1) * P], col.broadcast_to([P, P]), ident,
                                           start=True, stop=True)
                        mm.then_inc(ga_sum, 1)

            def residual_products(m):
                l, i = res[m]
                src, groups, total = (x3, KT // KDN, KT) if i == 0 else (g3, DN_GROUPS, FT)
                base = 2 * tiles_before[m]
                for n in range(2):
                    for g in range(groups):
                        key = ("out" if i == 0 else "down", l, n, g)
                        wk = slot(key).rearrange("p (k c) -> p k c", k=KDN)
                        for t in range(tiles(l)):
                            job = n * tiles(l) + t
                            if g == 0:
                                if 4 <= job < 8:
                                    pe.wait_ge(ga_in, ga_before(m + 1))
                                if job >= 8:
                                    pe.wait_ge(acc_read, base + job - 8 + 1)
                            ks = range(g * KDN, min(g * KDN + KDN, total))
                            for k in ks:
                                mm = pe.matmul(bank((job + 4) % 8), src[:, k, t * P:(t + 1) * P], wk[:, k % KDN, :],
                                               start=(k == 0), stop=(k == total - 1))
                            if g == groups - 1:
                                mm.then_inc(acc_sum, 1)
                        if g < groups - 1:
                            mm.then_inc(slot_read, 1)

            def ffn_up(l):
                us = ups_of[l]
                for u in us:
                    if u.kind == "mod" or u.half == 0:
                        ws = slot(u.key)
                    if u.freed:
                        wait_all(pe, (conv_done, u.freed[0]), (mod_done, u.freed[1]))
                    if u.kind == "mod":
                        mm = mod_products(ws.rearrange("p (k c) -> p k c", k=KT), 2 * u.pos)
                        mm.then_inc(mod_sum, 1)
                        continue
                    wk = ws.rearrange("p (k h c) -> p k h c", k=KT, h=2)
                    for lo, hi in ((0, SEQ), (SEQ, TOK)) if has_ctx(l) else ((0, SEQ),):
                        for k in range(KT):
                            mm = pe.matmul(PS[u.pos][:, lo:hi], wk[:, k, u.half, :], x3[:, k, lo:hi],
                                           start=(k == 0), stop=(k == KT - 1))
                    mm.then_inc(up_sum, 1)

            for l in range(DEPTH):
                transposes(2 * l)
                projections(l)
                hgrn(l)
                attention(l)
                spread_gates(2 * l)
                residual_products(2 * l)
                pe.wait_ge(acc_read, 2 * tiles_before[2 * l + 1])
                transposes(2 * l + 1)
                ffn_up(l)
                spread_gates(2 * l + 1)
                residual_products(2 * l + 1)
                pe.wait_ge(acc_read, 2 * tiles_before[2 * l + 2])

        @block.scalar
        def _(act):
            steps = [0]

            def step(ins):
                steps[0] += 1
                ins.then_inc(act_step, 1)
                act.wait_ge(act_step, steps[0])

            act.wait_ge(consts_in, 48)
            act.activation(SC[:, 0:16], cvec, ACT.Silu).then_inc(sc_ready, 1)
            act.wait_ge(dve_step, 2)
            act.activation(cexp[:, 8:16], cexp[:, 0:8], ACT.Exp).then_inc(e_lb, 1)

            def modulate_latent(m):
                l, j0, _ = stages[m]
                act.wait_ge(mod_done, MOD_FIRST if m == 0 else mods_done(l))
                for k in range(KT):
                    act.wait_ge(tp_lat, KT * m + k + 1)
                    act.activation(x3[:, k, 0:SEQ], bank(k % 2), ACT.Identity, bias=mod3[:, l, j0 + k, 0:1],
                                   scale=mod3[:, l, j0 + 8 + k, 0:1]).then_inc(x_lat, 1)

            def take_projections(l):
                dest = {QC: lambda a: cq[:, a, :], FCF: lambda a: cz[0][:, a, :], FCB: lambda a: cz[1][:, a, :],
                        QD: lambda a: dqk[:, a, :], KD: lambda a: dqk[:, 2 + a, :]}
                tok_dest = {IC: ci, GC: cg, VD: vv["D"]}
                for j in jobs_of[l]:
                    if j.kind != "mod":
                        act.wait_ge(job_sum, jobs.index(j) + 1)
                        ps3 = bank(j.bank).rearrange("p (i c) -> p i c", i=2)
                        if j.kind == "feat":
                            lo, hi = (0, SEQ) if j.b == 0 else (SEQ, TOK)
                            func, sc = {QC: (ACT.Silu, 1.0), FCF: (ACT.Exp, -1.0), FCB: (ACT.Exp, -1.0)}.get(
                                j.slot, (ACT.Copy, 1.0))
                            ins = act.activation(dest[j.slot](j.a)[:, lo:hi], bank(j.bank)[:, 0:hi - lo], func, scale=sc)
                        elif j.rope:
                            if j.slot in (KVA, KVB):
                                v = vv["A" if j.slot == KVA else "B"]
                                act.activation(v[:, 2 * j.a:2 * j.a + 2, :], ps3[:, :, P:], ACT.Copy)
                            if j.r >= 3:
                                act.wait_ge(roped, j.r - 2)
                            elif l == 0 and j.r == 0:
                                pass
                            ins = act.activation(raw[:, j.r % 3, :], bank(j.bank), ACT.Copy)
                        else:
                            ins = act.activation(tok_dest[j.slot][:, 2 * j.a:2 * j.a + 2, :], ps3,
                                                 ACT.Silu if j.slot == GC else ACT.Copy)
                        ins.then_inc(job_act, 1)
                    for q in j.turns:
                        act.wait_ge(rot_tp, q.r + 1)
                        grp = "A" if q.slot in (QA, KVA) else "B"
                        tb = bank(6 + q.r % 2)
                        cols = slice(q.a * 256, q.a * 256 + 256)
                        if q.slot in (QA, QB):
                            ins = act.activation(qkT[grp][:, 0:2, cols], tb.rearrange("p (g t) -> p g t", g=2), ACT.Copy)
                        else:
                            ins = act.activation(qkT[grp][:, 2, cols], tb[:, 0:256], ACT.Copy)
                        ins.then_inc(qk_in, 1)

            def hgrn(l):
                us = units_of[l]
                for i in range(-3, len(us)):
                    if 0 <= i + 3 < len(us):
                        u = us[i + 3]
                        act.wait_ge(yk, u.g + 1)
                        if u.g >= 2:
                            act.wait_ge(subs, u.g - 1)
                        act.activation(LN[u.g % 2], YB[u.g % 2], ACT.Ln).then_inc(lnr, 1)
                    if 0 <= i + 2 < len(us):
                        u = us[i + 2]
                        last = (P - 1, 0)[u.d]
                        act.wait_ge(subs, u.g + 1)
                        if u.g >= 2:
                            act.wait_ge(ke, u.g - 1)
                        if u.g >= 2 and units[u.g - 2].out:
                            act.wait_ge(qe, units[u.g - 2].no + 1)
                        if u.ns >= 4:
                            act.wait_ge(s_new, u.ns - 3)
                        E = EX[u.g % 2]
                        if u.out:
                            step(act.activation(E[:, 1:8, :], E[:, 1:8, :], ACT.Abs))
                        act.activation(E[:, 0, :], CB[u.g % 2], ACT.Exp)
                        act.activation(DEC[:, u.g % 4:u.g % 4 + 1], CB[u.g % 2][:, last:last + 1], ACT.Exp)
                        lo = 1 if u.out else 8
                        act.activation(E[:, lo:9, :], E[:, lo:9, :], ACT.Exp, scale=-1.0).then_inc(expd, 1)
                    if i >= 0 and us[i].state:
                        u = us[i]
                        act.wait_ge(kdt, u.ns + 1)
                        if u.ns >= 2:
                            act.wait_ge(kv_sum, u.ns - 1)
                        act.activation(KDT[u.ns % 2], bank(4)[:, 0:P], ACT.Copy).then_inc(kd_in, 1)
                n = 0
                for b in range(2):
                    for lo, hi in ((0, NLT), (NLT, tiles(l))):
                        if hi > lo:
                            act.wait_ge(ro_tp, ro_parts(l) + n + 1)
                            act.activation(x3[:, 4 + b, lo * P:hi * P], bank(n)[:, 0:(hi - lo) * P],
                                           ACT.Copy).then_inc(ro_in, 1)
                            n += 1
                act.dma_start(biasv, bias_d[l]).then_inc(bias_in, 16)

            def attention(l):
                au = atts_of[l]
                for i in range(len(au) + 4):
                    if i < len(au):
                        a = au[i]
                        sbk, pb = PS[a.g % 2], PB[a.g % 2]
                        nl = (a.hi - a.lo) * P
                        s4 = stat[:, a.quad % 4]
                        act.wait_ge(mx, a.g + 1)
                        if i >= 2:
                            act.wait_ge(p_tp, au[i - 2].p_items[-1].index + 1)
                        negm = s4[:, 3, a.h:a.h + 1]
                        if a.grp == "A":
                            act.activation(s4[:, 6, a.h:a.h + 1], sinkv[:, l, a.h:a.h + 1], ACT.Exp, bias=negm)
                        if nl and a.grp != "B":
                            act.activation(pb[:, 0:nl], pb[:, 0:nl], ACT.Exp, bias=negm,
                                           accum_out=s4[:, 4, a.h:a.h + 1])
                            act.activation(pb[:, nl:nl + CTX], sbk[:, 512:768], ACT.Exp, bias=negm, scale=SCALE,
                                           accum_out=s4[:, 5, a.h:a.h + 1]).then_inc(ex, 1)
                        else:
                            act.activation(pb[:, 0:nl + CTX], sbk[:, 512 - nl:768], ACT.Exp, bias=negm, scale=SCALE,
                                           accum_out=s4[:, 4, a.h:a.h + 1]).then_inc(ex, 1)
                    for o in items_at[l, i]:
                        if o.eng != "act":
                            continue
                        act.wait_ge(p_tp, o.index + 1)
                        tb = bank(4 + o.n % 2)
                        if o.kind == "p":
                            if o.a.g - au[0].g >= 2:
                                act.wait_ge(o_pv, o.a.g - 1)
                            act.activation(PT[o.a.g % 2][:, o.lo * P:o.hi * P], tb[:, 0:(o.hi - o.lo) * P],
                                           ACT.Copy).then_inc(pt_act, 1)
                        else:
                            k0 = {"A": 0, "B": 2, "D": 6}[o.a.grp]
                            act.activation(x3[:, k0:k0 + 2, o.a.t * P:(o.a.t + 1) * P],
                                           tb[:, 0:256].rearrange("p (k t) -> p k t", k=2),
                                           ACT.Copy).then_inc(pt_act, 1)

            def gates(m):
                l, i = res[m]
                base = ga_before(m)
                n = 0
                for v in range(2 if has_ctx(l) else 1):
                    for hf in range(2):
                        act.wait_ge(ga_sum, base + n + 1)
                        if n == 0:
                            act.dma_start(lnp, ln_rows[2 * l + i].partition_broadcast(P)).then_inc(ln_in, 16)
                        act.activation(gav[:, v, hf * 512:(hf + 1) * 512], bank(2 * v + hf), ACT.Copy).then_inc(ga_in, 1)
                        n += 1

            def ffn(l):
                n = TOK if has_ctx(l) else SEQ

                def gate(j):
                    jg = FT * l + j
                    act.wait_ge(conv_done, 2 * jg + 1)
                    if jg >= 2:
                        act.wait_ge(hid_ready, jg - 1)
                    act.activation(sl[jg % 2][:, 0:n], at[jg % 2][:, 0:n], ACT.Silu).then_inc(gate_ready, 1)

                for u in ups_of[l]:
                    if u.kind == "mod":
                        continue
                    jg = FT * l + u.j
                    dst = (at, vt)[u.half][jg % 2]
                    act.wait_ge(up_sum, u.c + 1)
                    if jg >= 2:
                        act.wait_ge(hid_ready, jg - 1)
                    jj = u.half * FT + u.j
                    act.activation(dst[:, 0:n], PS[u.pos][:, 0:n], ACT.Identity, bias=convp[:, l, 3, jj:jj + 1],
                                   scale=convp[:, l, 1, jj:jj + 1]).then_inc(base_ready, 1)
                    if u.half == 1 and u.j >= 1:
                        gate(u.j - 1)
                gate(FT - 1)

            for l in range(DEPTH):
                modulate_latent(2 * l)
                take_projections(l)
                hgrn(l)
                attention(l)
                gates(2 * l)
                modulate_latent(2 * l + 1)
                ffn(l)
                gates(2 * l + 1)
            for t in range(NLT):
                act.wait_ge(ln_done, tiles_before[3] + t + 1)
                act.dma_start(out[t * P:(t + 1) * P, :], h3[:, t, :]).then_inc(out_stored, 16)
            act.wait_ge(out_stored, 16 * NLT)

        @block.vector
        def _(dve):
            steps = [0]

            def mark(ins):
                steps[0] += 1
                ins.then_inc(dve_step, 1)

            def step(ins):
                mark(ins)
                dve.wait_ge(dve_step, steps[0])

            dve.wait_ge(consts_in, 48)
            step(dve.tensor_tensor(lbt[:, 0, :], lbl[:, 0, :], lbl[:, 1, :], ALU.max))
            step(dve.tensor_tensor(cexp[:, 0:8].rearrange("p (l e) -> p l e", l=2), lbl,
                                   lbt[:, 0:1, :].broadcast_to([P, 2, 4]), ALU.subtract))
            dve.wait_ge(e_lb, 1)
            e2 = cexp[:, 8:16].rearrange("p (l e) -> p l e", l=2)
            step(dve.tensor_tensor(lbt[:, 1, :], e2[:, 0, :], e2[:, 1, :], ALU.add))
            step(dve.reciprocal(lbt[:, 1, :], lbt[:, 1, :]))
            step(dve.tensor_tensor(e2, e2, lbt[:, 1:2, :].broadcast_to([P, 2, 4]), ALU.mult))
            step(dve.tensor_tensor(lb4[:, 0, :], e2[:, 0, :], e2[:, 0, :], ALU.subtract))
            step(dve.tensor_tensor(lbt[:, 2, :], e2[:, 0, :], e2[:, 1, :], ALU.add))
            step(dve.tensor_tensor(lb4[:, 1, :], lbt[:, 2, :], e2[:, 0, :], ALU.subtract))
            step(dve.tensor_scalar(oml4, lb4, -1.0, 1.0, ALU.mult, ALU.add))
            dve.memset(mhalf, -0.5).then_inc(halves, 1)
            step(dve.tensor_copy(MK[:, :], W[:, 0:2 * 8 * P]))

            def mod_out(l, i, src):
                b = bmod[:, l, 2 * i:2 * i + 2].unsqueeze(2).broadcast_to([P, 2, 2])
                o = mod3[:, l, 2 * i:2 * i + 2, :]
                s3 = src[:, 0:4].rearrange("p (j v) -> p j v", j=2)
                if 4 <= i < 8 or 16 <= i < 20:
                    step(dve.tensor_tensor(o, s3, b, ALU.add))
                    dve.tensor_scalar(o, o, 1.0, None, ALU.add).then_inc(mod_done, 1)
                else:
                    dve.tensor_tensor(o, s3, b, ALU.add).then_inc(mod_done, 1)

            for i in range(MOD_FIRST):
                dve.wait_ge(mod_sum, i + 1)
                mod_out(0, i, bank(i))

            def modulate_context(m):
                l, j0, with_ctx = stages[m]
                if with_ctx:
                    for k in range(KT):
                        if k == 0:
                            dve.wait_ge(mod_done, MOD_FIRST if m == 0 else mods_done(l))
                        dve.wait_ge(tp_ctx, ctx_before[m] + k + 1)
                        dve.tensor_scalar(x3[:, k, SEQ:TOK], bank(2 + k % 2, 256), mod3[:, l, j0 + 8 + k, 1:2],
                                          mod3[:, l, j0 + k, 1:2], ALU.mult, ALU.add).then_inc(x_ctx, 1)

            def rotate(j):
                l, heads = j.l, 4 if j.slot in (QA, QB) else 2
                rw = raw[:, j.r % 3, :]
                ro = rot[:, j.r % 3, :]
                dve.wait_ge(job_act, j.after[0])
                if j.r >= 1:
                    dve.wait_ge(roped, j.r)
                if j.r >= 3:
                    dve.wait_ge(rot_tp, j.r - 2)
                src4 = rw.rearrange("p (i h d) -> p i h d", i=2, d=HD)[:, :, 0:heads, :]
                if j.slot in (QB, KVB):
                    nh = 2 * heads
                    ra4 = ra.rearrange("p (i h d) -> p i h d", i=2, d=HD)[:, :, 0:heads, :]
                    step(dve.tensor_tensor(ra4, src4, src4, ALU.mult))
                    for i in range(2):
                        ins = dve.tensor_reduce(rss[:, 4 * i:4 * i + heads], ra4[:, i], AX, ALU.add)
                        mark(ins) if i == 0 else step(ins)
                    r8 = rss[:, 0:8]
                    if heads == 2:
                        for i in range(2):
                            ins = dve.tensor_scalar(rss[:, 4 * i:4 * i + 2], rss[:, 4 * i:4 * i + 2], 1.0 / HD, EPS,
                                                    ALU.mult, ALU.add)
                    else:
                        ins = dve.tensor_scalar(r8, r8, 1.0 / HD, EPS, ALU.mult, ALU.add)
                    ins.then_inc(ss_ready, 1)
                    rs[0] += 1
                    dve.wait_ge(root_ready, rs[0])
                    for i in range(2):
                        ins = dve.tensor_tensor(ra4[:, i], src4[:, i],
                                                rss[:, 8 + 4 * i:8 + 4 * i + heads].unsqueeze(2).broadcast_to([P, heads, HD]),
                                                ALU.mult)
                        mark(ins) if i == 0 else step(ins)
                    gain = qkn[:, l, 0 if j.slot == QB else 1, :].unsqueeze(1).broadcast_to([P, heads, HD])
                    plain = j.a * 2 >= NLT
                    dst = ro.rearrange("p (i h d) -> p i h d", i=2, d=HD)[:, :, 0:heads, :] if plain else src4
                    for i in range(2):
                        ins = dve.tensor_tensor(dst[:, i], ra4[:, i], gain, ALU.mult)
                        if plain and i == 1:
                            ins.then_inc(roped, 1)
                        elif i == 0:
                            mark(ins)
                        else:
                            step(ins)
                    if plain:
                        return
                elif j.a * 2 >= NLT:
                    dve.tensor_copy(ro, rw).then_inc(roped, 1)
                    return
                for i in range(2):
                    t = 2 * j.a + i
                    s = rw[:, i * 256:i * 256 + heads * HD]
                    o = ro[:, i * 256:i * 256 + heads * HD]
                    a_ = ra[:, i * 256:i * 256 + heads * HD]
                    b_ = rb[:, i * 256:i * 256 + heads * HD]
                    mark(dve.tensor_tensor(a_.rearrange("p (h d) -> p h d", d=HD), s.rearrange("p (h d) -> p h d", d=HD),
                                           cosv[:, t, :].unsqueeze(1).broadcast_to([P, heads, HD]), ALU.mult))
                    s5 = s.rearrange("p (h a f d) -> p h a f d", a=2, f=2, d=HD // 4)
                    b5 = b_.rearrange("p (h a f d) -> p h a f d", a=2, f=2, d=HD // 4)
                    t5 = sinv[:, t, :].rearrange("p (a f d) -> p a f d", a=2, f=2)
                    for f in range(2):
                        ins = dve.tensor_tensor(b5[:, :, :, f, :], s5[:, :, :, 1 - f, :],
                                                t5[:, :, f, :].unsqueeze(1).broadcast_to([P, heads, 2, HD // 4]), ALU.mult)
                        mark(ins)
                dve.wait_ge(dve_step, steps[0])
                v4 = lambda w: w.rearrange("p (i c) -> p i c", i=2)[:, :, 0:heads * HD]
                dve.tensor_tensor(v4(ro), v4(ra), v4(rb), ALU.add).then_inc(roped, 1)

            def project(l):
                for j in jobs_of[l]:
                    if j.kind == "mod":
                        dve.wait_ge(job_sum, jobs.index(j) + 1)
                        mod_out(0, j.slot, bank(j.bank))
                    elif j.is_e:
                        lo, hi = (0, SEQ) if j.b == 0 else (SEQ, TOK)
                        d = 0 if j.slot == FCF else 1
                        z = cz[d][:, j.a, lo:hi]
                        e = 2 * d + j.a
                        dve.wait_ge(job_act, j.after[0])
                        step(dve.tensor_scalar(z, z, 1.0, None, ALU.add))
                        step(dve.reciprocal(z, z))
                        dve.tensor_scalar(z, z, oml4[:, l, e:e + 1], lb4[:, l, e:e + 1], ALU.mult,
                                          ALU.add).then_inc(e_in, 1)
                    elif j.rope:
                        rotate(j)

            def hgrn(l):
                us = units_of[l]
                dve.memset(W[:, 8192:9728], 0.0).then_inc(zeroed, 1)
                dve.wait_ge(zeroed, l + 1)
                for i in range(-2, len(us) + 1):
                    if 0 <= i + 2 < len(us):
                        u = us[i + 2]
                        E, cb, ln = EX[u.g % 2], CB[u.g % 2], LN[u.g % 2]
                        dve.wait_ge(lnr, u.g + 1)
                        if u.g >= 2:
                            dve.wait_ge(expd, u.g - 1)
                            dve.wait_ge(ke, u.g - 1)
                            dve.wait_ge(subs, u.g)
                            if units[u.g - 2].out:
                                dve.wait_ge(qe, units[u.g - 2].no + 1)
                        r = slice(None, None, 1 - 2 * u.d)
                        step(dve.tensor_tensor_scan(cb[:, r], ln[:, 0:P][:, r], ln[:, P:2 * P][:, r], 0.0, ALU.add, ALU.add))
                        if u.out:
                            for m in range(LEVELS):
                                half = P >> (m + 1)
                                ref = half - 1 + u.d
                                c3 = cb.rearrange("p (n w) -> p n w", w=2 * half)
                                dve.tensor_tensor(E[:, 1 + m, :].rearrange("p (n w) -> p n w", w=2 * half), c3,
                                                  c3[:, :, ref:ref + 1].broadcast_to([P, P // (2 * half), 2 * half]),
                                                  ALU.subtract)
                        last = (P - 1, 0)[u.d]
                        dve.tensor_tensor(E[:, 8, :], cb, cb[:, last:last + 1].broadcast_to([P, P]),
                                          ALU.subtract).then_inc(subs, 1)
                    if 0 <= i + 1 < len(us) and us[i + 1].out:
                        u = us[i + 1]
                        dve.wait_ge(expd, u.g + 1)
                        if u.no >= 2:
                            dve.wait_ge(o_sum, u.no - 1)
                        q = cq[:, u.b, u.t * P:(u.t + 1) * P].unsqueeze(1).broadcast_to([P, 8, P])
                        dve.tensor_tensor(QE[u.g % 2], EX[u.g % 2][:, 0:8, :], q, ALU.mult).then_inc(qe, 1)
                    if 0 <= i < len(us) and us[i].out:
                        u = us[i]
                        if u.no >= 2:
                            dve.wait_ge(o_sum, u.no - 1)
                        for half in range(2):
                            dve.wait_ge(maps, 2 * u.no + half + 1)
                            for m in range(4 * half, 4 * half + 4):
                                ins = dve.copy_predicated(
                                    AT[u.d][u.no % 2], mk4[:, u.d, m:m + 1, :].broadcast_to([P, 2, P]),
                                    PS[half][:, :].rearrange("p (h c) -> p h c", h=2)[:, :, (m % 4) * P:(m % 4 + 1) * P])
                                if m % 4 < 3:
                                    step(ins)
                            ins.then_inc(atd, 1)
                            dve.wait_ge(atd, 2 * u.no + half + 1)
                    if i >= 1:
                        u = us[i - 1]
                        if u.out:
                            dve.wait_ge(o_sum, u.no + 1)
                            o = cz[0][:, u.b, u.t * P:(u.t + 1) * P]
                            ob = bank(6 + u.no % 2)[:, 0:P]
                            dve.wait_ge(o_out, u.no) if u.no else None
                            if u.d == 0:
                                ins = dve.tensor_copy(o, ob)
                            else:
                                ins = dve.tensor_tensor(o, ob, o, ALU.add)
                            ins.then_inc(o_out, 1)
                        if u.state:
                            dve.wait_ge(kv_sum, u.ns + 1)
                            if u.ns >= 1:
                                dve.wait_ge(s_new, u.ns)
                            for hh in range(2):
                                rows, cols = slice(64 * hh, 64 * hh + 64), slice(64 * hh, 64 * hh + 64)
                                s = SS[rows, u.d, u.b, cols]
                                ins = dve.scalar_tensor_tensor(s, s, DEC[rows, u.g % 4:u.g % 4 + 1], bank(5)[rows, cols],
                                                               ALU.mult, ALU.add)
                            ins.then_inc(s_new, 1)
                nt = tiles(l)
                dve.wait_ge(o_out, unit_end(l)[1])
                o3 = cz[0][:, :, 0:nt * P]
                n = 2 * nt * 2
                step(dve.tensor_tensor(osq[:, 0:n * HD].rearrange("p (b c) -> p b c", b=2), o3, o3, ALU.mult))
                dve.tensor_reduce(ross[:, 0:n], osq[:, 0:n * HD].rearrange("p (n d) -> p n d", d=HD), AX,
                                  ALU.add).then_inc(ro_sq, 1)
                dve.wait_ge(ro_rstd, l + 1)
                for b in range(2):
                    ob3 = cz[0][:, b, 0:nt * P].rearrange("p (n d) -> p n d", d=HD)
                    rr = ross[:, b * 2 * nt:(b + 1) * 2 * nt].unsqueeze(2).broadcast_to([P, 2 * nt, HD])
                    ins = dve.tensor_tensor(ob3, ob3, rr, ALU.mult)
                    mark(ins) if b == 0 else step(ins)
                for b in range(2):
                    obt = cz[0][:, b, 0:nt * P].rearrange("p (t c) -> p t c", c=P)
                    on = onorm[:, l, b * P:(b + 1) * P].unsqueeze(1).broadcast_to([P, nt, P])
                    ins = dve.tensor_tensor(obt, obt, on, ALU.mult)
                    mark(ins) if b == 0 else step(ins)
                for b in range(2):
                    obt = cz[0][:, b, 0:nt * P].rearrange("p (t c) -> p t c", c=P)
                    ins = dve.tensor_tensor(obt, obt, cg[:, 0:nt, b * P:(b + 1) * P], ALU.mult)
                ins.then_inc(ro_out, 1)

            def attention(l):
                au = atts_of[l]
                for i in range(len(au) + 4):
                    if i < len(au):
                        a = au[i]
                        sbk, pb = PS[a.g % 2], PB[a.g % 2]
                        nl = (a.hi - a.lo) * P
                        s4 = stat[:, a.quad % 4]
                        m1, m2, m3, negm = [s4[:, w, a.h:a.h + 1] for w in range(4)]
                        sink = sinkv[:, l, a.h:a.h + 1]
                        if a.grp == "D" and a.t == 0 and a.h == 0:
                            dve.wait_ge(bias_in, 16 * (l + 1))
                            step(dve.tensor_scalar(U[:, 0:HEADS * BIAS_ROWS * 64], U[:, 0:HEADS * BIAS_ROWS * 64],
                                                   1.0 / SCALE, None, ALU.mult))
                        dve.wait_ge(sc_sum, a.g + 1)
                        if i == 0:
                            dve.wait_ge(ro_in, ro_parts(l + 1))
                        if nl and a.grp != "B":
                            if i >= 2:
                                dve.wait_ge(p_tp, au[i - 2].p_items[-1].index + 1)
                            mark(dve.tensor_reduce(m1, sbk[:, 512:768], AX, ALU.max))
                            if a.grp == "A":
                                at0 = P * (1 - (a.t - a.lo))
                                add = amask[:, at0:at0 + nl]
                            else:
                                e0 = 64 * (6 - 2 * a.t)
                                add = biasv[:, a.h, e0:e0 + nl]
                            step(dve.tensor_tensor_reduce(pb[:, 0:nl], sbk[:, 0:nl], add, SCALE, NEG * 8, ALU.add, ALU.max, m2))
                            step(dve.scalar_tensor_tensor(m3, m1, SCALE, m2, ALU.mult, ALU.max))
                            if a.grp == "A":
                                ins = dve.tensor_scalar(negm, m3, sink, -1.0, ALU.max, ALU.mult)
                            else:
                                ins = dve.tensor_scalar(negm, m3, -1.0, None, ALU.mult)
                            ins.then_inc(mx, 1)
                        else:
                            step(dve.tensor_reduce(m1, sbk[:, 512 - nl:768], AX, ALU.max))
                            if a.grp == "A":
                                step(dve.tensor_scalar(m3, m1, SCALE, sink, ALU.mult, ALU.max))
                                dve.tensor_scalar(negm, m3, -1.0, None, ALU.mult).then_inc(mx, 1)
                            else:
                                dve.tensor_scalar(negm, m1, -SCALE, None, ALU.mult).then_inc(mx, 1)
                    for o in items_at[l, i]:
                        if o.eng == "dve":
                            dve.wait_ge(p_tp, o.index + 1)
                            if o.a.g - au[0].g >= 2:
                                dve.wait_ge(o_pv, o.a.g - 1)
                            dve.tensor_copy(PT[o.a.g % 2][:, o.lo * P:o.hi * P],
                                            bank(4 + o.n % 2)[:, 0:(o.hi - o.lo) * P]).then_inc(pt_dve, 1)
                    if 2 <= i < len(au) + 2 and au[i - 2].h == HEADS - 1:
                        a = au[i - 2]
                        s4 = stat[:, a.quad % 4]
                        den = s4[:, 4, :]
                        dve.wait_ge(o_pv, a.g + 1)
                        dve.wait_ge(ex, a.g + 1)
                        if a.hi > a.lo and a.grp != "B":
                            step(dve.tensor_tensor(den, den, s4[:, 5, :], ALU.add))
                        if a.grp == "A":
                            step(dve.tensor_tensor(den, den, s4[:, 6, :], ALU.add))
                        step(dve.reciprocal(s4[:, 7, :], den))
                        if a.quad - au[0].quad >= 2:
                            dve.wait_ge(p_tp, quads[a.quad - 2].index + 1)
                        dve.tensor_tensor(OB[a.quad % 2].rearrange("p (h d) -> p h d", d=HD),
                                          bank(6 + a.quad % 2)[:, 0:256].rearrange("p (h d) -> p h d", d=HD),
                                          s4[:, 7, :].unsqueeze(2).broadcast_to([P, HEADS, HD]),
                                          ALU.mult).then_inc(o_norm, 1)

            def residual(m):
                l, i = res[m]
                nt, tb = tiles(l), tiles_before[m]

                def normalise(t):
                    b = bnb[:, (tb + t) % 3, :]
                    dve.wait_ge(rstd_ready, tb + t + 1)
                    dve.tensor_scalar(h3[:, t, :], h3[:, t, :], b[:, 12:13], b[:, 14:15], ALU.subtract,
                                      ALU.mult).then_inc(ln_norm, 1)

                for n in range(2):
                    for t in range(nt):
                        job = n * nt + t
                        if job == 0:
                            dve.wait_ge(ga_in, ga_before(m + 1))
                        dve.wait_ge(acc_sum, 2 * tb + job + 1)
                        tmp = gtmp[:, job % 2, :]
                        hs = h3[:, t, n * 512:(n + 1) * 512]
                        dve.tensor_tensor(tmp, bank((job + 4) % 8), gav[:, int(t >= NLT), n * 512:(n + 1) * 512],
                                          ALU.mult).then_inc(acc_read, 1)
                        dve.wait_ge(acc_read, 2 * tb + job + 1)
                        step(dve.scalar_tensor_tensor(hs, hs, ALPHA, tmp, ALU.mult, ALU.add))
                        if n == 1:
                            b = bnb[:, (tb + t) % 3, :]
                            if tb + t >= 3:
                                dve.wait_ge(ln_done, tb + t - 2)
                            mark(dve.bn_stats(b[:, 0:6], h3[:, t, 0:512]))
                            step(dve.bn_stats(b[:, 6:12], h3[:, t, 512:1024]))
                            dve.bn_aggr(b[:, 12:14], b[:, 0:12]).then_inc(bn_ready, 1)
                            if t >= 1:
                                normalise(t - 1)
                normalise(nt - 1)

            def ffn(l):
                segs = ((0, SEQ), (SEQ, TOK)) if has_ctx(l) else ((0, SEQ),)
                for u in ups_of[l]:
                    if u.kind == "mod":
                        dve.wait_ge(mod_sum, u.sum)
                        mod_out(u.l + 1, u.j, PS[u.pos][:, 0:4])
                        continue
                    jg = FT * l + u.j
                    y = (at, vt)[u.half][jg % 2]
                    jj = u.half * FT + u.j
                    ps = PS[u.pos]
                    dve.wait_ge(base_ready, u.c + 1)
                    for lo, hi in segs:
                        ins = dve.scalar_tensor_tensor(y[:, lo + 1:hi], ps[:, lo:hi - 1], convp[:, l, 0, jj:jj + 1],
                                                       y[:, lo + 1:hi], ALU.mult, ALU.add)
                        mark(ins)
                    dve.wait_ge(dve_step, steps[0])
                    for lo, hi in segs:
                        ins = dve.scalar_tensor_tensor(y[:, lo:hi - 1], ps[:, lo + 1:hi], convp[:, l, 2, jj:jj + 1],
                                                       y[:, lo:hi - 1], ALU.mult, ALU.add)
                    ins.then_inc(conv_done, 1)

            rs = [0]
            for l in range(DEPTH):
                modulate_context(2 * l)
                project(l)
                hgrn(l)
                attention(l)
                residual(2 * l)
                modulate_context(2 * l + 1)
                ffn(l)
                residual(2 * l + 1)

        @block.gpsimd
        def _(pool):
            steps = [0]

            def step(ins):
                steps[0] += 1
                ins.then_inc(pool_step, 1)
                pool.wait_ge(pool_step, steps[0])

            roots = [0]
            pool.wait_ge(halves, 1)

            def head_roots(l):
                for j in jobs_of[l]:
                    if j.rope and j.slot in (QB, KVB):
                        heads = 4 if j.slot == QB else 2
                        pool.wait_ge(ss_ready, roots[0] + 1)
                        for i in range(2):
                            ins = pool.tensor_tensor(rss[:, 8 + 4 * i:8 + 4 * i + heads], rss[:, 4 * i:4 * i + heads],
                                                     mhalf[:, 0:heads], ALU.pow)
                        ins.then_inc(root_ready, 1)
                        roots[0] += 1

            def hgrn(l):
                us = units_of[l]
                pool.wait_ge(e_in, e_end[l])
                for i in range(-3, len(us)):
                    if 0 <= i + 3 < len(us):
                        u = us[i + 3]
                        f = cz[u.d][:, u.b, u.t * P:(u.t + 1) * P]
                        y = YB[u.g % 2]
                        if u.g >= 2:
                            pool.wait_ge(lnr, u.g - 1)
                        if u.g >= 4 and units[u.g - 4].out:
                            pool.wait_ge(maps, 2 * units[u.g - 4].no + 2)
                        pool.tensor_scalar(y[:, 0:P], f, 2.0 ** -60, None, ALU.max)
                        step(pool.tensor_scalar(y[:, P:2 * P], f, 2.0 ** -60, 2.0 ** 60, ALU.min, ALU.mult))
                        pool.tensor_scalar(y[:, P:2 * P], y[:, P:2 * P], 2.0 ** -63, None, ALU.max)
                        pool.tensor_scalar(KB[u.g % 4], f, -1.0, 1.0, ALU.mult, ALU.add).then_inc(yk, 1)
                    if 0 <= i + 1 < len(us):
                        u = us[i + 1]
                        pool.wait_ge(expd, u.g + 1)
                        pool.wait_ge(yk, u.g + 1)
                        if u.g >= 2:
                            w = units[u.g - 2]
                            if w.out:
                                pool.wait_ge(maps, 2 * w.no + 2)
                            if w.state:
                                pool.wait_ge(kdt, w.ns + 1)
                        lo = 0 if u.out else 7
                        pool.tensor_tensor(KE[u.g % 2][:, lo:8, :], EX[u.g % 2][:, 1 + lo:9, :],
                                           KB[u.g % 4].unsqueeze(1).broadcast_to([P, 8 - lo, P]), ALU.mult).then_inc(ke, 1)
                n = 2 * tiles(l) * 2
                pool.wait_ge(ro_sq, l + 1)
                step(pool.tensor_scalar(ross[:, 0:n], ross[:, 0:n], 1.0 / HD, EPS, ALU.mult, ALU.add))
                pool.tensor_tensor(ross[:, 0:n], ross[:, 0:n], mhalf[:, 0:n], ALU.pow).then_inc(ro_rstd, 1)

            def layer_norm(m):
                l, i = res[m]
                nt, tb = tiles(l), tiles_before[m]

                def affine(t):
                    pool.wait_ge(ln_norm, tb + t + 1)
                    pool.wait_ge(ln_in, 16 * (m + 1))
                    step(pool.tensor_tensor(h3[:, t, :], h3[:, t, :], lnp[:, 0:1024], ALU.mult))
                    pool.tensor_tensor(h3[:, t, :], h3[:, t, :], lnp[:, 1024:2048], ALU.add).then_inc(ln_done, 1)

                for t in range(nt):
                    b = bnb[:, (tb + t) % 3, :]
                    pool.wait_ge(bn_ready, tb + t + 1)
                    step(pool.tensor_scalar(b[:, 14:15], b[:, 13:14], EPS, None, ALU.add))
                    pool.tensor_tensor(b[:, 14:15], b[:, 14:15], mhalf[:, 0:1], ALU.pow).then_inc(rstd_ready, 1)
                    if t >= 1:
                        affine(t - 1)
                affine(nt - 1)

            def gated(l):
                n = TOK if has_ctx(l) else SEQ
                for j in range(FT):
                    jg = FT * l + j
                    pool.wait_ge(gate_ready, jg + 1)
                    pool.wait_ge(conv_done, 2 * jg + 2)
                    pool.tensor_tensor(g3[:, j, 0:n], sl[jg % 2][:, 0:n], vt[jg % 2][:, 0:n], ALU.mult).then_inc(hid_ready, 1)

            for l in range(DEPTH):
                head_roots(l)
                hgrn(l)
                layer_norm(2 * l)
                gated(l)
                layer_norm(2 * l + 1)


def constants():
    import numpy as np

    f = np.float32
    t = np.arange(SEQ)
    pos = np.stack([t // GRID_W, t % GRID_W], -1).astype(f)
    nf = HD // 4
    inv = (f(10000.0) ** (-np.arange(nf, dtype=f) / f(nf))).astype(f)
    ang = (pos[:, :, None] * inv).astype(f)
    cos, sin = np.cos(ang), np.sin(ang)
    c = np.stack([cos, cos], 2).reshape(SEQ, HD)
    s = np.stack([-sin, sin], 2).reshape(SEQ, HD)
    rows = lambda a: a.reshape(NLT, P, HD).transpose(1, 0, 2).reshape(P, -1)
    i, j = np.arange(P)[:, None], np.arange(P)[None, :]
    am = np.concatenate([np.where(j >= i, 0, NEG), np.zeros((P, P)), np.where(j <= i, 0, NEG)], 1)
    cn = np.concatenate([np.eye(P), rows(c), rows(s), am], 1).astype(f)
    mk = np.zeros((P, 2, 8, P), f)
    for m in range(LEVELS):
        h = P >> (m + 1)
        same = (i // (2 * h)) == (j // (2 * h))
        mk[:, 0, m, :] = same & (i % (2 * h) < h) & (j % (2 * h) >= h)
        mk[:, 1, m, :] = same & (i % (2 * h) >= h) & (j % (2 * h) < h)
    mk[:, :, 7, :] = (i == j)[:, None, :]
    return cn, mk.reshape(P, -1)


def kernel(x, c, ctx, c_ctx, w_mod, b_mod, w_in, w_out, ln_g, ln_b, attn_sink, qk_norm, hgrn_lb_logits,
           hgrn_onorm, na_rpb, ffn_w_up, ffn_conv_w, ffn_conv_b, ffn_w_down):
    import numpy as np
    import concourse.bacc as bacc
    from concourse.bass_utils import run_bass_kernel_spmd

    A = np.asarray
    f = np.float32
    w_mod, w_in, w_out, w_up, w_down = A(w_mod), A(w_in), A(w_out), A(ffn_w_up), A(ffn_w_down)
    weights = np.zeros((len(STREAM), P, SLOT), f)
    for n, (kind, l, i, g) in enumerate(STREAM):
        if kind == "up":
            w = w_up[l].reshape(KT, P, 2, FT, P)[:, :, :, i, :].transpose(1, 0, 2, 3)
        elif kind in ("mod", "in"):
            w = (w_mod if kind == "mod" else w_in)[l][:, i * 256:(i + 1) * 256].reshape(KT, P, 256).transpose(1, 0, 2)
            if kind == "in" and i in (QA, QB):
                w = w.reshape(P, KT, 2, 2, HD).transpose(0, 1, 3, 2, 4)
        else:
            w = (w_out if kind == "out" else w_down)[l][g * KDN * P:(g + 1) * KDN * P, i * 512:(i + 1) * 512]
            w = w.reshape(-1, P, 512).transpose(1, 0, 2)
        w = w.reshape(P, -1)
        weights[n, :, :w.shape[1]] = w
    cn, mk = constants()
    per = lambda a: np.moveaxis(a.reshape(a.shape[:-1] + (-1, P)), -1, 0)
    every = lambda a: np.broadcast_to(a.reshape(1, -1), (P, a.size))
    cv = np.stack([per(A(c)[0]), per(A(c_ctx))], -1)
    conv = np.concatenate([A(ffn_conv_w), A(ffn_conv_b)[:, None, :]], 1)
    lbl = per(A(hgrn_lb_logits)).transpose(0, 2, 1, 3)
    params = np.concatenate([q.reshape(P, -1) for q in (
        cv, per(A(b_mod)), per(conv), lbl, every(A(qk_norm)), every(A(hgrn_onorm)), every(A(attn_sink)))], 1)
    rpb = A(na_rpb)
    bias = np.full((DEPTH, 2, GRID_W, HEADS, BIAS_ROWS, GRID_W), NEG, f)
    for col in range(GRID_W):
        c0 = min(max(col - NA_COLS // 2, 0), GRID_W - NA_COLS)
        o0 = c0 - col + NA_COLS - 1
        for a in range(2):
            bias[:, a, col, :, :, c0:c0 + NA_COLS] = rpb[:, :, 1 - a:1 - a + BIAS_ROWS, o0:o0 + NA_COLS]
    bias = bias.reshape(DEPTH, P, HEADS, BIAS_ROWS * GRID_W)
    ln_rows = np.concatenate([A(ln_g), A(ln_b)], -1).reshape(2 * DEPTH, 2 * D_MODEL)
    arrays = {"weights": weights, "x": A(x)[0], "ctx": A(ctx)[0], "consts": cn, "masks": mk,
              "params": params, "bias": bias, "ln_rows": ln_rows}
    arrays = {k: np.ascontiguousarray(v) for k, v in arrays.items()}
    nc = bacc.Bacc("TRN2", target_bir_lowering=False, num_devices=1)
    aps = [nc.dram_tensor(f"in_{k}", v.shape, mybir.dt.from_np(v.dtype), kind="ExternalInput").ap()
           for k, v in arrays.items()]
    out = nc.dram_tensor("out_h", (SEQ, D_MODEL), mybir.dt.float32, kind="ExternalOutput").ap()
    hybrid_backbone(nc, *aps, out)
    r = run_bass_kernel_spmd(nc, [{f"in_{k}": v for k, v in arrays.items()}], core_ids=[0])
    return r.results[0]["out_h"].reshape(1, SEQ, D_MODEL)
```

```python
import concourse.bass as bass
from concourse import mybir
from contextlib import ExitStack
import math

D_MODEL, SEQ, CTX, DEPTH = 1024, 512, 256, 2
P = 128
KT = D_MODEL // P
TOK = SEQ + CTX
NLT, NCT = SEQ // P, CTX // P
NT = NLT + NCT
HEADS, HD = 4, 64
D_FF = 256 * ((8 * D_MODEL // 3 + 255) // 256)
FT = D_FF // P
ALPHA = (2 * DEPTH) ** 0.25
EPS = 1e-6
SCALE = HD ** -0.5
NEG = -1e30
LEVELS = 7
GRID_W, NA_ROWS, NA_COLS = 64, 8, 16
BIAS_ROWS = 2 * NA_ROWS - 2

SLOT = 2048
RING = 3
KDN = 4
DN_GROUPS = -(-FT // KDN)
QA, KVA, QB, KVB, QC, IC, FCF, FCB, GC, QD, KD, VD = range(12)
IN_ORDER = (QC, GC, IC, FCF, FCB, QA, KVA, QB, KVB, QD, KD, VD)
FEATURE = (QC, FCF, FCB, QD, KD)
LATENT_ONLY = (QA, QB, QC, GC, QD)
OWN_SLOTS = 9
MOD_FIRST = 8


def weight_stream():
    s = [("mod", 0, i, 0) for i in range(MOD_FIRST)]
    for l in range(DEPTH):
        extra = list(range(MOD_FIRST, 24)) if l == 0 else []
        for n, i in enumerate(IN_ORDER):
            s.append(("in", l, i, 0))
            for _ in range(2):
                if extra:
                    s.append(("mod", 0, extra.pop(0), 0))
        assert not extra
        s += [("out", l, n, g) for n in range(2) for g in range(KT // KDN)]
        nxt = list(range(24)) if l + 1 < DEPTH else []
        for j in range(FT):
            s.append(("up", l, j, 0))
            for _ in range(2 if j < 2 else 1):
                if nxt:
                    s.append(("mod", l + 1, nxt.pop(0), 0))
        assert not nxt
        s += [("down", l, n, g) for n in range(2) for g in range(DN_GROUPS)]
    return s


STREAM = weight_stream()
SLOT_AT = {key: n for n, key in enumerate(STREAM)}


def hybrid_backbone(nc, weights, x, ctx_in, consts, masks, params, bias_d, ln_rows, out):
    f32, u8 = mybir.dt.float32, mybir.dt.uint8
    ALU, ACT, AX = mybir.AluOpType, mybir.ActivationFunctionType, mybir.AxisListType.X
    stack = ExitStack()

    def sb(name, cols, dt=f32):
        return stack.enter_context(nc.sbuf_tensor(name, [P, cols], dt))

    def sem(name):
        return stack.enter_context(nc.semaphore(name))

    with stack:
        H = sb("H", NT * D_MODEL)
        X = sb("X", KT * TOK)
        U = sb("U", 21504)
        W = sb("W", 9984)
        WR = sb("WR", RING * SLOT)
        CN = sb("CN", 1024)
        MK = sb("MK", 2 * LEVELS * 64, u8)
        PR = sb("PR", 1312)
        MOD = sb("MOD", DEPTH * 96)
        SC = sb("SC", 104)
        ST = sb("ST", 4 * 32 + 64 + 64)
        PS = [stack.enter_context(nc.psum_tensor(f"PS{i}", [P, 1024], f32)) for i in range(4)]

        def bank(n, cols=512):
            return PS[n // 2][:, (n % 2) * 512:(n % 2) * 512 + cols]

        h3 = H[:, :].rearrange("p (t d) -> p t d", t=NT)
        x3 = X[:, :].rearrange("p (k t) -> p k t", k=KT)

        def uview(at, blocks, cols):
            return U[:, at:at + blocks * cols].rearrange("p (b c) -> p b c", b=blocks)

        cq, ci = uview(0, 2, TOK), uview(1536, NT, 256)
        cz = [uview(4608, 2, TOK), uview(3072, 2, TOK)]
        cg = uview(6144, NT, 256)
        qT = {"A": uview(7680, 2, TOK), "B": uview(11520, 2, TOK), "D": uview(15360, 2, TOK)}
        kT = {"A": uview(9216, 2, TOK), "B": uview(13056, 2, TOK), "D": uview(16896, 4, TOK)}
        vv = {"A": uview(10752, NT, 128), "B": uview(14592, NT, 128), "D": uview(19968, NT, 256)}
        biasv = U[:, 0:HEADS * BIAS_ROWS * 64].rearrange("p (h e) -> p h e", h=HEADS)
        g3 = uview(0, FT, TOK)

        ident = CN[:, 0:128]
        cosv = CN[:, 128:384].rearrange("p (t d) -> p t d", t=NLT)
        sinv = CN[:, 384:640].rearrange("p (t d) -> p t d", t=NLT)
        amask = CN[:, 640:1024]
        mk4 = MK[:, :].rearrange("p (d m t) -> p d m t", d=2, m=LEVELS)
        cvec = PR[:, 0:16]
        bmod = PR[:, 16:112].rearrange("p (l j) -> p l j", l=DEPTH)
        convp = PR[:, 112:464].rearrange("p (l w j) -> p l w j", l=DEPTH, w=4)
        lbl = PR[:, 464:472].rearrange("p (l e) -> p l e", l=DEPTH)
        qkn = PR[:, 472:728].rearrange("p (l w d) -> p l w d", l=DEPTH, w=2)
        onorm = PR[:, 728:1240].rearrange("p (l c) -> p l c", l=DEPTH)
        sinkv = PR[:, 1240:1248].rearrange("p (l h) -> p l h", l=DEPTH)
        scv = SC[:, 0:16].rearrange("p (k v) -> p k v", k=KT)
        lb4 = SC[:, 16:24].rearrange("p (l e) -> p l e", l=DEPTH)
        oml4 = SC[:, 24:32].rearrange("p (l e) -> p l e", l=DEPTH)
        lbt = SC[:, 32:48].rearrange("p (a e) -> p a e", a=4)
        cexp = SC[:, 48:64]
        sel = SC[:, 96:98]
        ones = SC[:, 98:99]
        mhalf = SC[:, 64:64 + 32]
        mod3 = MOD[:, :].rearrange("p (l j v) -> p l j v", l=DEPTH, j=48)
        ring = WR[:, :].rearrange("p (r c) -> p r c", r=RING)

        raw = W[:, 0:1536].rearrange("p (r c) -> p r c", r=3)
        rot = W[:, 1536:3072].rearrange("p (r c) -> p r c", r=3)
        ra = W[:, 3072:3584]
        rb = W[:, 3584:4096]
        rss = W[:, 4096:4112]
        macc = W[:, 5120:6144].rearrange("p (r v c) -> p r v c", r=2, v=2)
        EX = [W[:, i * 1152:(i + 1) * 1152].rearrange("p (e t) -> p e t", e=9) for i in range(2)]
        QE = [W[:, 2304 + i * 1024:2304 + (i + 1) * 1024].rearrange("p (e t) -> p e t", e=8) for i in range(2)]
        KE = [W[:, 4352 + i * 1024:4352 + (i + 1) * 1024].rearrange("p (e t) -> p e t", e=8) for i in range(2)]
        YB = [W[:, 6400 + i * 256:6400 + (i + 1) * 256] for i in range(2)]
        QK = [W[:, 6912 + i * 128:6912 + (i + 1) * 128] for i in range(2)]
        KB = [W[:, 7424 + i * 128:7424 + (i + 1) * 128] for i in range(4)]
        CB = [W[:, 7936 + i * 128:7936 + (i + 1) * 128] for i in range(2)]
        AT = [[W[:, 8192 + (2 * d + i) * 256:8192 + (2 * d + i + 1) * 256].rearrange("p (h t) -> p h t", h=2)
               for i in range(2)] for d in range(2)]
        SS = W[:, 9216:9728].rearrange("p (d b v) -> p d b v", d=2, b=2)
        KDT = [W[:, 9728 + i * 128:9728 + (i + 1) * 128] for i in range(2)]
        osq = W[:, 0:1536]
        PB = [W[:, i * 768:(i + 1) * 768] for i in range(3)]
        PT = [W[:, 2304 + i * 768:2304 + (i + 1) * 768] for i in range(2)]
        OB = [W[:, 3840 + i * 256:3840 + (i + 1) * 256] for i in range(2)]
        stat = ST[:, 0:128].rearrange("p (q s h) -> p q s h", q=4, s=8)
        lnp = W[:, 0:2048]
        gav = W[:, 2048:4096].rearrange("p (v c) -> p v c", v=2)
        gtmp = W[:, 4096:5120].rearrange("p (r c) -> p r c", r=2)
        bnb = ST[:, 128:128 + 48].rearrange("p (r c) -> p r c", r=3)
        ross = ST[:, 192:192 + 24]
        DEC = ST[:, 216:220]
        at = [W[:, i * 768:(i + 1) * 768] for i in range(2)]
        vt = [W[:, 1536 + i * 768:1536 + (i + 1) * 768] for i in range(2)]
        sl = [W[:, 3072 + i * 768:3072 + (i + 1) * 768] for i in range(2)]

        w_arrived = [sem(f"w_arrived{r}") for r in range(RING)]
        slot_read = sem("slot_read")
        consts_in = sem("consts_in")
        h_in = sem("h_in")
        sc_ready = sem("sc_ready")
        e_lb = sem("e_lb")
        halves = sem("halves")
        bias_in = sem("bias_in")
        ln_in = sem("ln_in")
        out_stored = sem("out_stored")
        dve_step = sem("dve_step")
        pool_step = sem("pool_step")
        act_step = sem("act_step")
        mod_sum = sem("mod_sum")
        mod_done = sem("mod_done")
        tp_lat = sem("tp_lat")
        tp_ctx = sem("tp_ctx")
        x_lat = sem("x_lat")
        x_ctx = sem("x_ctx")
        job_sum = sem("job_sum")
        job_act = sem("job_act")
        roped = sem("roped")
        rot_tp = sem("rot_tp")
        qk_in = sem("qk_in")
        ss_ready = sem("ss_ready")
        root_ready = sem("root_ready")
        e_in = sem("e_in")
        yk = sem("yk")
        lnr = sem("lnr")
        subs = sem("subs")
        expd = sem("expd")
        qe = sem("qe")
        ke = sem("ke")
        maps = sem("maps")
        kdt = sem("kdt")
        kd_in = sem("kd_in")
        atd = sem("atd")
        o_sum = sem("o_sum")
        kv_sum = sem("kv_sum")
        o_out = sem("o_out")
        s_new = sem("s_new")
        ro_sq = sem("ro_sq")
        ro_rstd = sem("ro_rstd")
        ro_out = sem("ro_out")
        ro_tp = sem("ro_tp")
        ro_in = sem("ro_in")
        sc_sum = sem("sc_sum")
        mx = sem("mx")
        ex = sem("ex")
        p_tp = sem("p_tp")
        pt_act = sem("pt_act")
        pt_dve = sem("pt_dve")
        o_pv = sem("o_pv")
        o_norm = sem("o_norm")
        ga_sum = sem("ga_sum")
        ga_in = sem("ga_in")
        acc_sum = sem("acc_sum")
        acc_read = sem("acc_read")
        bn_ready = sem("bn_ready")
        rstd_ready = sem("rstd_ready")
        ln_norm = sem("ln_norm")
        ln_done = sem("ln_done")
        up_sum = sem("up_sum")
        base_ready = sem("base_ready")
        conv_done = sem("conv_done")
        gate_ready = sem("gate_ready")
        hid_ready = sem("hid_ready")
        zeroed = sem("zeroed")
        mac_done = sem("mac_done")
        padded = sem("padded")

        def has_ctx(l):
            return l + 1 < DEPTH

        def tiles(l):
            return NT if has_ctx(l) else NLT

        class Job:
            pass

        jobs = []
        for l in range(DEPTH):
            order = [k for k in STREAM if (k[0] == "in" and k[1] == l)
                     or (k[0] == "mod" and l == 0 and k[2] >= MOD_FIRST and k[1] == 0)]
            for key in order:
                kind, _, s, _ = key
                parts = []
                if kind == "mod":
                    parts = [("mod", s, 0)]
                else:
                    with_ctx = has_ctx(l) or s not in LATENT_ONLY
                    if s in FEATURE:
                        parts = [("feat", b, w) for b in range(2) for w in range(1 + with_ctx)]
                    else:
                        parts = [("tok", p, 0) for p in range(2 + with_ctx)]
                for n, (kind, a, b) in enumerate(parts):
                    j = Job()
                    j.l, j.slot, j.kind, j.a, j.b, j.key = l, s, kind, a, b, key
                    j.first, j.last = n == 0, n == len(parts) - 1
                    j.rope = kind == "tok" and s in (QA, KVA, QB, KVB)
                    jobs.append(j)
        n_act = n_rope = n_e = 0
        n_dve = MOD_FIRST
        for j in jobs:
            if j.kind == "mod":
                n_dve += 1
            else:
                n_act += 1
            j.after = (n_act, n_dve)
            if j.rope:
                j.r = n_rope
                n_rope += 1
            j.is_e = j.slot in (FCF, FCB) and j.kind == "feat"
            if j.is_e:
                n_e += 1
                j.e = n_e
        jobs_of = [[j for j in jobs if j.l == l] for l in range(DEPTH)]
        own_of = [[j for j in js if j.kind == "mod" or j.slot in IN_ORDER[:OWN_SLOTS]] for js in jobs_of]
        beside_of = [[j for j in js if j not in own] for js, own in zip(jobs_of, own_of)]
        n_sum = n_mac = 0
        for j in jobs:
            if j.kind == "mod":
                n_mac += 1
                j.mac = n_mac
            else:
                n_sum += 1
                j.sum = n_sum
        for l in range(DEPTH):
            js = jobs_of[l]
            real = [j for j in js if j.kind != "mod"]
            own = [j for j in real if j.slot in IN_ORDER[:OWN_SLOTS]]
            for n, j in enumerate(real):
                j.bank = n % 2
                j.freed = real[n - 2].after[0] if n >= 2 else None
                j.turns = [real[n - 2]] if n >= 2 and real[n - 2].rope else []
                if j is own[-1]:
                    j.turns += [q for q in real[n - 1:n + 1] if q.rope]
                elif j not in own:
                    j.turns = []
            for j in js:
                if j.kind == "mod":
                    j.turns = []

        units = []
        n_out = n_st = n_u = 0
        for l in range(DEPTH):
            for d in range(2):
                order = [NLT + c for c in range(NCT)][::1 - 2 * d] + list(range(NLT))[::1 - 2 * d]
                for step, t in enumerate(order):
                    for b in range(2):
                        u = Job()
                        u.l, u.d, u.t, u.b, u.step, u.g = l, d, t, b, step, n_u
                        n_u += 1
                        u.out = t < NLT or has_ctx(l)
                        u.state = step < NT - 1
                        u.no, u.ns = n_out, n_st
                        n_out += u.out
                        n_st += u.state
                        units.append(u)
        units_of = [[u for u in units if u.l == l] for l in range(DEPTH)]
        beside = {}
        for l in range(DEPTH):
            n, m = len(units_of[l]) + 1, len(beside_of[l])
            for i in range(n):
                beside[l, i] = beside_of[l][i * m // n:(i + 1) * m // n]

        atts = []
        for l in range(DEPTH):
            for g in "ABD":
                for t in range(tiles(l)):
                    for hd in range(HEADS):
                        a = Job()
                        a.l, a.grp, a.t, a.h, a.g, a.quad = l, g, t, hd, len(atts), len(atts) // HEADS
                        if t >= NLT:
                            a.lo, a.hi = 0, 0
                        elif g == "A":
                            a.lo, a.hi = max(0, t - 1), min(NLT, t + 2)
                        else:
                            a.lo, a.hi = 0, NLT
                        a.p_items = []
                        a.keys = list(range(a.lo, a.hi)) + [NLT + c for c in range(NCT)]
                        atts.append(a)
        atts_of = [[a for a in atts if a.l == l] for l in range(DEPTH)]
        LAG = 2
        n_pa = n_pd = 0
        items_at = {}
        flat = []
        for l in range(DEPTH):
            au = atts_of[l]
            first_item = len(flat)
            for i in range(len(au) + LAG + 3):
                its = []
                if LAG <= i < len(au) + LAG:
                    a = au[i - LAG]
                    cuts = [0, min(3, len(a.keys)), len(a.keys)]
                    for n in range(2):
                        if cuts[n + 1] > cuts[n]:
                            its.append(("p", a, cuts[n], cuts[n + 1], "act" if n == 0 else "dve"))
                if LAG + 2 <= i < len(au) + LAG + 2 and au[i - LAG - 2].h == HEADS - 1:
                    its.append(("o", au[i - LAG - 2], 0, 2, "act"))
                made = []
                for it in its:
                    o = Job()
                    o.kind, o.a, o.lo, o.hi, o.eng = it
                    if o.eng == "act":
                        n_pa += 1
                    else:
                        n_pd += 1
                    o.done = (n_pa, n_pd)
                    o.n = len(flat) - first_item
                    o.index = len(flat)
                    o.prev = flat[-2].done if o.n >= 2 else None
                    flat.append(o)
                    made.append(o)
                items_at[l, i] = made
        quads = []
        for o in flat:
            if o.kind == "p":
                o.a.p_items.append(o)
            else:
                quads.append(o)

        ups = []
        n_c = n_m = 0
        for key in STREAM:
            if key[0] == "up":
                for half in range(2):
                    u = Job()
                    u.kind, u.l, u.j, u.half, u.key = "up", key[1], key[2], half, key
                    u.c = n_c
                    n_c += 1
                    ups.append(u)
            elif key[0] == "mod" and key[1] > 0:
                u = Job()
                u.kind, u.l, u.j, u.key = "mod", key[1] - 1, key[2], key
                ups.append(u)
        n_m = 24
        c = 0
        for u in ups:
            if u.kind == "mod":
                n_m += 1
            else:
                c += 1
            u.done = (c, n_m)
        ups_of = [[u for u in ups if u.l == l] for l in range(DEPTH)]
        for l in range(DEPTH):
            for n, u in enumerate(ups_of[l]):
                u.pos = n % 4
                u.freed = ups_of[l][n - 4].done if n >= 4 else None

        stages = [(0, 0, True), (0, 24, True), (1, 0, True), (1, 24, False)]
        ctx_before = [KT * sum(s[2] for s in stages[:m]) for m in range(5)]
        res = [(l, i) for l in range(DEPTH) for i in range(2)]
        tiles_before = [sum(tiles(l) for l, _ in res[:m]) for m in range(5)]
        e_end = [sum(j.is_e for j in jobs if j.l <= l) for l in range(DEPTH)]

        def ga_before(m):
            return sum(4 if has_ctx(l) else 2 for l, _ in res[:m])

        def ro_parts(n):
            return sum(4 if has_ctx(l) else 2 for l in range(n))

        def flat_end(l):
            return [o for o in flat if o.a.l <= l][-1].done

        release = {}
        for i in range(MOD_FIRST):
            release["mod", 0, i, 0] = (mod_sum, i + 1)
        for j in jobs:
            release[j.key] = (mac_done, j.mac) if j.kind == "mod" else (job_sum, j.sum)
        for u in ups:
            if u.kind == "mod":
                n_mac += 1
                u.mac = n_mac
                release[u.key] = (mac_done, u.mac)
            else:
                release[u.key] = (up_sum, u.c + 1)
        n_read = 0
        for m, (l, i) in enumerate(res):
            groups = KT // KDN if i == 0 else DN_GROUPS
            for n in range(2):
                for g in range(groups):
                    if g < groups - (1 if n == 0 else 2):
                        n_read += 1
                        release["down" if i else "out", l, n, g] = (slot_read, n_read)
                    else:
                        release["down" if i else "out", l, n, g] = (
                            acc_sum, 2 * tiles_before[m] + (n + 1) * tiles(l))

        def wait_all(eng, *pairs):
            for s, v in pairs:
                if v > 0:
                    eng.wait_ge(s, v)

        def att_end(l):
            return len([a for a in atts if a.l <= l])

        def unit_end(l):
            us = [u for u in units if u.l <= l]
            return len(us), sum(u.out for u in us), sum(u.state for u in us)

        def mods_done(l):
            return 24 * (l + 1)

        block = stack.enter_context(nc.Block())

        @block.sync
        def _(sp):
            for dst, src in ((PR[:, 0:1248], params), (CN[:, :], consts), (W[:, 0:2 * LEVELS * 64], masks)):
                sp.dma_start(dst, src).then_inc(consts_in, 16)
            sp.dma_start(h3[:, 0:NLT, :], x.rearrange("(t p) d -> p t d", p=P)).then_inc(h_in, 16)
            sp.dma_start(h3[:, NLT:NT, :], ctx_in.rearrange("(t p) d -> p t d", p=P)).then_inc(h_in, 16)
            for n, key in enumerate(STREAM):
                if n >= RING:
                    sp.wait_ge(*release[STREAM[n - RING]])
                half = key[0] == "down" and key[3] == DN_GROUPS - 1 and FT % KDN
                cols = (FT % KDN) * 512 if half else SLOT
                sp.dma_start(ring[:, n % RING, 0:cols], weights[n, :, 0:cols]).then_inc(w_arrived[n % RING], 16)

        @block.tensor
        def _(pe):
            def slot(key):
                n = SLOT_AT[key]
                pe.wait_ge(w_arrived[n % RING], 16 * (n // RING + 1))
                return ring[:, n % RING, :]

            def mod_products(wk, b):
                for jj in range(2):
                    for k in range(KT):
                        mm = pe.matmul(bank(b)[:, 2 * jj:2 * jj + 2], wk[:, k, jj * P:(jj + 1) * P], scv[:, k, :],
                                       start=(k == 0), stop=(k == KT - 1))
                mm.then_inc(mod_sum, 1)

            def mod_sums(mac, out4):
                pe.wait_ge(mac_done, mac)
                for jj in range(2):
                    for v in range(2):
                        mm = pe.matmul(out4[:, 2 * jj + v:2 * jj + v + 1], macc[:, mac % 2, v, jj * P:(jj + 1) * P], ones,
                                       start=True, stop=True)
                mm.then_inc(mod_sum, 1)

            pe.wait_ge(consts_in, 48)
            pe.wait_ge(sc_ready, 1)
            for i in range(MOD_FIRST):
                mod_products(slot(("mod", 0, i, 0)).rearrange("p (k c) -> p k c", k=KT), i)

            def transposes(m):
                l, _, with_ctx = stages[m]
                if m == 0:
                    pe.wait_ge(h_in, 32)
                    pe.wait_ge(mod_done, MOD_FIRST)
                for k in range(KT):
                    a = KT * m + k
                    if k >= 2:
                        pe.wait_ge(x_lat, a - 1)
                    for t in range(NLT):
                        if m > 0 and k == 0:
                            pe.wait_ge(ln_done, tiles_before[m - 1] + t + 1)
                        mm = pe.transpose(bank(k % 2)[:, t * P:(t + 1) * P], h3[:, t, k * P:(k + 1) * P], ident)
                    mm.then_inc(tp_lat, 1)
                if with_ctx:
                    for k in range(KT):
                        c = ctx_before[m] + k
                        if k >= 2:
                            pe.wait_ge(x_ctx, c - 1)
                        if m > 0 and k == 0:
                            pe.wait_ge(ln_done, tiles_before[m])
                        for t in range(NCT):
                            mm = pe.transpose(bank(2 + k % 2)[:, t * P:(t + 1) * P],
                                              h3[:, NLT + t, k * P:(k + 1) * P], ident)
                        mm.then_inc(tp_ctx, 1)
                pe.wait_ge(x_lat, KT * (m + 1))
                if with_ctx:
                    pe.wait_ge(x_ctx, ctx_before[m + 1])

            ws = [None]

            def projections(l, js):
                for j in js:
                    if j.kind == "mod":
                        pe.wait_ge(mod_done, MOD_FIRST + j.mac - 1)
                        mod_sums(j.mac, bank(5))
                        continue
                    if j.first:
                        ws[0] = slot(j.key)
                    wk = ws[0].rearrange("p (k c) -> p k c", k=KT)
                    if j.freed:
                        pe.wait_ge(job_act, j.freed)
                    if j.kind == "feat":
                        lo, hi = (0, SEQ) if j.b == 0 else (SEQ, TOK)
                        for k in range(KT):
                            mm = pe.matmul(bank(j.bank)[:, 0:hi - lo], wk[:, k, j.a * P:(j.a + 1) * P],
                                           x3[:, k, lo:hi], start=(k == 0), stop=(k == KT - 1))
                    else:
                        for i in range(2):
                            t = 2 * j.a + i
                            for k in range(KT):
                                mm = pe.matmul(bank(j.bank)[:, i * 256:(i + 1) * 256], x3[:, k, t * P:(t + 1) * P],
                                               wk[:, k, :], start=(k == 0), stop=(k == KT - 1))
                    mm.then_inc(job_sum, 1)
                    for q in j.turns:
                        pe.wait_ge(roped, q.r + 1)
                        if q.r >= 2:
                            pe.wait_ge(qk_in, q.r - 1)
                        tb = bank(6 + q.r % 2)
                        r3 = rot[:, q.r % 3, :].rearrange("p (i c) -> p i c", i=2)
                        if q.slot in (QA, QB):
                            for g in range(2):
                                for i in range(2):
                                    mm = pe.transpose(tb[:, g * 256 + i * P:g * 256 + (i + 1) * P],
                                                      r3[:, i, g * P:(g + 1) * P], ident)
                        else:
                            for i in range(2):
                                mm = pe.transpose(tb[:, i * P:(i + 1) * P], r3[:, i, 0:P], ident)
                        mm.then_inc(rot_tp, 1)

            def hgrn(l):
                us = units_of[l]
                wait_all(pe, (mod_done, own_of[l][-1].after[1]), (qk_in, max(j.r for j in jobs_of[l] if j.rope) + 1))

                def score_maps(u):
                    par = u.g % 2
                    pe.wait_ge(qe, u.no + 1)
                    pe.wait_ge(ke, u.g + 1)
                    if u.no >= 2:
                        pe.wait_ge(atd, u.no - 1)
                    for m in range(LEVELS):
                        for hh in range(2):
                            rows = slice(64 * hh, 64 * hh + 64)
                            later = QE[par][rows, 1 + m, :].rearrange("p (n f t) -> p n f t", f=2, t=P >> (m + 1))
                            mm = pe.matmul(bank(2 + 2 * (u.no % 2) + hh)[:, m * 64:(m + 1) * 64], KE[par][rows, m, :],
                                           later[:, :, 1 - u.d, :], start=True, stop=True)
                    mm.then_inc(maps, 1)

                def turn_keys(u):
                    pe.wait_ge(ke, u.g + 1)
                    if u.ns >= 1:
                        pe.wait_ge(s_new, u.ns)
                    pe.transpose(bank(6)[:, 0:P], KE[u.g % 2][:, 7, :], ident).then_inc(kdt, 1)

                def outputs(u):
                    vslice = ci[:, u.t, u.b * P:(u.b + 1) * P]
                    if u.out:
                        ob = bank(7)
                        pe.wait_ge(atd, u.no + 1)
                        if u.no >= 1:
                            pe.wait_ge(o_out, u.no)
                        if u.step >= 1:
                            prev = [w for w in us if w.d == u.d and w.b == u.b and w.step == u.step - 1][0]
                            pe.wait_ge(s_new, prev.ns + 1)
                        pe.wait_ge(zeroed, l + 1)
                        pe.matmul(ob[:, P:P + 2], QK[u.g % 2], sel, start=True, stop=True)
                        for hh in range(2):
                            oh = ob[:, hh * 64:(hh + 1) * 64]
                            pe.matmul(oh, QE[u.g % 2][:, 0, :], SS[:, u.d, u.b, hh * 64:(hh + 1) * 64],
                                      start=True, stop=False)
                            mm = pe.matmul(oh, AT[u.d][u.no % 2][:, hh, :], vslice[:, hh * 64:(hh + 1) * 64],
                                           start=False, stop=True)
                        mm.then_inc(o_sum, 1)
                    if u.state:
                        pe.wait_ge(kd_in, u.ns + 1)
                        pe.matmul(bank(6)[:, 0:P], KDT[u.ns % 2], vslice, start=True, stop=True).then_inc(kv_sum, 1)

                for i in range(len(us) + 1):
                    if i < len(us) and us[i].out:
                        score_maps(us[i])
                    if i >= 1:
                        outputs(us[i - 1])
                    if i < len(us) and us[i].state:
                        turn_keys(us[i])
                    projections(l, beside[l, i])
                pe.wait_ge(ro_out, l + 1)
                pe.wait_ge(job_act, jobs_of[l][-1].after[0])
                n = 0
                for b in range(2):
                    for lo, hi in ((0, NLT), (NLT, tiles(l))):
                        if hi > lo:
                            for t in range(lo, hi):
                                mm = pe.transpose(bank(n)[:, (t - lo) * P:(t - lo + 1) * P],
                                                  cz[0][:, b, t * P:(t + 1) * P], ident)
                            mm.then_inc(ro_tp, 1)
                            n += 1

            def attention(l):
                au = atts_of[l]
                pe.wait_ge(ro_in, ro_parts(l + 1))
                pe.wait_ge(s_new, unit_end(l)[2])
                pe.wait_ge(o_out, unit_end(l)[1])

                def scores(a):
                    n = a.g
                    sbk = PS[n % 2]
                    if n - atts_of[l][0].g >= 2:
                        pe.wait_ge(ex, n - 1)
                    if a.grp == "D":
                        q, kk = qT["D"][:, a.h // 2, :], kT["D"][:, a.h, :]
                    else:
                        q, kk = qT[a.grp][:, a.h % 2, :], kT[a.grp][:, a.h // 2, :]
                    q = q[:, a.t * P:(a.t + 1) * P]
                    if a.hi > a.lo:
                        pe.matmul(sbk[:, 0:(a.hi - a.lo) * P], q, kk[:, a.lo * P:a.hi * P], start=True, stop=True)
                    pe.matmul(sbk[:, 512:512 + CTX], q, kk[:, SEQ:TOK], start=True, stop=True).then_inc(sc_sum, 1)

                def turn(o):
                    if o.prev:
                        wait_all(pe, (pt_act, o.prev[0]), (pt_dve, o.prev[1]))
                    tb = bank(4 + o.n % 2)
                    if o.kind == "p":
                        pe.wait_ge(ex, o.a.g + 1)
                        for i in range(o.lo, o.hi):
                            mm = pe.transpose(tb[:, (i - o.lo) * P:(i - o.lo + 1) * P],
                                              PB[o.a.g % 3][:, i * P:(i + 1) * P], ident)
                    else:
                        pe.wait_ge(o_norm, o.a.quad + 1)
                        for i in range(2):
                            mm = pe.transpose(tb[:, i * P:(i + 1) * P], OB[o.a.quad % 2][:, i * P:(i + 1) * P], ident)
                    mm.then_inc(p_tp, 1)

                def values(a):
                    if a.h == 0 and a.quad - atts_of[l][0].quad >= 2:
                        pe.wait_ge(o_norm, a.quad - 1)
                    last = a.p_items[-1]
                    wait_all(pe, (pt_act, last.done[0]), (pt_dve, last.done[1]))
                    ob = bank(6 + a.quad % 2)[:, a.h * 64:(a.h + 1) * 64]
                    vc = slice(a.h * 64, a.h * 64 + 64) if a.grp == "D" else slice((a.h // 2) * 64, (a.h // 2) * 64 + 64)
                    for i, kt in enumerate(a.keys):
                        mm = pe.matmul(ob, PT[a.g % 2][:, i * P:(i + 1) * P], vv[a.grp][:, kt, vc],
                                       start=(i == 0), stop=(i == len(a.keys) - 1))
                    mm.then_inc(o_pv, 1)

                for i in range(len(au) + LAG + 3):
                    if i < len(au):
                        scores(au[i])
                    for o in items_at[l, i]:
                        if o.kind == "p":
                            turn(o)
                    if LAG + 1 <= i < len(au) + LAG + 1:
                        values(au[i - LAG - 1])
                    for o in items_at[l, i]:
                        if o.kind == "o":
                            turn(o)

            def spread_gates(m):
                l, i = res[m]
                if i == 0:
                    wait_all(pe, (pt_act, flat_end(l)[0]), (pt_dve, flat_end(l)[1]), (o_norm, att_end(l) // HEADS))
                    pe.wait_ge(mod_done, mods_done(l))
                else:
                    wait_all(pe, (conv_done, ups_of[l][-1].done[0]), (mod_done, ups_of[l][-1].done[1]))
                    pe.wait_ge(hid_ready, FT * (l + 1))
                for v in range(2 if has_ctx(l) else 1):
                    for hf in range(2):
                        for k in range(4):
                            col = mod3[:, l, (16 if i == 0 else 40) + hf * 4 + k, v:v + 1]
                            mm = pe.matmul(bank(2 * v + hf)[:, k * P:(k + 1) * P], col.broadcast_to([P, P]), ident,
                                           start=True, stop=True)
                        mm.then_inc(ga_sum, 1)

            def residual_products(m):
                l, i = res[m]
                src, groups, total = (x3, KT // KDN, KT) if i == 0 else (g3, DN_GROUPS, FT)
                base = 2 * tiles_before[m]
                def product(job, t, wk, k):
                    return pe.matmul(bank((job + 4) % 8), src[:, k, t * P:(t + 1) * P], wk[:, k % KDN, :],
                                     start=(k == 0), stop=(k == total - 1))

                def first_use(job):
                    if 4 <= job < 8:
                        pe.wait_ge(ga_in, ga_before(m + 1))
                    if job >= 8:
                        pe.wait_ge(acc_read, base + job - 8 + 1)

                def weights_of(n, g):
                    return slot(("out" if i == 0 else "down", l, n, g)).rearrange("p (k c) -> p k c", k=KDN)

                for n in range(2):
                    together = 1 if n == 0 else 2
                    for g in range(groups - together):
                        wk = weights_of(n, g)
                        for t in range(tiles(l)):
                            job = n * tiles(l) + t
                            if g == 0:
                                first_use(job)
                            for k in range(g * KDN, g * KDN + KDN):
                                mm = product(job, t, wk, k)
                        mm.then_inc(slot_read, 1)
                    last = [(g, weights_of(n, g)) for g in range(groups - together, groups)]
                    for t in range(tiles(l)):
                        job = n * tiles(l) + t
                        if groups == together:
                            first_use(job)
                        for g, wk in last:
                            for k in range(g * KDN, min(g * KDN + KDN, total)):
                                mm = product(job, t, wk, k)
                        mm.then_inc(acc_sum, 1)

            def ffn_up(l):
                us = ups_of[l]
                for u in us:
                    if u.kind == "up" and u.half == 0:
                        ws = slot(u.key)
                    if u.freed:
                        wait_all(pe, (conv_done, u.freed[0]), (mod_done, u.freed[1]))
                    if u.kind == "mod":
                        mod_sums(u.mac, PS[u.pos])
                        continue
                    wk = ws.rearrange("p (k h c) -> p k h c", k=KT, h=2)
                    for lo, hi in ((0, SEQ), (SEQ, TOK)) if has_ctx(l) else ((0, SEQ),):
                        for k in range(KT):
                            mm = pe.matmul(PS[u.pos][:, lo:hi], wk[:, k, u.half, :], x3[:, k, lo:hi],
                                           start=(k == 0), stop=(k == KT - 1))
                    mm.then_inc(up_sum, 1)

            for l in range(DEPTH):
                transposes(2 * l)
                projections(l, own_of[l])
                hgrn(l)
                attention(l)
                spread_gates(2 * l)
                residual_products(2 * l)
                pe.wait_ge(acc_read, 2 * tiles_before[2 * l + 1])
                transposes(2 * l + 1)
                ffn_up(l)
                spread_gates(2 * l + 1)
                residual_products(2 * l + 1)
                pe.wait_ge(acc_read, 2 * tiles_before[2 * l + 2])

        @block.scalar
        def _(act):
            steps = [0]

            def step(ins):
                steps[0] += 1
                ins.then_inc(act_step, 1)
                act.wait_ge(act_step, steps[0])

            act.wait_ge(consts_in, 48)
            act.activation(SC[:, 0:16], cvec, ACT.Silu).then_inc(sc_ready, 1)
            act.wait_ge(dve_step, 2)
            act.activation(cexp[:, 8:16], cexp[:, 0:8], ACT.Exp).then_inc(e_lb, 1)

            def modulate_latent(m):
                l, j0, _ = stages[m]
                act.wait_ge(mod_done, MOD_FIRST if m == 0 else mods_done(l))
                for k in range(KT):
                    act.wait_ge(tp_lat, KT * m + k + 1)
                    act.activation(x3[:, k, 0:SEQ], bank(k % 2), ACT.Identity, bias=mod3[:, l, j0 + k, 0:1],
                                   scale=mod3[:, l, j0 + 8 + k, 0:1]).then_inc(x_lat, 1)

            def take_projections(l, js):
                dest = {QC: lambda a: cq[:, a, :], FCF: lambda a: cz[0][:, a, :], FCB: lambda a: cz[1][:, a, :],
                        QD: lambda a: qT["D"][:, a, :]}
                tok_dest = {IC: ci, GC: cg, VD: vv["D"]}
                for j in js:
                    if j.kind != "mod":
                        act.wait_ge(job_sum, j.sum)
                        ps3 = bank(j.bank).rearrange("p (i c) -> p i c", i=2)
                        if j.slot == KD:
                            lo, hi = (0, SEQ) if j.b == 0 else (SEQ, TOK)
                            act.wait_ge(padded, l + 1)
                            for hh in range(2):
                                rows = slice(64 * hh, 64 * hh + 64)
                                ins = act.activation(kT["D"][rows, 2 * j.a + hh, lo:hi], bank(j.bank)[rows, 0:hi - lo], ACT.Copy)
                        elif j.kind == "feat":
                            lo, hi = (0, SEQ) if j.b == 0 else (SEQ, TOK)
                            func, sc = {QC: (ACT.Silu, 1.0), FCF: (ACT.Exp, -1.0), FCB: (ACT.Exp, -1.0)}.get(
                                j.slot, (ACT.Copy, 1.0))
                            ins = act.activation(dest[j.slot](j.a)[:, lo:hi], bank(j.bank)[:, 0:hi - lo], func, scale=sc)
                        elif j.rope:
                            if j.slot in (KVA, KVB):
                                v = vv["A" if j.slot == KVA else "B"]
                                act.activation(v[:, 2 * j.a:2 * j.a + 2, :], ps3[:, :, P:], ACT.Copy)
                            if j.r >= 3:
                                act.wait_ge(roped, j.r - 2)
                            ins = act.activation(raw[:, j.r % 3, :], bank(j.bank), ACT.Copy)
                        else:
                            ins = act.activation(tok_dest[j.slot][:, 2 * j.a:2 * j.a + 2, :], ps3,
                                                 ACT.Silu if j.slot == GC else ACT.Copy)
                        ins.then_inc(job_act, 1)
                    for q in j.turns:
                        act.wait_ge(rot_tp, q.r + 1)
                        grp = "A" if q.slot in (QA, KVA) else "B"
                        tb = bank(6 + q.r % 2)
                        cols = slice(q.a * 256, q.a * 256 + 256)
                        if q.slot in (QA, QB):
                            ins = act.activation(qT[grp][:, :, cols], tb.rearrange("p (g t) -> p g t", g=2), ACT.Copy)
                        else:
                            act.wait_ge(padded, l + 1)
                            for hh in range(2):
                                rows = slice(64 * hh, 64 * hh + 64)
                                ins = act.activation(kT[grp][rows, hh, cols], tb[rows, 0:256], ACT.Copy)
                        ins.then_inc(qk_in, 1)

            def hgrn(l):
                us = units_of[l]
                for i in range(-3, len(us)):
                    if 0 <= i + 3 < len(us):
                        u = us[i + 3]
                        act.wait_ge(yk, u.g + 1)
                        act.activation(YB[u.g % 2], YB[u.g % 2], ACT.Ln).then_inc(lnr, 1)
                    if 0 <= i + 2 < len(us):
                        u = us[i + 2]
                        last = (P - 1, 0)[u.d]
                        act.wait_ge(subs, u.g + 1)
                        if u.g >= 2:
                            act.wait_ge(ke, u.g - 1)
                        if u.g >= 2 and units[u.g - 2].out:
                            act.wait_ge(qe, units[u.g - 2].no + 1)
                        if u.ns >= 4:
                            act.wait_ge(s_new, u.ns - 3)
                        E = EX[u.g % 2]
                        if u.out:
                            step(act.activation(E[:, 1:8, :], E[:, 1:8, :], ACT.Abs))
                        act.activation(E[:, 0, :], CB[u.g % 2], ACT.Exp)
                        act.activation(DEC[:, u.g % 4:u.g % 4 + 1], CB[u.g % 2][:, last:last + 1], ACT.Exp)
                        lo = 1 if u.out else 8
                        act.activation(E[:, lo:9, :], E[:, lo:9, :], ACT.Exp, scale=-1.0).then_inc(expd, 1)
                    if i >= 0 and us[i].state:
                        u = us[i]
                        act.wait_ge(kdt, u.ns + 1)
                        if u.ns >= 2:
                            act.wait_ge(kv_sum, u.ns - 1)
                        act.activation(KDT[u.ns % 2], bank(6)[:, 0:P], ACT.Copy).then_inc(kd_in, 1)
                    take_projections(l, beside.get((l, i), []))
                take_projections(l, beside[l, len(us)])
                n = 0
                for b in range(2):
                    for lo, hi in ((0, NLT), (NLT, tiles(l))):
                        if hi > lo:
                            act.wait_ge(ro_tp, ro_parts(l) + n + 1)
                            act.activation(x3[:, 4 + b, lo * P:hi * P], bank(n)[:, 0:(hi - lo) * P],
                                           ACT.Copy).then_inc(ro_in, 1)
                            n += 1
                act.dma_start(biasv, bias_d[l]).then_inc(bias_in, 16)

            def attention(l):
                au = atts_of[l]
                for i in range(len(au) + LAG + 3):
                    if i < len(au):
                        a = au[i]
                        sbk, pb = PS[a.g % 2], PB[a.g % 3]
                        nl = (a.hi - a.lo) * P
                        s4 = stat[:, a.quad % 4]
                        act.wait_ge(mx, a.g + 1)
                        if i >= 3:
                            act.wait_ge(p_tp, au[i - 3].p_items[-1].index + 1)
                        negm = s4[:, 3, a.h:a.h + 1]
                        if a.grp == "A":
                            act.activation(s4[:, 6, a.h:a.h + 1], sinkv[:, l, a.h:a.h + 1], ACT.Exp, bias=negm)
                        if nl and a.grp != "B":
                            act.activation(pb[:, 0:nl], pb[:, 0:nl], ACT.Exp, bias=negm,
                                           accum_out=s4[:, 4, a.h:a.h + 1])
                            act.activation(pb[:, nl:nl + CTX], sbk[:, 512:768], ACT.Exp, bias=negm, scale=SCALE,
                                           accum_out=s4[:, 5, a.h:a.h + 1]).then_inc(ex, 1)
                        else:
                            act.activation(pb[:, 0:nl + CTX], sbk[:, 512 - nl:768], ACT.Exp, bias=negm, scale=SCALE,
                                           accum_out=s4[:, 4, a.h:a.h + 1]).then_inc(ex, 1)
                    for o in items_at[l, i]:
                        if o.eng != "act":
                            continue
                        act.wait_ge(p_tp, o.index + 1)
                        tb = bank(4 + o.n % 2)
                        if o.kind == "p":
                            if o.a.g - au[0].g >= 2:
                                act.wait_ge(o_pv, o.a.g - 1)
                            act.activation(PT[o.a.g % 2][:, o.lo * P:o.hi * P], tb[:, 0:(o.hi - o.lo) * P],
                                           ACT.Copy).then_inc(pt_act, 1)
                        else:
                            k0 = {"A": 0, "B": 2, "D": 6}[o.a.grp]
                            act.activation(x3[:, k0:k0 + 2, o.a.t * P:(o.a.t + 1) * P],
                                           tb[:, 0:256].rearrange("p (k t) -> p k t", k=2),
                                           ACT.Copy).then_inc(pt_act, 1)

            def gates(m):
                l, i = res[m]
                base = ga_before(m)
                n = 0
                for v in range(2 if has_ctx(l) else 1):
                    for hf in range(2):
                        act.wait_ge(ga_sum, base + n + 1)
                        if n == 0:
                            act.dma_start(lnp, ln_rows[2 * l + i].partition_broadcast(P)).then_inc(ln_in, 16)
                        act.activation(gav[:, v, hf * 512:(hf + 1) * 512], bank(2 * v + hf), ACT.Copy).then_inc(ga_in, 1)
                        n += 1

            def ffn(l):
                n = TOK if has_ctx(l) else SEQ

                def gate(j):
                    jg = FT * l + j
                    act.wait_ge(conv_done, 2 * jg + 1)
                    if jg >= 2:
                        act.wait_ge(hid_ready, jg - 1)
                    act.activation(sl[jg % 2][:, 0:n], at[jg % 2][:, 0:n], ACT.Silu).then_inc(gate_ready, 1)

                for u in ups_of[l]:
                    if u.kind == "mod":
                        continue
                    jg = FT * l + u.j
                    dst = (at, vt)[u.half][jg % 2]
                    act.wait_ge(up_sum, u.c + 1)
                    if jg >= 2:
                        act.wait_ge(hid_ready, jg - 1)
                    jj = u.half * FT + u.j
                    act.activation(dst[:, 0:n], PS[u.pos][:, 0:n], ACT.Identity, bias=convp[:, l, 3, jj:jj + 1],
                                   scale=convp[:, l, 1, jj:jj + 1]).then_inc(base_ready, 1)
                    if u.half == 1 and u.j >= 1:
                        gate(u.j - 1)
                gate(FT - 1)

            for l in range(DEPTH):
                modulate_latent(2 * l)
                take_projections(l, own_of[l])
                hgrn(l)
                attention(l)
                gates(2 * l)
                modulate_latent(2 * l + 1)
                ffn(l)
                gates(2 * l + 1)
            for t in range(NLT):
                act.wait_ge(ln_done, tiles_before[3] + t + 1)
                act.dma_start(out[t * P:(t + 1) * P, :], h3[:, t, :]).then_inc(out_stored, 16)
            act.wait_ge(out_stored, 16 * NLT)

        @block.vector
        def _(dve):
            steps = [0]

            def mark(ins):
                steps[0] += 1
                ins.then_inc(dve_step, 1)

            def step(ins):
                mark(ins)
                dve.wait_ge(dve_step, steps[0])

            dve.wait_ge(consts_in, 48)
            step(dve.tensor_tensor(lbt[:, 0, :], lbl[:, 0, :], lbl[:, 1, :], ALU.max))
            step(dve.tensor_tensor(cexp[:, 0:8].rearrange("p (l e) -> p l e", l=2), lbl,
                                   lbt[:, 0:1, :].broadcast_to([P, 2, 4]), ALU.subtract))
            dve.wait_ge(e_lb, 1)
            e2 = cexp[:, 8:16].rearrange("p (l e) -> p l e", l=2)
            step(dve.tensor_tensor(lbt[:, 1, :], e2[:, 0, :], e2[:, 1, :], ALU.add))
            step(dve.reciprocal(lbt[:, 1, :], lbt[:, 1, :]))
            step(dve.tensor_tensor(e2, e2, lbt[:, 1:2, :].broadcast_to([P, 2, 4]), ALU.mult))
            step(dve.tensor_tensor(lb4[:, 0, :], e2[:, 0, :], e2[:, 0, :], ALU.subtract))
            step(dve.tensor_tensor(lbt[:, 2, :], e2[:, 0, :], e2[:, 1, :], ALU.add))
            step(dve.tensor_tensor(lb4[:, 1, :], lbt[:, 2, :], e2[:, 0, :], ALU.subtract))
            step(dve.tensor_scalar(oml4, lb4, -1.0, 1.0, ALU.mult, ALU.add))
            dve.memset(ones, 1.0)
            step(dve.memset(sel, 0.0))
            dve.memset(sel[0:64, 0:1], 1.0)
            step(dve.memset(sel[64:P, 1:2], 1.0))
            dve.memset(mhalf, -0.5).then_inc(halves, 1)

            def mod_macs(key, mac):
                n = SLOT_AT[key]
                wk = ring[:, n % RING, :].rearrange("p (k c) -> p k c", k=KT)
                if mac >= 3:
                    dve.wait_ge(mod_sum, MOD_FIRST + mac - 2)
                dve.wait_ge(w_arrived[n % RING], 16 * (n // RING + 1))
                if mac == 1:
                    dve.wait_ge(sc_ready, 1)
                for k in range(KT):
                    for v in range(2):
                        acc = macc[:, mac % 2, v, :]
                        if k == 0:
                            ins = dve.tensor_scalar(acc, wk[:, k, :], scv[:, k, v:v + 1], None, ALU.mult)
                        else:
                            ins = dve.scalar_tensor_tensor(acc, wk[:, k, :], scv[:, k, v:v + 1], acc, ALU.mult, ALU.add)
                        if k < KT - 1:
                            mark(ins)
                    if k < KT - 1:
                        dve.wait_ge(dve_step, steps[0])
                ins.then_inc(mac_done, 1)
            step(dve.tensor_copy(MK[:, :], W[:, 0:2 * LEVELS * 64]))

            def mod_out(l, i, src):
                b = bmod[:, l, 2 * i:2 * i + 2].unsqueeze(2).broadcast_to([P, 2, 2])
                o = mod3[:, l, 2 * i:2 * i + 2, :]
                s3 = src[:, 0:4].rearrange("p (j v) -> p j v", j=2)
                if 4 <= i < 8 or 16 <= i < 20:
                    step(dve.tensor_tensor(o, s3, b, ALU.add))
                    dve.tensor_scalar(o, o, 1.0, None, ALU.add).then_inc(mod_done, 1)
                else:
                    dve.tensor_tensor(o, s3, b, ALU.add).then_inc(mod_done, 1)

            for i in range(MOD_FIRST):
                dve.wait_ge(mod_sum, i + 1)
                mod_out(0, i, bank(i))

            def modulate_context(m):
                l, j0, with_ctx = stages[m]
                if with_ctx:
                    for k in range(KT):
                        if k == 0:
                            dve.wait_ge(mod_done, MOD_FIRST if m == 0 else mods_done(l))
                        dve.wait_ge(tp_ctx, ctx_before[m] + k + 1)
                        dve.tensor_scalar(x3[:, k, SEQ:TOK], bank(2 + k % 2, 256), mod3[:, l, j0 + 8 + k, 1:2],
                                          mod3[:, l, j0 + k, 1:2], ALU.mult, ALU.add).then_inc(x_ctx, 1)

            def rotate(j):
                l, heads = j.l, 4 if j.slot in (QA, QB) else 2
                rw = raw[:, j.r % 3, :]
                ro = rot[:, j.r % 3, :]
                dve.wait_ge(job_act, j.after[0])
                if j.r >= 1:
                    dve.wait_ge(roped, j.r)
                if j.r >= 3:
                    dve.wait_ge(rot_tp, j.r - 2)
                src4 = rw.rearrange("p (i h d) -> p i h d", i=2, d=HD)[:, :, 0:heads, :]
                if j.slot in (QB, KVB):
                    nh = 2 * heads
                    ra4 = ra.rearrange("p (i h d) -> p i h d", i=2, d=HD)[:, :, 0:heads, :]
                    step(dve.tensor_tensor(ra4, src4, src4, ALU.mult))
                    for i in range(2):
                        ins = dve.tensor_reduce(rss[:, 4 * i:4 * i + heads], ra4[:, i], AX, ALU.add)
                        mark(ins) if i == 0 else step(ins)
                    r8 = rss[:, 0:8]
                    if heads == 2:
                        for i in range(2):
                            ins = dve.tensor_scalar(rss[:, 4 * i:4 * i + 2], rss[:, 4 * i:4 * i + 2], 1.0 / HD, EPS,
                                                    ALU.mult, ALU.add)
                    else:
                        ins = dve.tensor_scalar(r8, r8, 1.0 / HD, EPS, ALU.mult, ALU.add)
                    ins.then_inc(ss_ready, 1)
                    rs[0] += 1
                    dve.wait_ge(root_ready, rs[0])
                    for i in range(2):
                        ins = dve.tensor_tensor(ra4[:, i], src4[:, i],
                                                rss[:, 8 + 4 * i:8 + 4 * i + heads].unsqueeze(2).broadcast_to([P, heads, HD]),
                                                ALU.mult)
                        mark(ins) if i == 0 else step(ins)
                    gain = qkn[:, l, 0 if j.slot == QB else 1, :].unsqueeze(1).broadcast_to([P, heads, HD])
                    plain = j.a * 2 >= NLT
                    dst = ro.rearrange("p (i h d) -> p i h d", i=2, d=HD)[:, :, 0:heads, :] if plain else src4
                    for i in range(2):
                        ins = dve.tensor_tensor(dst[:, i], ra4[:, i], gain, ALU.mult)
                        if plain and i == 1:
                            ins.then_inc(roped, 1)
                        elif i == 0:
                            mark(ins)
                        else:
                            step(ins)
                    if plain:
                        return
                elif j.a * 2 >= NLT:
                    dve.tensor_copy(ro, rw).then_inc(roped, 1)
                    return
                for i in range(2):
                    t = 2 * j.a + i
                    s = rw[:, i * 256:i * 256 + heads * HD]
                    o = ro[:, i * 256:i * 256 + heads * HD]
                    a_ = ra[:, i * 256:i * 256 + heads * HD]
                    b_ = rb[:, i * 256:i * 256 + heads * HD]
                    mark(dve.tensor_tensor(a_.rearrange("p (h d) -> p h d", d=HD), s.rearrange("p (h d) -> p h d", d=HD),
                                           cosv[:, t, :].unsqueeze(1).broadcast_to([P, heads, HD]), ALU.mult))
                    s5 = s.rearrange("p (h a f d) -> p h a f d", a=2, f=2, d=HD // 4)
                    b5 = b_.rearrange("p (h a f d) -> p h a f d", a=2, f=2, d=HD // 4)
                    t5 = sinv[:, t, :].rearrange("p (a f d) -> p a f d", a=2, f=2)
                    for f in range(2):
                        ins = dve.tensor_tensor(b5[:, :, :, f, :], s5[:, :, :, 1 - f, :],
                                                t5[:, :, f, :].unsqueeze(1).broadcast_to([P, heads, 2, HD // 4]), ALU.mult)
                        mark(ins)
                dve.wait_ge(dve_step, steps[0])
                v4 = lambda w: w.rearrange("p (i c) -> p i c", i=2)[:, :, 0:heads * HD]
                dve.tensor_tensor(v4(ro), v4(ra), v4(rb), ALU.add).then_inc(roped, 1)

            def project(l):
                mods = [j for j in own_of[l] if j.kind == "mod"]
                for j in own_of[l]:
                    if j.kind != "mod" and j.first:
                        for q in mods[:2]:
                            mod_macs(q.key, q.mac)
                        mods = mods[2:]
                    if j.kind == "mod":
                        dve.wait_ge(mod_sum, MOD_FIRST + j.mac)
                        mod_out(0, j.slot, bank(5))
                    elif j.is_e:
                        lo, hi = (0, SEQ) if j.b == 0 else (SEQ, TOK)
                        d = 0 if j.slot == FCF else 1
                        z = cz[d][:, j.a, lo:hi]
                        e = 2 * d + j.a
                        dve.wait_ge(job_act, j.after[0])
                        step(dve.tensor_scalar(z, z, 1.0, None, ALU.add))
                        step(dve.reciprocal(z, z))
                        dve.tensor_scalar(z, z, oml4[:, l, e:e + 1], lb4[:, l, e:e + 1], ALU.mult,
                                          ALU.add).then_inc(e_in, 1)
                    elif j.rope:
                        rotate(j)

            def hgrn(l):
                us = units_of[l]
                dve.memset(W[:, 8192:9728], 0.0).then_inc(zeroed, 1)
                dve.wait_ge(zeroed, l + 1)
                for i in range(-2, len(us) + 1):
                    if 0 <= i + 2 < len(us):
                        u = us[i + 2]
                        E, cb, ln = EX[u.g % 2], CB[u.g % 2], YB[u.g % 2]
                        dve.wait_ge(lnr, u.g + 1)
                        if u.g >= 2:
                            dve.wait_ge(expd, u.g - 1)
                            dve.wait_ge(ke, u.g - 1)
                            dve.wait_ge(subs, u.g)
                            if units[u.g - 2].out:
                                dve.wait_ge(qe, units[u.g - 2].no + 1)
                        r = slice(None, None, 1 - 2 * u.d)
                        step(dve.tensor_tensor_scan(cb[:, r], ln[:, 0:P][:, r], ln[:, P:2 * P][:, r], 0.0, ALU.add, ALU.add))
                        if u.out:
                            for m in range(LEVELS):
                                half = P >> (m + 1)
                                ref = half - 1 + u.d
                                c3 = cb.rearrange("p (n w) -> p n w", w=2 * half)
                                dve.tensor_tensor(E[:, 1 + m, :].rearrange("p (n w) -> p n w", w=2 * half), c3,
                                                  c3[:, :, ref:ref + 1].broadcast_to([P, P // (2 * half), 2 * half]),
                                                  ALU.subtract)
                        last = (P - 1, 0)[u.d]
                        dve.tensor_tensor(E[:, 8, :], cb, cb[:, last:last + 1].broadcast_to([P, P]),
                                          ALU.subtract).then_inc(subs, 1)
                    if 0 <= i + 1 < len(us) and us[i + 1].out:
                        u = us[i + 1]
                        dve.wait_ge(expd, u.g + 1)
                        if u.no >= 2:
                            dve.wait_ge(o_sum, u.no - 1)
                        q = cq[:, u.b, u.t * P:(u.t + 1) * P].unsqueeze(1).broadcast_to([P, 8, P])
                        dve.tensor_tensor(QE[u.g % 2], EX[u.g % 2][:, 0:8, :], q, ALU.mult).then_inc(qe, 1)
                    if 0 <= i < len(us) and us[i].out:
                        u = us[i]
                        if u.no >= 2:
                            dve.wait_ge(o_sum, u.no - 1)
                        dve.wait_ge(maps, u.no + 1)
                        pair = PS[1 + u.no % 2][:, :].rearrange("p (h c) -> p h c", h=2)
                        for m in range(LEVELS):
                            w = P >> (m + 1)
                            dst = AT[u.d][u.no % 2].rearrange("p h (n f t) -> p h n f t", f=2, t=w)[:, :, :, 1 - u.d, :]
                            src = pair[:, :, m * 64:(m + 1) * 64].rearrange("p h (n t) -> p h n t", t=w)
                            msk = mk4[:, u.d, m, :].rearrange("p (n t) -> p n t", t=w).unsqueeze(1)
                            ins = dve.copy_predicated(dst, msk.broadcast_to([P, 2, 64 // w, w]), src)
                            if m < LEVELS - 1:
                                step(ins)
                        ins.then_inc(atd, 1)
                        dve.wait_ge(atd, u.no + 1)
                    if i >= 1:
                        u = us[i - 1]
                        if u.out:
                            dve.wait_ge(o_sum, u.no + 1)
                            o = cz[0][:, u.b, u.t * P:(u.t + 1) * P]
                            ob = bank(7)
                            if u.no:
                                dve.wait_ge(o_out, u.no)
                            base = ob[:, 0:P]
                            if u.d == 1:
                                step(dve.tensor_tensor(o, base, o, ALU.add))
                                base = o
                            for hh in range(2):
                                c = slice(64 * hh, 64 * hh + 64)
                                ins = dve.scalar_tensor_tensor(o[:, c], ci[:, u.t, u.b * P + 64 * hh:u.b * P + 64 * hh + 64],
                                                               ob[:, P + hh:P + hh + 1], base[:, c], ALU.mult, ALU.add)
                            ins.then_inc(o_out, 1)
                        if u.state:
                            dve.wait_ge(kv_sum, u.ns + 1)
                            if u.ns >= 1:
                                dve.wait_ge(s_new, u.ns)
                            for hh in range(2):
                                rows, cols = slice(64 * hh, 64 * hh + 64), slice(64 * hh, 64 * hh + 64)
                                s = SS[rows, u.d, u.b, cols]
                                ins = dve.scalar_tensor_tensor(s, s, DEC[rows, u.g % 4:u.g % 4 + 1], bank(6)[rows, cols],
                                                               ALU.mult, ALU.add)
                            ins.then_inc(s_new, 1)
                nt = tiles(l)
                dve.wait_ge(o_out, unit_end(l)[1])
                o3 = cz[0][:, :, 0:nt * P]
                n = 2 * nt * 2
                step(dve.tensor_tensor(osq[:, 0:n * HD].rearrange("p (b c) -> p b c", b=2), o3, o3, ALU.mult))
                dve.tensor_reduce(ross[:, 0:n], osq[:, 0:n * HD].rearrange("p (n d) -> p n d", d=HD), AX,
                                  ALU.add).then_inc(ro_sq, 1)
                dve.wait_ge(ro_rstd, l + 1)
                for b in range(2):
                    ob3 = cz[0][:, b, 0:nt * P].rearrange("p (n d) -> p n d", d=HD)
                    rr = ross[:, b * 2 * nt:(b + 1) * 2 * nt].unsqueeze(2).broadcast_to([P, 2 * nt, HD])
                    ins = dve.tensor_tensor(ob3, ob3, rr, ALU.mult)
                    mark(ins) if b == 0 else step(ins)
                for b in range(2):
                    obt = cz[0][:, b, 0:nt * P].rearrange("p (t c) -> p t c", c=P)
                    on = onorm[:, l, b * P:(b + 1) * P].unsqueeze(1).broadcast_to([P, nt, P])
                    ins = dve.tensor_tensor(obt, obt, on, ALU.mult)
                    mark(ins) if b == 0 else step(ins)
                for b in range(2):
                    obt = cz[0][:, b, 0:nt * P].rearrange("p (t c) -> p t c", c=P)
                    ins = dve.tensor_tensor(obt, obt, cg[:, 0:nt, b * P:(b + 1) * P], ALU.mult)
                ins.then_inc(ro_out, 1)

            def attention(l):
                au = atts_of[l]
                for i in range(len(au) + LAG + 3):
                    if i < len(au):
                        a = au[i]
                        sbk, pb = PS[a.g % 2], PB[a.g % 3]
                        nl = (a.hi - a.lo) * P
                        s4 = stat[:, a.quad % 4]
                        m1, m2, m3, negm = [s4[:, w, a.h:a.h + 1] for w in range(4)]
                        sink = sinkv[:, l, a.h:a.h + 1]
                        if a.grp == "D" and a.t == 0 and a.h == 0:
                            dve.wait_ge(bias_in, 16 * (l + 1))
                            step(dve.tensor_scalar(U[:, 0:HEADS * BIAS_ROWS * 64], U[:, 0:HEADS * BIAS_ROWS * 64],
                                                   1.0 / SCALE, None, ALU.mult))
                        dve.wait_ge(sc_sum, a.g + 1)
                        if i == 0:
                            dve.wait_ge(ro_in, ro_parts(l + 1))
                        if nl and a.grp != "B":
                            if i >= 3:
                                dve.wait_ge(p_tp, au[i - 3].p_items[-1].index + 1)
                            mark(dve.tensor_reduce(m1, sbk[:, 512:768], AX, ALU.max))
                            if a.grp == "A":
                                at0 = P * (1 - (a.t - a.lo))
                                add = amask[:, at0:at0 + nl]
                            else:
                                e0 = 64 * (6 - 2 * a.t)
                                add = biasv[:, a.h, e0:e0 + nl]
                            step(dve.tensor_tensor_reduce(pb[:, 0:nl], sbk[:, 0:nl], add, SCALE, NEG * 8, ALU.add, ALU.max, m2))
                            step(dve.scalar_tensor_tensor(m3, m1, SCALE, m2, ALU.mult, ALU.max))
                            if a.grp == "A":
                                ins = dve.tensor_scalar(negm, m3, sink, -1.0, ALU.max, ALU.mult)
                            else:
                                ins = dve.tensor_scalar(negm, m3, -1.0, None, ALU.mult)
                            ins.then_inc(mx, 1)
                        else:
                            step(dve.tensor_reduce(m1, sbk[:, 512 - nl:768], AX, ALU.max))
                            if a.grp == "A":
                                step(dve.tensor_scalar(m3, m1, SCALE, sink, ALU.mult, ALU.max))
                                dve.tensor_scalar(negm, m3, -1.0, None, ALU.mult).then_inc(mx, 1)
                            else:
                                dve.tensor_scalar(negm, m1, -SCALE, None, ALU.mult).then_inc(mx, 1)
                    for o in items_at[l, i]:
                        if o.eng == "dve":
                            dve.wait_ge(p_tp, o.index + 1)
                            if o.a.g - au[0].g >= 2:
                                dve.wait_ge(o_pv, o.a.g - 1)
                            dve.tensor_copy(PT[o.a.g % 2][:, o.lo * P:o.hi * P],
                                            bank(4 + o.n % 2)[:, 0:(o.hi - o.lo) * P]).then_inc(pt_dve, 1)
                    if LAG + 1 <= i < len(au) + LAG + 1 and au[i - LAG - 1].h == HEADS - 1:
                        a = au[i - LAG - 1]
                        s4 = stat[:, a.quad % 4]
                        den = s4[:, 4, :]
                        dve.wait_ge(o_pv, a.g + 1)
                        dve.wait_ge(ex, a.g + 1)
                        if a.hi > a.lo and a.grp != "B":
                            step(dve.tensor_tensor(den, den, s4[:, 5, :], ALU.add))
                        if a.grp == "A":
                            step(dve.tensor_tensor(den, den, s4[:, 6, :], ALU.add))
                        step(dve.reciprocal(s4[:, 7, :], den))
                        if a.quad - au[0].quad >= 2:
                            dve.wait_ge(p_tp, quads[a.quad - 2].index + 1)
                        dve.tensor_tensor(OB[a.quad % 2].rearrange("p (h d) -> p h d", d=HD),
                                          bank(6 + a.quad % 2)[:, 0:256].rearrange("p (h d) -> p h d", d=HD),
                                          s4[:, 7, :].unsqueeze(2).broadcast_to([P, HEADS, HD]),
                                          ALU.mult).then_inc(o_norm, 1)

            def residual(m):
                l, i = res[m]
                nt, tb = tiles(l), tiles_before[m]

                def normalise(t):
                    b = bnb[:, (tb + t) % 3, :]
                    dve.wait_ge(rstd_ready, tb + t + 1)
                    step(dve.scalar_tensor_tensor(h3[:, t, :], h3[:, t, :], b[:, 12:13], lnp[:, 0:1024], ALU.subtract,
                                                  ALU.mult))
                    dve.scalar_tensor_tensor(h3[:, t, :], h3[:, t, :], b[:, 14:15], lnp[:, 1024:2048], ALU.mult,
                                             ALU.add).then_inc(ln_done, 1)

                for n in range(2):
                    for t in range(nt):
                        job = n * nt + t
                        if job == 0:
                            dve.wait_ge(ga_in, ga_before(m + 1))
                            dve.wait_ge(ln_in, 16 * (m + 1))
                        dve.wait_ge(acc_sum, 2 * tb + job + 1)
                        tmp = gtmp[:, job % 2, :]
                        hs = h3[:, t, n * 512:(n + 1) * 512]
                        dve.tensor_tensor(tmp, bank((job + 4) % 8), gav[:, int(t >= NLT), n * 512:(n + 1) * 512],
                                          ALU.mult).then_inc(acc_read, 1)
                        dve.wait_ge(acc_read, 2 * tb + job + 1)
                        step(dve.scalar_tensor_tensor(hs, hs, ALPHA, tmp, ALU.mult, ALU.add))
                        if n == 1:
                            b = bnb[:, (tb + t) % 3, :]
                            if tb + t >= 3:
                                dve.wait_ge(ln_done, tb + t - 2)
                            mark(dve.bn_stats(b[:, 0:6], h3[:, t, 0:512]))
                            step(dve.bn_stats(b[:, 6:12], h3[:, t, 512:1024]))
                            dve.bn_aggr(b[:, 12:14], b[:, 0:12]).then_inc(bn_ready, 1)
                            if t >= 1:
                                normalise(t - 1)
                normalise(nt - 1)

            def ffn(l):
                segs = ((0, SEQ), (SEQ, TOK)) if has_ctx(l) else ((0, SEQ),)
                mods = [u for u in ups_of[l] if u.kind == "mod"]
                for u in ups_of[l]:
                    if u.kind == "up" and u.half == 0:
                        for q in mods[:2 if u.j < 2 else 1]:
                            mod_macs(q.key, q.mac)
                        mods = mods[2 if u.j < 2 else 1:]
                    if u.kind == "mod":
                        dve.wait_ge(mod_sum, MOD_FIRST + u.mac)
                        mod_out(u.l + 1, u.j, PS[u.pos][:, 0:4])
                        continue
                    jg = FT * l + u.j
                    y = (at, vt)[u.half][jg % 2]
                    jj = u.half * FT + u.j
                    ps = PS[u.pos]
                    dve.wait_ge(base_ready, u.c + 1)
                    for lo, hi in segs:
                        ins = dve.scalar_tensor_tensor(y[:, lo + 1:hi], ps[:, lo:hi - 1], convp[:, l, 0, jj:jj + 1],
                                                       y[:, lo + 1:hi], ALU.mult, ALU.add)
                        mark(ins)
                    dve.wait_ge(dve_step, steps[0])
                    for lo, hi in segs:
                        ins = dve.scalar_tensor_tensor(y[:, lo:hi - 1], ps[:, lo + 1:hi], convp[:, l, 2, jj:jj + 1],
                                                       y[:, lo:hi - 1], ALU.mult, ALU.add)
                    ins.then_inc(conv_done, 1)

            rs = [0]
            for l in range(DEPTH):
                modulate_context(2 * l)
                project(l)
                hgrn(l)
                attention(l)
                residual(2 * l)
                modulate_context(2 * l + 1)
                ffn(l)
                residual(2 * l + 1)

        @block.gpsimd
        def _(pool):
            steps = [0]

            def step(ins):
                steps[0] += 1
                ins.then_inc(pool_step, 1)
                pool.wait_ge(pool_step, steps[0])

            roots = [0]
            pool.wait_ge(halves, 1)

            def head_roots(l):
                for j in jobs_of[l]:
                    if j.rope and j.slot in (QB, KVB):
                        heads = 4 if j.slot == QB else 2
                        pool.wait_ge(ss_ready, roots[0] + 1)
                        for i in range(2):
                            ins = pool.tensor_tensor(rss[:, 8 + 4 * i:8 + 4 * i + heads], rss[:, 4 * i:4 * i + heads],
                                                     mhalf[:, 0:heads], ALU.pow)
                        ins.then_inc(root_ready, 1)
                        roots[0] += 1

            def hgrn(l):
                us = units_of[l]
                pool.wait_ge(e_in, e_end[l])
                for i in range(-3, len(us)):
                    if 0 <= i + 3 < len(us):
                        u = us[i + 3]
                        f = cz[u.d][:, u.b, u.t * P:(u.t + 1) * P]
                        y = YB[u.g % 2]
                        if u.g >= 2:
                            pool.wait_ge(subs, u.g - 1)
                        if u.g >= 4:
                            pool.wait_ge(ke, u.g - 3)
                        pool.tensor_scalar(y[:, 0:P], f, 2.0 ** -60, None, ALU.max)
                        step(pool.tensor_scalar(y[:, P:2 * P], f, 2.0 ** -60, 2.0 ** 60, ALU.min, ALU.mult))
                        pool.tensor_scalar(y[:, P:2 * P], y[:, P:2 * P], 2.0 ** -63, None, ALU.max)
                        pool.tensor_scalar(KB[u.g % 4], f, -1.0, 1.0, ALU.mult, ALU.add).then_inc(yk, 1)
                    if 0 <= i + 1 < len(us):
                        u = us[i + 1]
                        pool.wait_ge(expd, u.g + 1)
                        pool.wait_ge(yk, u.g + 1)
                        if u.g >= 2:
                            w = units[u.g - 2]
                            if w.out:
                                pool.wait_ge(o_sum, w.no + 1)
                            if w.state:
                                pool.wait_ge(kdt, w.ns + 1)
                        lo = 0 if u.out else 7
                        if u.out:
                            pool.tensor_tensor(QK[u.g % 2], cq[:, u.b, u.t * P:(u.t + 1) * P], KB[u.g % 4], ALU.mult)
                        pool.tensor_tensor(KE[u.g % 2][:, lo:8, :], EX[u.g % 2][:, 1 + lo:9, :],
                                           KB[u.g % 4].unsqueeze(1).broadcast_to([P, 8 - lo, P]), ALU.mult).then_inc(ke, 1)
                n = 2 * tiles(l) * 2
                pool.wait_ge(ro_sq, l + 1)
                step(pool.tensor_scalar(ross[:, 0:n], ross[:, 0:n], 1.0 / HD, EPS, ALU.mult, ALU.add))
                pool.tensor_tensor(ross[:, 0:n], ross[:, 0:n], mhalf[:, 0:n], ALU.pow).then_inc(ro_rstd, 1)

            def layer_norm(m):
                l, i = res[m]
                nt, tb = tiles(l), tiles_before[m]

                for t in range(nt):
                    b = bnb[:, (tb + t) % 3, :]
                    pool.wait_ge(bn_ready, tb + t + 1)
                    step(pool.tensor_scalar(b[:, 14:15], b[:, 13:14], EPS, None, ALU.add))
                    pool.tensor_tensor(b[:, 14:15], b[:, 14:15], mhalf[:, 0:1], ALU.pow).then_inc(rstd_ready, 1)

            def gated(l):
                n = TOK if has_ctx(l) else SEQ
                for j in range(FT):
                    jg = FT * l + j
                    pool.wait_ge(gate_ready, jg + 1)
                    pool.wait_ge(conv_done, 2 * jg + 2)
                    pool.tensor_tensor(g3[:, j, 0:n], sl[jg % 2][:, 0:n], vt[jg % 2][:, 0:n], ALU.mult).then_inc(hid_ready, 1)

            def pad_keys(l):
                if l:
                    pool.wait_ge(acc_sum, 2 * tiles_before[2 * l])
                    pool.wait_ge(rstd_ready, tiles_before[2 * l])
                for g in "ABD":
                    for hh in range(2):
                        ins = pool.memset(kT[g][64 * (1 - hh):64 * (1 - hh) + 64, hh::2, :], 0.0)
                ins.then_inc(padded, 1)

            for l in range(DEPTH):
                pad_keys(l)
                head_roots(l)
                hgrn(l)
                layer_norm(2 * l)
                gated(l)
                layer_norm(2 * l + 1)


def constants():
    import numpy as np

    f = np.float32
    t = np.arange(SEQ)
    pos = np.stack([t // GRID_W, t % GRID_W], -1).astype(f)
    nf = HD // 4
    inv = (f(10000.0) ** (-np.arange(nf, dtype=f) / f(nf))).astype(f)
    ang = (pos[:, :, None] * inv).astype(f)
    cos, sin = np.cos(ang), np.sin(ang)
    c = np.stack([cos, cos], 2).reshape(SEQ, HD)
    s = np.stack([-sin, sin], 2).reshape(SEQ, HD)
    rows = lambda a: a.reshape(NLT, P, HD).transpose(1, 0, 2).reshape(P, -1)
    i, j = np.arange(P)[:, None], np.arange(P)[None, :]
    am = np.concatenate([np.where(j >= i, 0, NEG), np.zeros((P, P)), np.where(j <= i, 0, NEG)], 1)
    cn = np.concatenate([np.eye(P), rows(c), rows(s), am], 1).astype(f)
    mk = np.zeros((P, 2, LEVELS, 64), f)
    for m in range(LEVELS):
        h = P >> (m + 1)
        same = (i // (2 * h)) == (j // (2 * h))
        late = (np.arange(P) % (2 * h)) >= h
        mk[:, 0, m, :] = (same & (i % (2 * h) < h))[:, late]
        mk[:, 1, m, :] = (same & (i % (2 * h) >= h))[:, ~late]
    return cn, mk.reshape(P, -1)


def kernel(x, c, ctx, c_ctx, w_mod, b_mod, w_in, w_out, ln_g, ln_b, attn_sink, qk_norm, hgrn_lb_logits,
           hgrn_onorm, na_rpb, ffn_w_up, ffn_conv_w, ffn_conv_b, ffn_w_down):
    import numpy as np
    import concourse.bacc as bacc
    from concourse.bass_utils import run_bass_kernel_spmd

    A = np.asarray
    f = np.float32
    w_mod, w_in, w_out, w_up, w_down = A(w_mod), A(w_in), A(w_out), A(ffn_w_up), A(ffn_w_down)
    weights = np.zeros((len(STREAM), P, SLOT), f)
    for n, (kind, l, i, g) in enumerate(STREAM):
        if kind == "up":
            w = w_up[l].reshape(KT, P, 2, FT, P)[:, :, :, i, :].transpose(1, 0, 2, 3)
        elif kind in ("mod", "in"):
            w = (w_mod if kind == "mod" else w_in)[l][:, i * 256:(i + 1) * 256].reshape(KT, P, 256).transpose(1, 0, 2)
            if kind == "in" and i in (QA, QB):
                w = w.reshape(P, KT, 2, 2, HD).transpose(0, 1, 3, 2, 4)
        else:
            w = (w_out if kind == "out" else w_down)[l][g * KDN * P:(g + 1) * KDN * P, i * 512:(i + 1) * 512]
            w = w.reshape(-1, P, 512).transpose(1, 0, 2)
        w = w.reshape(P, -1)
        weights[n, :, :w.shape[1]] = w
    cn, mk = constants()
    per = lambda a: np.moveaxis(a.reshape(a.shape[:-1] + (-1, P)), -1, 0)
    every = lambda a: np.broadcast_to(a.reshape(1, -1), (P, a.size))
    cv = np.stack([per(A(c)[0]), per(A(c_ctx))], -1)
    conv = np.concatenate([A(ffn_conv_w), A(ffn_conv_b)[:, None, :]], 1)
    lbl = per(A(hgrn_lb_logits)).transpose(0, 2, 1, 3)
    params = np.concatenate([q.reshape(P, -1) for q in (
        cv, per(A(b_mod)), per(conv), lbl, every(A(qk_norm)), every(A(hgrn_onorm)), every(A(attn_sink)))], 1)
    rpb = A(na_rpb)
    bias = np.full((DEPTH, 2, GRID_W, HEADS, BIAS_ROWS, GRID_W), NEG, f)
    for col in range(GRID_W):
        c0 = min(max(col - NA_COLS // 2, 0), GRID_W - NA_COLS)
        o0 = c0 - col + NA_COLS - 1
        for a in range(2):
            bias[:, a, col, :, :, c0:c0 + NA_COLS] = rpb[:, :, 1 - a:1 - a + BIAS_ROWS, o0:o0 + NA_COLS]
    bias = bias.reshape(DEPTH, P, HEADS, BIAS_ROWS * GRID_W)
    ln_rows = np.concatenate([A(ln_g), A(ln_b)], -1).reshape(2 * DEPTH, 2 * D_MODEL)
    arrays = {"weights": weights, "x": A(x)[0], "ctx": A(ctx)[0], "consts": cn, "masks": mk,
              "params": params, "bias": bias, "ln_rows": ln_rows}
    arrays = {k: np.ascontiguousarray(v) for k, v in arrays.items()}
    nc = bacc.Bacc("TRN2", target_bir_lowering=False, num_devices=1)
    aps = [nc.dram_tensor(f"in_{k}", v.shape, mybir.dt.from_np(v.dtype), kind="ExternalInput").ap()
           for k, v in arrays.items()]
    out = nc.dram_tensor("out_h", (SEQ, D_MODEL), mybir.dt.float32, kind="ExternalOutput").ap()
    hybrid_backbone(nc, *aps, out)
    r = run_bass_kernel_spmd(nc, [{f"in_{k}": v for k, v in arrays.items()}], core_ids=[0])
    return r.results[0]["out_h"].reshape(1, SEQ, D_MODEL)
```

```python
import concourse.bass as bass
from concourse import mybir
from contextlib import ExitStack
import math

D_MODEL, SEQ, CTX, DEPTH = 1024, 512, 256, 2
P = 128
KT = D_MODEL // P
TOK = SEQ + CTX
NLT, NCT = SEQ // P, CTX // P
NT = NLT + NCT
HEADS, HD = 4, 64
D_FF = 256 * ((8 * D_MODEL // 3 + 255) // 256)
FT = D_FF // P
ALPHA = (2 * DEPTH) ** 0.25
EPS = 1e-6
SCALE = HD ** -0.5
NEG = -1e30
LEVELS = 7
GRID_W, NA_ROWS, NA_COLS = 64, 8, 16
BIAS_ROWS = 2 * NA_ROWS - 2

SLOT = 2048
RING = 3
ACT_LEVELS = 2
KDN = 4
DN_GROUPS = -(-FT // KDN)
QA, KVA, QB, KVB, QC, IC, FCF, FCB, GC, QD, KD, VD = range(12)
IN_ORDER = (QC, GC, IC, FCF, FCB, QA, KVA, QB, KVB, QD, KD, VD)
FEATURE = (QC, FCF, FCB, QD, KD)
LATENT_ONLY = (QA, QB, QC, GC, QD)
OWN_SLOTS = 9
MOD_FIRST = 8


def weight_stream():
    s = [("mod", 0, i, 0) for i in range(MOD_FIRST)]
    for l in range(DEPTH):
        extra = list(range(MOD_FIRST, 24)) if l == 0 else []
        for n, i in enumerate(IN_ORDER):
            s.append(("in", l, i, 0))
            for _ in range(2):
                if extra:
                    s.append(("mod", 0, extra.pop(0), 0))
        assert not extra
        s += [("out", l, n, g) for n in range(2) for g in range(KT // KDN)]
        nxt = list(range(24)) if l + 1 < DEPTH else []
        for j in range(FT):
            s.append(("up", l, j, 0))
            for _ in range(2 if j < 2 else 1):
                if nxt:
                    s.append(("mod", l + 1, nxt.pop(0), 0))
        assert not nxt
        s += [("down", l, n, g) for n in range(2) for g in range(DN_GROUPS)]
    return s


STREAM = weight_stream()
SLOT_AT = {key: n for n, key in enumerate(STREAM)}


def ring_plan():
    last, count, plan, place = {}, [0] * RING, [], 0
    for n, (kind, l, _, _) in enumerate(STREAM):
        place = (place + 1) % RING
        if place == 0 and (kind in ("up", "down") or (kind == "mod" and l > 0)):
            place = 1
        count[place] += 1
        plan.append((place, count[place], last.get(place)))
        last[place] = n
    return plan


PLAN = ring_plan()
ENTRY = 2 * TOK + 2 * 512


def hybrid_backbone(nc, weights, x, ctx_in, consts, masks, params, bias_d, ln_rows, out):
    f32, u8 = mybir.dt.float32, mybir.dt.uint8
    f32r = mybir.dt.float32r
    ALU, ACT, AX = mybir.AluOpType, mybir.ActivationFunctionType, mybir.AxisListType.X
    stack = ExitStack()

    starts = {}

    def sb(name, cols, dt=f32):
        starts[name] = nc.sbuf_base
        return stack.enter_context(nc.sbuf_tensor(name, [P, cols], dt))

    def sem(name):
        return stack.enter_context(nc.semaphore(name))

    with stack:
        H = sb("H", NT * D_MODEL)
        X = sb("X", KT * TOK)
        U = sb("U", 21504)
        W = sb("W", 9984)
        WR = sb("WR", RING * SLOT)
        CN = sb("CN", 1024)
        MK = sb("MK", 2 * LEVELS * 64, u8)
        PR = sb("PR", 1312)
        MOD = sb("MOD", DEPTH * 96)
        SC = sb("SC", 104)
        ST = sb("ST", 4 * 32 + 64 + 64)
        PS = [stack.enter_context(nc.psum_tensor(f"PS{i}", [P, 1024], f32)) for i in range(4)]

        XH = nc.alloc_sbuf_tensor_at("XH", [P, KT * TOK], f32r, offset=starts["X"])
        XL = nc.alloc_sbuf_tensor_at("XL", [P, KT * TOK], f32r, offset=starts["U"] + 4 * FT * TOK)
        EU = nc.alloc_sbuf_tensor_at("EU", [P, 8 * ENTRY], f32r, offset=starts["U"])
        EW = nc.alloc_sbuf_tensor_at("EW", [P, 2 * ENTRY], f32r, offset=starts["W"] + 4 * 6656)
        WS = nc.alloc_sbuf_tensor_at("WS", [P, 2 * SLOT], f32r, offset=starts["W"] + 4 * 7680)

        def bank(n, cols=512):
            return PS[n // 2][:, (n % 2) * 512:(n % 2) * 512 + cols]

        h3 = H[:, :].rearrange("p (t d) -> p t d", t=NT)
        x3 = X[:, :].rearrange("p (k t) -> p k t", k=KT)
        xh3 = XH[:, :].rearrange("p (k t) -> p k t", k=KT)
        xl3 = XL[:, :].rearrange("p (k t) -> p k t", k=KT)
        entries = ([EU[:, e * ENTRY:(e + 1) * ENTRY] for e in range(8)],
                   [t[:, e * ENTRY:(e + 1) * ENTRY] for t in (XH, XL, EW) for e in range(2)])
        ws5 = WS[:, :].rearrange("p (b s k c) -> p b s k c", b=2, s=2, k=KT)

        def uview(at, blocks, cols):
            return U[:, at:at + blocks * cols].rearrange("p (b c) -> p b c", b=blocks)

        cq, ci = uview(0, 2, TOK), uview(1536, NT, 256)
        cz = [uview(4608, 2, TOK), uview(3072, 2, TOK)]
        cg = uview(6144, NT, 256)
        qT = {"A": uview(7680, 2, TOK), "B": uview(11520, 2, TOK), "D": uview(15360, 2, TOK)}
        kT = {"A": uview(9216, 2, TOK), "B": uview(13056, 2, TOK), "D": uview(16896, 4, TOK)}
        vv = {"A": uview(10752, NT, 128), "B": uview(14592, NT, 128), "D": uview(19968, NT, 256)}
        biasv = U[:, 0:HEADS * BIAS_ROWS * 64].rearrange("p (h e) -> p h e", h=HEADS)
        g3 = uview(0, FT, TOK)

        ident = CN[:, 0:128]
        cosv = CN[:, 128:384].rearrange("p (t d) -> p t d", t=NLT)
        sinv = CN[:, 384:640].rearrange("p (t d) -> p t d", t=NLT)
        amask = CN[:, 640:1024]
        mk4 = MK[:, :].rearrange("p (d m t) -> p d m t", d=2, m=LEVELS)
        cvec = PR[:, 0:16]
        bmod = PR[:, 16:112].rearrange("p (l j) -> p l j", l=DEPTH)
        convp = PR[:, 112:464].rearrange("p (l w j) -> p l w j", l=DEPTH, w=4)
        lbl = PR[:, 464:472].rearrange("p (l e) -> p l e", l=DEPTH)
        qkn = PR[:, 472:728].rearrange("p (l w d) -> p l w d", l=DEPTH, w=2)
        onorm = PR[:, 728:1240].rearrange("p (l c) -> p l c", l=DEPTH)
        sinkv = PR[:, 1240:1248].rearrange("p (l h) -> p l h", l=DEPTH)
        scv = SC[:, 0:16].rearrange("p (k v) -> p k v", k=KT)
        lb4 = SC[:, 16:24].rearrange("p (l e) -> p l e", l=DEPTH)
        oml4 = SC[:, 24:32].rearrange("p (l e) -> p l e", l=DEPTH)
        lbt = SC[:, 32:48].rearrange("p (a e) -> p a e", a=4)
        cexp = SC[:, 48:64]
        sel = SC[:, 96:98]
        ones = SC[:, 98:99]
        mhalf = SC[:, 64:64 + 32]
        mod3 = MOD[:, :].rearrange("p (l j v) -> p l j v", l=DEPTH, j=48)
        ring = WR[:, :].rearrange("p (r c) -> p r c", r=RING)

        raw = W[:, 0:1536].rearrange("p (r c) -> p r c", r=3)
        rot = W[:, 1536:3072].rearrange("p (r c) -> p r c", r=3)
        ra = W[:, 3072:3584]
        rb = W[:, 3584:4096]
        rss = W[:, 4096:4112]
        maccs = [W[:, a:a + 1024].rearrange("p (r v c) -> p r v c", r=2, v=2) for a in (5120, 6144)]
        macc_of = lambda mac: maccs[mac > 24 - MOD_FIRST][:, mac % 2]
        EX = [W[:, i * 1152:(i + 1) * 1152].rearrange("p (e t) -> p e t", e=9) for i in range(2)]
        QE = [W[:, 2304 + i * 1024:2304 + (i + 1) * 1024] for i in range(2)]
        QL = [q[:, P:].rearrange("p (m h t) -> p m h t", m=LEVELS, h=2) for q in QE]
        KE = [W[:, 4352 + i * 1024:4352 + (i + 1) * 1024].rearrange("p (e t) -> p e t", e=8) for i in range(2)]
        YB = [W[:, 6400 + i * 256:6400 + (i + 1) * 256] for i in range(2)]
        QK = [W[:, 6912 + i * 128:6912 + (i + 1) * 128] for i in range(2)]
        KB = [W[:, 7424 + i * 128:7424 + (i + 1) * 128] for i in range(4)]
        CB = [W[:, 7936 + i * 128:7936 + (i + 1) * 128] for i in range(2)]
        AT = [[W[:, 8192 + (2 * d + i) * 256:8192 + (2 * d + i + 1) * 256].rearrange("p (h t) -> p h t", h=2)
               for i in range(2)] for d in range(2)]
        SS = W[:, 9216:9728].rearrange("p (d b v) -> p d b v", d=2, b=2)
        KDT = [W[:, 9728 + i * 128:9728 + (i + 1) * 128] for i in range(2)]
        osq = W[:, 0:1536]
        PB = [W[:, i * 768:(i + 1) * 768] for i in range(3)]
        PT = [W[:, 2304 + i * 768:2304 + (i + 1) * 768] for i in range(2)]
        OB = [W[:, 3840 + i * 256:3840 + (i + 1) * 256] for i in range(2)]
        stat = ST[:, 0:128].rearrange("p (q s h) -> p q s h", q=4, s=8)
        lnp = W[:, 1536:3584]
        gav = W[:, 3584:5632].rearrange("p (v c) -> p v c", v=2)
        gtmp = W[:, 5632:6656].rearrange("p (r c) -> p r c", r=2)
        xv = W[:, 6656:7680].rearrange("p (r c) -> p r c", r=2)
        xvc = W[:, 6144:6656].rearrange("p (r c) -> p r c", r=2)
        bnb = ST[:, 128:128 + 48].rearrange("p (r c) -> p r c", r=3)
        ross = ST[:, 192:192 + 24]
        DEC = ST[:, 216:220]
        at = [W[:, 1536 + i * 768:1536 + (i + 1) * 768] for i in range(2)]
        vt = [W[:, 3072 + i * 768:3072 + (i + 1) * 768] for i in range(2)]
        sl = [W[:, 4608 + i * 768:4608 + (i + 1) * 768] for i in range(2)]

        w_arrived = [sem(f"w_arrived{r}") for r in range(RING)]
        consts_in = sem("consts_in")
        h_in = sem("h_in")
        sc_ready = sem("sc_ready")
        e_lb = sem("e_lb")
        halves = sem("halves")
        bias_in = sem("bias_in")
        ln_in = sem("ln_in")
        out_stored = sem("out_stored")
        dve_step = sem("dve_step")
        pool_step = sem("pool_step")
        act_step = sem("act_step")
        mod_sum = sem("mod_sum")
        mod_done = sem("mod_done")
        tp_lat = sem("tp_lat")
        tp_ctx = sem("tp_ctx")
        x_lat = sem("x_lat")
        x_ctx = sem("x_ctx")
        x_high = sem("x_high")
        x_low = sem("x_low")
        w_high = sem("w_high")
        w_low = sem("w_low")
        tile_high = sem("tile_high")
        acts_low = sem("acts_low")
        rows_low = sem("rows_low")
        tile_used = sem("tile_used")
        job_sum = sem("job_sum")
        job_act = sem("job_act")
        roped = sem("roped")
        rot_tp = sem("rot_tp")
        qk_in = sem("qk_in")
        ss_ready = sem("ss_ready")
        root_ready = sem("root_ready")
        e_in = sem("e_in")
        yk = sem("yk")
        lnr = sem("lnr")
        subs = sem("subs")
        expd = sem("expd")
        qe = sem("qe")
        ke = sem("ke")
        maps = sem("maps")
        kdt = sem("kdt")
        kd_in = sem("kd_in")
        atd = sem("atd")
        o_sum = sem("o_sum")
        kv_sum = sem("kv_sum")
        o_out = sem("o_out")
        s_new = sem("s_new")
        ro_sq = sem("ro_sq")
        ro_rstd = sem("ro_rstd")
        ro_out = sem("ro_out")
        ro_tp = sem("ro_tp")
        ro_in = sem("ro_in")
        sc_sum = sem("sc_sum")
        mx = sem("mx")
        ex = sem("ex")
        p_tp = sem("p_tp")
        pt_act = sem("pt_act")
        pt_dve = sem("pt_dve")
        o_pv = sem("o_pv")
        o_norm = sem("o_norm")
        ga_sum = sem("ga_sum")
        ga_in = sem("ga_in")
        acc_sum = sem("acc_sum")
        acc_read = sem("acc_read")
        bn_ready = sem("bn_ready")
        rstd_ready = sem("rstd_ready")
        ln_norm = sem("ln_norm")
        ln_done = sem("ln_done")
        up_sum = sem("up_sum")
        base_ready = sem("base_ready")
        conv_done = sem("conv_done")
        gate_ready = sem("gate_ready")
        hid_ready = sem("hid_ready")
        zeroed = sem("zeroed")
        mac_done = sem("mac_done")
        padded = sem("padded")

        def has_ctx(l):
            return l + 1 < DEPTH

        def tiles(l):
            return NT if has_ctx(l) else NLT

        class Job:
            pass

        jobs = []
        for l in range(DEPTH):
            order = [k for k in STREAM if (k[0] == "in" and k[1] == l)
                     or (k[0] == "mod" and l == 0 and k[2] >= MOD_FIRST and k[1] == 0)]
            for key in order:
                kind, _, s, _ = key
                parts = []
                if kind == "mod":
                    parts = [("mod", s, 0)]
                else:
                    with_ctx = has_ctx(l) or s not in LATENT_ONLY
                    if s in FEATURE:
                        parts = [("feat", b, w) for b in range(2) for w in range(1 + with_ctx)]
                    else:
                        parts = [("tok", p, 0) for p in range(2 + with_ctx)]
                for n, (kind, a, b) in enumerate(parts):
                    j = Job()
                    j.l, j.slot, j.kind, j.a, j.b, j.key = l, s, kind, a, b, key
                    j.first, j.last = n == 0, n == len(parts) - 1
                    j.rope = kind == "tok" and s in (QA, KVA, QB, KVB)
                    jobs.append(j)
        n_act = n_rope = n_e = 0
        n_dve = MOD_FIRST
        for j in jobs:
            if j.kind == "mod":
                n_dve += 1
            else:
                n_act += 1
            j.after = (n_act, n_dve)
            if j.rope:
                j.r = n_rope
                n_rope += 1
            j.is_e = j.slot in (FCF, FCB) and j.kind == "feat"
            if j.is_e:
                n_e += 1
                j.e = n_e
        jobs_of = [[j for j in jobs if j.l == l] for l in range(DEPTH)]
        own_of = [[j for j in js if j.kind == "mod" or j.slot in IN_ORDER[:OWN_SLOTS]] for js in jobs_of]
        beside_of = [[j for j in js if j not in own] for js, own in zip(jobs_of, own_of)]
        n_sum = n_mac = 0
        for j in jobs:
            if j.kind == "mod":
                n_mac += 1
                j.mac = n_mac
            else:
                n_sum += 1
                j.sum = n_sum
        for l in range(DEPTH):
            js = jobs_of[l]
            real = [j for j in js if j.kind != "mod"]
            own = [j for j in real if j.slot in IN_ORDER[:OWN_SLOTS]]
            for n, j in enumerate(real):
                j.bank = n % 2
                j.freed = real[n - 2].after[0] if n >= 2 else None
                j.turns = [real[n - 2]] if n >= 2 and real[n - 2].rope else []
                if j is own[-1]:
                    j.turns += [q for q in real[n - 1:n + 1] if q.rope]
                elif j not in own:
                    j.turns = []
            for j in js:
                if j.kind == "mod":
                    j.turns = []

        units = []
        n_out = n_st = n_u = 0
        for l in range(DEPTH):
            for d in range(2):
                order = [NLT + c for c in range(NCT)][::1 - 2 * d] + list(range(NLT))[::1 - 2 * d]
                for step, t in enumerate(order):
                    for b in range(2):
                        u = Job()
                        u.l, u.d, u.t, u.b, u.step, u.g = l, d, t, b, step, n_u
                        n_u += 1
                        u.out = t < NLT or has_ctx(l)
                        u.state = step < NT - 1
                        u.no, u.ns = n_out, n_st
                        n_out += u.out
                        n_st += u.state
                        units.append(u)
        units_of = [[u for u in units if u.l == l] for l in range(DEPTH)]
        beside = {}
        for l in range(DEPTH):
            n, m = len(units_of[l]) + 1, len(beside_of[l])
            for i in range(n):
                beside[l, i] = beside_of[l][i * m // n:(i + 1) * m // n]

        atts = []
        for l in range(DEPTH):
            for g in "ABD":
                for t in range(tiles(l)):
                    for hd in range(HEADS):
                        a = Job()
                        a.l, a.grp, a.t, a.h, a.g, a.quad = l, g, t, hd, len(atts), len(atts) // HEADS
                        if t >= NLT:
                            a.lo, a.hi = 0, 0
                        elif g == "A":
                            a.lo, a.hi = max(0, t - 1), min(NLT, t + 2)
                        else:
                            a.lo, a.hi = 0, NLT
                        a.p_items = []
                        a.keys = list(range(a.lo, a.hi)) + [NLT + c for c in range(NCT)]
                        atts.append(a)
        atts_of = [[a for a in atts if a.l == l] for l in range(DEPTH)]
        LAG = 2
        n_pa = n_pd = 0
        items_at = {}
        flat = []
        for l in range(DEPTH):
            au = atts_of[l]
            first_item = len(flat)
            for i in range(len(au) + LAG + 3):
                its = []
                if LAG <= i < len(au) + LAG:
                    a = au[i - LAG]
                    cuts = [0, min(3, len(a.keys)), len(a.keys)]
                    for n in range(2):
                        if cuts[n + 1] > cuts[n]:
                            its.append(("p", a, cuts[n], cuts[n + 1], "act" if n == 0 else "dve"))
                if LAG + 2 <= i < len(au) + LAG + 2 and au[i - LAG - 2].h == HEADS - 1:
                    its.append(("o", au[i - LAG - 2], 0, 2, "act"))
                made = []
                for it in its:
                    o = Job()
                    o.kind, o.a, o.lo, o.hi, o.eng = it
                    if o.eng == "act":
                        n_pa += 1
                    else:
                        n_pd += 1
                    o.done = (n_pa, n_pd)
                    o.n = len(flat) - first_item
                    o.index = len(flat)
                    o.prev = flat[-2].done if o.n >= 2 else None
                    flat.append(o)
                    made.append(o)
                items_at[l, i] = made
        quads = []
        for o in flat:
            if o.kind == "p":
                o.a.p_items.append(o)
            else:
                quads.append(o)

        ups = []
        n_c = n_m = 0
        for key in STREAM:
            if key[0] == "up":
                for half in range(2):
                    u = Job()
                    u.kind, u.l, u.j, u.half, u.key = "up", key[1], key[2], half, key
                    u.c = n_c
                    n_c += 1
                    ups.append(u)
            elif key[0] == "mod" and key[1] > 0:
                u = Job()
                u.kind, u.l, u.j, u.key = "mod", key[1] - 1, key[2], key
                ups.append(u)
        n_m = 24
        c = 0
        for u in ups:
            if u.kind == "mod":
                n_m += 1
            else:
                c += 1
            u.done = (c, n_m)
        ups_of = [[u for u in ups if u.l == l] for l in range(DEPTH)]
        for l in range(DEPTH):
            for n, u in enumerate(ups_of[l]):
                u.pos = n % 4
                u.freed = ups_of[l][n - 4].done if n >= 4 else None

        stages = [(0, 0, True), (0, 24, True), (1, 0, True), (1, 24, False)]
        ctx_before = [KT * sum(s[2] for s in stages[:m]) for m in range(5)]
        res = [(l, i) for l in range(DEPTH) for i in range(2)]
        tiles_before = [sum(tiles(l) for l, _ in res[:m]) for m in range(5)]
        e_end = [sum(j.is_e for j in jobs if j.l <= l) for l in range(DEPTH)]

        def ga_before(m):
            return sum(4 if has_ctx(l) else 2 for l, _ in res[:m])

        def ro_parts(n):
            return sum(4 if has_ctx(l) else 2 for l in range(n))

        def flat_end(l):
            return [o for o in flat if o.a.l <= l][-1].done

        release = {}
        for i in range(MOD_FIRST):
            release["mod", 0, i, 0] = (mod_sum, i + 1)
        for j in jobs:
            release[j.key] = (mac_done, j.mac) if j.kind == "mod" else (job_sum, j.sum)
        for u in ups:
            if u.kind == "mod":
                n_mac += 1
                u.mac = n_mac
                release[u.key] = (mac_done, u.mac)
            else:
                release[u.key] = (w_low, u.c + 1)
        k_tiles = [[] for _ in res]
        n_q = n_used = 0
        for m, (l, i) in enumerate(res):
            total = FT if i else KT
            for n in range(2):
                single = KT - 4 if i == 0 else (FT - 2, FT - 6)[n]
                for k in range(total):
                    q = Job()
                    q.n, q.k, q.q, q.i, q.single = n, k, n_q, len(k_tiles[m]), k >= single
                    n_q += 1
                    if q.single:
                        q.done = (acc_sum, 2 * tiles_before[m] + (n + 1) * tiles(l))
                    else:
                        n_used += 1
                        q.done = (tile_used, n_used)
                    q.key = ("down" if i else "out", l, n, k // KDN)
                    q.entry = entries[i][q.i % len(entries[i])]
                    q.before = k_tiles[m][q.i - len(entries[i])].done if q.i >= len(entries[i]) else None
                    release[q.key] = (rows_low, q.q + 1)
                    k_tiles[m].append(q)

        def split_parts(q, nt):
            e = q.entry
            return (e[:, 0:nt * P], e[:, TOK:TOK + nt * P]), (e[:, 2 * TOK:2 * TOK + 512], e[:, 2 * TOK + 512:])

        def rows_of(q):
            return ring[:, PLAN[SLOT_AT[q.key]][0], (q.k % KDN) * 512:(q.k % KDN) * 512 + 512]

        def before_up(l):
            n = max(n for n in range(SLOT_AT["up", l, 0, 0]) if PLAN[n][0] == 0)
            return release[STREAM[n]]

        def wait_all(eng, *pairs):
            for s, v in pairs:
                if v > 0:
                    eng.wait_ge(s, v)

        def att_end(l):
            return len([a for a in atts if a.l <= l])

        def unit_end(l):
            us = [u for u in units if u.l <= l]
            return len(us), sum(u.out for u in us), sum(u.state for u in us)

        def mods_done(l):
            return 24 * (l + 1)

        def half_slot(u):
            return ring[:, PLAN[SLOT_AT[u.key]][0], :].rearrange("p (k h c) -> p k h c", k=KT, h=2)[:, :, u.half, :]

        def turned(u):
            return PS[1 + u.g % 2][:, LEVELS * P:(LEVELS + 1) * P]

        block = stack.enter_context(nc.Block())

        @block.sync
        def _(sp):
            for dst, src in ((PR[:, 0:1248], params), (CN[:, :], consts), (W[:, 0:2 * LEVELS * 64], masks)):
                sp.dma_start(dst, src).then_inc(consts_in, 16)
            sp.dma_start(h3[:, 0:NLT, :], x.rearrange("(t p) d -> p t d", p=P)).then_inc(h_in, 16)
            sp.dma_start(h3[:, NLT:NT, :], ctx_in.rearrange("(t p) d -> p t d", p=P)).then_inc(h_in, 16)
            for n, key in enumerate(STREAM):
                place, count, before = PLAN[n]
                if before is not None:
                    sp.wait_ge(*release[STREAM[before]])
                if place == 0 and key[1] > 0 and STREAM[before][1] < key[1]:
                    sp.wait_ge(acc_sum, 2 * tiles_before[2 * key[1]])
                half = key[0] == "down" and key[3] == DN_GROUPS - 1 and FT % KDN
                cols = (FT % KDN) * 512 if half else SLOT
                sp.dma_start(ring[:, place, 0:cols], weights[n, :, 0:cols]).then_inc(w_arrived[place], 16)

        @block.tensor
        def _(pe):
            def slot(key):
                place, count, _ = PLAN[SLOT_AT[key]]
                pe.wait_ge(w_arrived[place], 16 * count)
                return ring[:, place, :]

            def mod_products(wk, b):
                for jj in range(2):
                    for k in range(KT):
                        mm = pe.matmul(bank(b)[:, 2 * jj:2 * jj + 2], wk[:, k, jj * P:(jj + 1) * P], scv[:, k, :],
                                       start=(k == 0), stop=(k == KT - 1))
                mm.then_inc(mod_sum, 1)

            def mod_sums(mac, out4):
                pe.wait_ge(mac_done, mac)
                for jj in range(2):
                    for v in range(2):
                        mm = pe.matmul(out4[:, 2 * jj + v:2 * jj + v + 1], macc_of(mac)[:, v, jj * P:(jj + 1) * P], ones,
                                       start=True, stop=True)
                mm.then_inc(mod_sum, 1)

            pe.wait_ge(consts_in, 48)
            pe.wait_ge(sc_ready, 1)
            for i in range(MOD_FIRST):
                mod_products(slot(("mod", 0, i, 0)).rearrange("p (k c) -> p k c", k=KT), i)

            def transposes(m):
                l, _, with_ctx = stages[m]
                if m == 0:
                    pe.wait_ge(h_in, 32)
                    pe.wait_ge(mod_done, MOD_FIRST)
                for k in range(KT):
                    a = KT * m + k
                    if k >= 2:
                        pe.wait_ge(x_lat, a - 1)
                    for t in range(NLT):
                        if m > 0 and k == 0:
                            pe.wait_ge(ln_done, tiles_before[m - 1] + t + 1)
                        mm = pe.transpose(bank(k % 2)[:, t * P:(t + 1) * P], h3[:, t, k * P:(k + 1) * P], ident)
                    mm.then_inc(tp_lat, 1)
                if with_ctx:
                    for k in range(KT):
                        c = ctx_before[m] + k
                        if k >= 2:
                            pe.wait_ge(x_ctx, c - 1)
                        if m > 0 and k == 0:
                            pe.wait_ge(ln_done, tiles_before[m])
                        for t in range(NCT):
                            mm = pe.transpose(bank(2 + k % 2)[:, t * P:(t + 1) * P],
                                              h3[:, NLT + t, k * P:(k + 1) * P], ident)
                        mm.then_inc(tp_ctx, 1)
                pe.wait_ge(x_lat, KT * (m + 1))
                if m % 2:
                    pe.wait_ge(x_low, KT * (m // 2 + 1))
                if with_ctx:
                    pe.wait_ge(x_ctx, ctx_before[m + 1])

            ws = [None]

            def projections(l, js):
                for j in js:
                    if j.kind == "mod":
                        pe.wait_ge(mod_done, MOD_FIRST + j.mac - 1)
                        mod_sums(j.mac, bank(5))
                        continue
                    if j.first:
                        ws[0] = slot(j.key)
                    wk = ws[0].rearrange("p (k c) -> p k c", k=KT)
                    if j.freed:
                        pe.wait_ge(job_act, j.freed)
                    if j.kind == "feat":
                        lo, hi = (0, SEQ) if j.b == 0 else (SEQ, TOK)
                        for k in range(KT):
                            mm = pe.matmul(bank(j.bank)[:, 0:hi - lo], wk[:, k, j.a * P:(j.a + 1) * P],
                                           x3[:, k, lo:hi], start=(k == 0), stop=(k == KT - 1))
                    else:
                        for i in range(2):
                            t = 2 * j.a + i
                            for k in range(KT):
                                mm = pe.matmul(bank(j.bank)[:, i * 256:(i + 1) * 256], x3[:, k, t * P:(t + 1) * P],
                                               wk[:, k, :], start=(k == 0), stop=(k == KT - 1))
                    mm.then_inc(job_sum, 1)
                    for q in j.turns:
                        pe.wait_ge(roped, q.r + 1)
                        if q.r >= 2:
                            pe.wait_ge(qk_in, q.r - 1)
                        tb = bank(6 + q.r % 2)
                        r3 = rot[:, q.r % 3, :].rearrange("p (i c) -> p i c", i=2)
                        if q.slot in (QA, QB):
                            for g in range(2):
                                for i in range(2):
                                    mm = pe.transpose(tb[:, g * 256 + i * P:g * 256 + (i + 1) * P],
                                                      r3[:, i, g * P:(g + 1) * P], ident)
                        else:
                            for i in range(2):
                                mm = pe.transpose(tb[:, i * P:(i + 1) * P], r3[:, i, 0:P], ident)
                        mm.then_inc(rot_tp, 1)

            def hgrn(l):
                us = units_of[l]
                wait_all(pe, (mod_done, own_of[l][-1].after[1]), (qk_in, max(j.r for j in jobs_of[l] if j.rope) + 1))

                def score_maps(u):
                    par = u.g % 2
                    pe.wait_ge(qe, u.no + 1)
                    pe.wait_ge(zeroed, l + 1)
                    for m in range(LEVELS):
                        mm = pe.matmul(PS[1 + par][:, m * P:(m + 1) * P], KE[par][:, m, :],
                                       QL[par][:, m, :, :].rearrange("p h t -> p (h t)"), start=True, stop=True)
                    mm.then_inc(maps, 1)

                def turn_keys(u):
                    pe.transpose(turned(u), KE[u.g % 2][:, 7, :], ident).then_inc(kdt, 1)

                def outputs(u):
                    vslice = ci[:, u.t, u.b * P:(u.b + 1) * P]
                    if u.out:
                        ob = bank(7)
                        pe.wait_ge(atd, u.no + 1)
                        if u.no >= 1:
                            pe.wait_ge(o_out, u.no)
                        if u.step >= 1:
                            prev = [w for w in us if w.d == u.d and w.b == u.b and w.step == u.step - 1][0]
                            pe.wait_ge(s_new, prev.ns + 1)
                        pe.matmul(ob[:, P:P + 2], QK[u.g % 2], sel, start=True, stop=True)
                        for hh in range(2):
                            oh = ob[:, hh * 64:(hh + 1) * 64]
                            pe.matmul(oh, QE[u.g % 2][:, 0:P], SS[:, u.d, u.b, hh * 64:(hh + 1) * 64],
                                      start=True, stop=False)
                            mm = pe.matmul(oh, AT[u.d][u.no % 2][:, hh, :], vslice[:, hh * 64:(hh + 1) * 64],
                                           start=False, stop=True)
                        mm.then_inc(o_sum, 1)
                    if u.state:
                        pe.wait_ge(kd_in, u.ns + 1)
                        if u.ns >= 1:
                            pe.wait_ge(s_new, u.ns)
                        pe.matmul(bank(6)[:, 0:P], KDT[u.ns % 2], vslice, start=True, stop=True).then_inc(kv_sum, 1)

                for i in range(len(us) + 1):
                    if i < len(us):
                        u = us[i]
                        pe.wait_ge(ke, u.g + 1)
                        if i >= 2:
                            if us[i - 2].out:
                                pe.wait_ge(atd, us[i - 2].no + 1)
                            if us[i - 2].state:
                                pe.wait_ge(kd_in, us[i - 2].ns + 1)
                        if u.out:
                            score_maps(u)
                        if u.state:
                            turn_keys(u)
                    if i >= 1:
                        outputs(us[i - 1])
                    projections(l, beside[l, i])
                pe.wait_ge(ro_out, l + 1)
                pe.wait_ge(job_act, jobs_of[l][-1].after[0])
                n = 0
                for b in range(2):
                    for lo, hi in ((0, NLT), (NLT, tiles(l))):
                        if hi > lo:
                            for t in range(lo, hi):
                                mm = pe.transpose(bank(n)[:, (t - lo) * P:(t - lo + 1) * P],
                                                  cz[0][:, b, t * P:(t + 1) * P], ident)
                            mm.then_inc(ro_tp, 1)
                            n += 1

            def attention(l):
                au = atts_of[l]
                pe.wait_ge(ro_in, ro_parts(l + 1))
                pe.wait_ge(s_new, unit_end(l)[2])
                pe.wait_ge(o_out, unit_end(l)[1])

                def scores(a):
                    n = a.g
                    sbk = PS[n % 2]
                    if n - atts_of[l][0].g >= 2:
                        pe.wait_ge(ex, n - 1)
                    if a.grp == "D":
                        q, kk = qT["D"][:, a.h // 2, :], kT["D"][:, a.h, :]
                    else:
                        q, kk = qT[a.grp][:, a.h % 2, :], kT[a.grp][:, a.h // 2, :]
                    q = q[:, a.t * P:(a.t + 1) * P]
                    if a.hi > a.lo:
                        pe.matmul(sbk[:, 0:(a.hi - a.lo) * P], q, kk[:, a.lo * P:a.hi * P], start=True, stop=True)
                    pe.matmul(sbk[:, 512:512 + CTX], q, kk[:, SEQ:TOK], start=True, stop=True).then_inc(sc_sum, 1)

                def turn(o):
                    if o.prev:
                        wait_all(pe, (pt_act, o.prev[0]), (pt_dve, o.prev[1]))
                    tb = bank(4 + o.n % 2)
                    if o.kind == "p":
                        pe.wait_ge(ex, o.a.g + 1)
                        for i in range(o.lo, o.hi):
                            mm = pe.transpose(tb[:, (i - o.lo) * P:(i - o.lo + 1) * P],
                                              PB[o.a.g % 3][:, i * P:(i + 1) * P], ident)
                    else:
                        pe.wait_ge(o_norm, o.a.quad + 1)
                        for i in range(2):
                            mm = pe.transpose(tb[:, i * P:(i + 1) * P], OB[o.a.quad % 2][:, i * P:(i + 1) * P], ident)
                    mm.then_inc(p_tp, 1)

                def values(a):
                    if a.h == 0 and a.quad - atts_of[l][0].quad >= 2:
                        pe.wait_ge(o_norm, a.quad - 1)
                    last = a.p_items[-1]
                    wait_all(pe, (pt_act, last.done[0]), (pt_dve, last.done[1]))
                    ob = bank(6 + a.quad % 2)[:, a.h * 64:(a.h + 1) * 64]
                    vc = slice(a.h * 64, a.h * 64 + 64) if a.grp == "D" else slice((a.h // 2) * 64, (a.h // 2) * 64 + 64)
                    for i, kt in enumerate(a.keys):
                        mm = pe.matmul(ob, PT[a.g % 2][:, i * P:(i + 1) * P], vv[a.grp][:, kt, vc],
                                       start=(i == 0), stop=(i == len(a.keys) - 1))
                    mm.then_inc(o_pv, 1)

                for i in range(len(au) + LAG + 3):
                    if i < len(au):
                        scores(au[i])
                    for o in items_at[l, i]:
                        if o.kind == "p":
                            turn(o)
                    if LAG + 1 <= i < len(au) + LAG + 1:
                        values(au[i - LAG - 1])
                    for o in items_at[l, i]:
                        if o.kind == "o":
                            turn(o)

            def spread_gates(m):
                l, i = res[m]
                if i == 0:
                    wait_all(pe, (pt_act, flat_end(l)[0]), (pt_dve, flat_end(l)[1]), (o_norm, att_end(l) // HEADS))
                    pe.wait_ge(mod_done, mods_done(l))
                else:
                    wait_all(pe, (conv_done, ups_of[l][-1].done[0]), (mod_done, ups_of[l][-1].done[1]))
                    pe.wait_ge(hid_ready, FT * (l + 1))
                for v in range(2 if has_ctx(l) else 1):
                    for hf in range(2):
                        for k in range(4):
                            col = mod3[:, l, (16 if i == 0 else 40) + hf * 4 + k, v:v + 1]
                            mm = pe.matmul(bank(2 * v + hf)[:, k * P:(k + 1) * P], col.broadcast_to([P, P]), ident,
                                           start=True, stop=True)
                        mm.then_inc(ga_sum, 1)

            def residual_products(m):
                l, i = res[m]
                total = FT if i else KT
                base = 2 * tiles_before[m]

                def product(job, t, q):
                    acts, rows = split_parts(q, tiles(l))
                    for n, (a, b) in enumerate(((0, 0), (0, 1), (1, 0))):
                        mm = pe.matmul(bank((job + 4) % 8), acts[a][:, t * P:(t + 1) * P], rows[b],
                                       start=(q.k == 0 and n == 0), stop=(q.k == total - 1 and n == 2))
                    return mm

                def first_use(job):
                    if 4 <= job < 8:
                        pe.wait_ge(ga_in, ga_before(m + 1))
                    if job >= 8:
                        pe.wait_ge(acc_read, base + job - 8 + 1)

                for n in range(2):
                    for q in k_tiles[m][n * total:(n + 1) * total]:
                        if not q.single:
                            pe.wait_ge(acts_low, q.q + 1)
                            pe.wait_ge(rows_low, q.q + 1)
                            for t in range(tiles(l)):
                                if q.k == 0:
                                    first_use(n * tiles(l) + t)
                                mm = product(n * tiles(l) + t, t, q)
                            mm.then_inc(tile_used, 1)
                    last = [q for q in k_tiles[m] if q.n == n and q.single]
                    for t in range(tiles(l)):
                        for q in last:
                            if t == 0:
                                pe.wait_ge(acts_low, q.q + 1)
                                pe.wait_ge(rows_low, q.q + 1)
                            mm = product(n * tiles(l) + t, t, q)
                        mm.then_inc(acc_sum, 1)

            def ffn_up(l):
                us = ups_of[l]
                for u in us:
                    if u.freed:
                        wait_all(pe, (conv_done, u.freed[0]), (mod_done, u.freed[1]))
                    if u.kind == "mod":
                        mod_sums(u.mac, PS[u.pos])
                        continue
                    pe.wait_ge(w_low, u.c + 1)
                    w = ws5[:, u.c % 2]
                    for lo, hi in ((0, SEQ), (SEQ, TOK)) if has_ctx(l) else ((0, SEQ),):
                        for k in range(KT):
                            for part, src in ((0, xh3), (0, xl3), (1, xh3)):
                                mm = pe.matmul(PS[u.pos][:, lo:hi], w[:, part, k, :],
                                               src[:, k, lo:hi], start=(k == 0 and src is xh3 and part == 0),
                                               stop=(k == KT - 1 and part == 1))
                    mm.then_inc(up_sum, 1)

            for l in range(DEPTH):
                transposes(2 * l)
                projections(l, own_of[l])
                hgrn(l)
                attention(l)
                spread_gates(2 * l)
                residual_products(2 * l)
                pe.wait_ge(acc_read, 2 * tiles_before[2 * l + 1])
                transposes(2 * l + 1)
                ffn_up(l)
                spread_gates(2 * l + 1)
                residual_products(2 * l + 1)
                pe.wait_ge(acc_read, 2 * tiles_before[2 * l + 2])

        @block.scalar
        def _(act):
            steps = [0]

            def step(ins):
                steps[0] += 1
                ins.then_inc(act_step, 1)
                act.wait_ge(act_step, steps[0])

            act.wait_ge(consts_in, 48)
            act.activation(SC[:, 0:16], cvec, ACT.Silu).then_inc(sc_ready, 1)
            act.wait_ge(dve_step, 2)
            act.activation(cexp[:, 8:16], cexp[:, 0:8], ACT.Exp).then_inc(e_lb, 1)

            def modulate_latent(m):
                l, j0, _ = stages[m]
                act.wait_ge(mod_done, MOD_FIRST if m == 0 else mods_done(l))
                for k in range(KT):
                    act.wait_ge(tp_lat, KT * m + k + 1)
                    to = x3[:, k, 0:SEQ]
                    if m % 2:
                        to = xv[:, k % 2, :]
                        if k >= 2:
                            act.wait_ge(x_low, KT * (m // 2) + k - 1)
                    act.activation(to, bank(k % 2), ACT.Identity, bias=mod3[:, l, j0 + k, 0:1],
                                   scale=mod3[:, l, j0 + 8 + k, 0:1]).then_inc(x_lat, 1)

            def take_projections(l, js):
                dest = {QC: lambda a: cq[:, a, :], FCF: lambda a: cz[0][:, a, :], FCB: lambda a: cz[1][:, a, :],
                        QD: lambda a: qT["D"][:, a, :]}
                tok_dest = {IC: ci, GC: cg, VD: vv["D"]}
                for j in js:
                    if j.kind != "mod":
                        act.wait_ge(job_sum, j.sum)
                        ps3 = bank(j.bank).rearrange("p (i c) -> p i c", i=2)
                        if j.slot == KD:
                            lo, hi = (0, SEQ) if j.b == 0 else (SEQ, TOK)
                            act.wait_ge(padded, l + 1)
                            for hh in range(2):
                                rows = slice(64 * hh, 64 * hh + 64)
                                ins = act.activation(kT["D"][rows, 2 * j.a + hh, lo:hi], bank(j.bank)[rows, 0:hi - lo], ACT.Copy)
                        elif j.kind == "feat":
                            lo, hi = (0, SEQ) if j.b == 0 else (SEQ, TOK)
                            func, sc = {QC: (ACT.Silu, 1.0), FCF: (ACT.Exp, -1.0), FCB: (ACT.Exp, -1.0)}.get(
                                j.slot, (ACT.Copy, 1.0))
                            ins = act.activation(dest[j.slot](j.a)[:, lo:hi], bank(j.bank)[:, 0:hi - lo], func, scale=sc)
                        elif j.rope:
                            if j.slot in (KVA, KVB):
                                v = vv["A" if j.slot == KVA else "B"]
                                act.activation(v[:, 2 * j.a:2 * j.a + 2, :], ps3[:, :, P:], ACT.Copy)
                            if j.r >= 3:
                                act.wait_ge(roped, j.r - 2)
                            ins = act.activation(raw[:, j.r % 3, :], bank(j.bank), ACT.Copy)
                        else:
                            ins = act.activation(tok_dest[j.slot][:, 2 * j.a:2 * j.a + 2, :], ps3,
                                                 ACT.Silu if j.slot == GC else ACT.Copy)
                        ins.then_inc(job_act, 1)
                    for q in j.turns:
                        act.wait_ge(rot_tp, q.r + 1)
                        grp = "A" if q.slot in (QA, KVA) else "B"
                        tb = bank(6 + q.r % 2)
                        cols = slice(q.a * 256, q.a * 256 + 256)
                        if q.slot in (QA, QB):
                            ins = act.activation(qT[grp][:, :, cols], tb.rearrange("p (g t) -> p g t", g=2), ACT.Copy)
                        else:
                            act.wait_ge(padded, l + 1)
                            for hh in range(2):
                                rows = slice(64 * hh, 64 * hh + 64)
                                ins = act.activation(kT[grp][rows, hh, cols], tb[rows, 0:256], ACT.Copy)
                        ins.then_inc(qk_in, 1)

            def hgrn(l):
                us = units_of[l]
                act.preload_act_table_set("natural_log_exp_and_others")
                for i in range(-3, len(us)):
                    if 0 <= i + 3 < len(us):
                        u = us[i + 3]
                        act.wait_ge(yk, u.g + 1)
                        act.activation(YB[u.g % 2], YB[u.g % 2], ACT.Ln).then_inc(lnr, 1)
                    if 0 <= i + 2 < len(us):
                        u = us[i + 2]
                        last = (P - 1, 0)[u.d]
                        act.wait_ge(subs, u.g + 1)
                        if u.g >= 2:
                            act.wait_ge(ke, u.g - 1)
                        if u.g >= 2 and units[u.g - 2].out:
                            act.wait_ge(qe, units[u.g - 2].no + 1)
                        if u.ns >= 4:
                            act.wait_ge(s_new, u.ns - 3)
                        E, cb = EX[u.g % 2], CB[u.g % 2]
                        if u.out:
                            for m in range(ACT_LEVELS):
                                w = P >> m
                                for n in range(P // w):
                                    ref = n * w + w // 2 - 1 + u.d
                                    act.activation(E[:, 1 + m, n * w:(n + 1) * w], cb[:, n * w:(n + 1) * w], ACT.Abs,
                                                   bias=cb[:, ref:ref + 1], scale=-1.0)
                            step(act.activation(E[:, 1 + ACT_LEVELS:8, :], E[:, 1 + ACT_LEVELS:8, :], ACT.Abs))
                            act.activation(E[:, 0, :], cb, ACT.Exp)
                            act.activation(E[:, 1:8, :], E[:, 1:8, :], ACT.Exp, scale=-1.0)
                        act.activation(DEC[:, u.g % 4:u.g % 4 + 1], cb[:, last:last + 1], ACT.Exp)
                        act.activation(E[:, 8, :], cb, ACT.Exp, bias=cb[:, last:last + 1], scale=-1.0).then_inc(expd, 1)
                    if i >= 0 and us[i].state:
                        u = us[i]
                        act.wait_ge(kdt, u.ns + 1)
                        if u.ns >= 2:
                            act.wait_ge(kv_sum, u.ns - 1)
                        act.activation(KDT[u.ns % 2], turned(u), ACT.Copy).then_inc(kd_in, 1)
                    take_projections(l, beside.get((l, i - 1), []))
                for i in (len(us) - 1, len(us)):
                    take_projections(l, beside[l, i])
                n = 0
                for b in range(2):
                    for lo, hi in ((0, NLT), (NLT, tiles(l))):
                        if hi > lo:
                            act.wait_ge(ro_tp, ro_parts(l) + n + 1)
                            act.activation(x3[:, 4 + b, lo * P:hi * P], bank(n)[:, 0:(hi - lo) * P],
                                           ACT.Copy).then_inc(ro_in, 1)
                            n += 1
                act.dma_start(biasv, bias_d[l]).then_inc(bias_in, 16)

            def attention(l):
                au = atts_of[l]
                for i in range(len(au) + LAG + 3):
                    if i < len(au):
                        a = au[i]
                        sbk, pb = PS[a.g % 2], PB[a.g % 3]
                        nl = (a.hi - a.lo) * P
                        s4 = stat[:, a.quad % 4]
                        act.wait_ge(mx, a.g + 1)
                        if i >= 3:
                            act.wait_ge(p_tp, au[i - 3].p_items[-1].index + 1)
                        negm = s4[:, 3, a.h:a.h + 1]
                        if a.grp == "A":
                            act.activation(s4[:, 6, a.h:a.h + 1], sinkv[:, l, a.h:a.h + 1], ACT.Exp, bias=negm)
                        if nl and a.grp != "B":
                            act.activation(pb[:, 0:nl], pb[:, 0:nl], ACT.Exp, bias=negm,
                                           accum_out=s4[:, 4, a.h:a.h + 1])
                            act.activation(pb[:, nl:nl + CTX], sbk[:, 512:768], ACT.Exp, bias=negm, scale=SCALE,
                                           accum_out=s4[:, 5, a.h:a.h + 1]).then_inc(ex, 1)
                        else:
                            act.activation(pb[:, 0:nl + CTX], sbk[:, 512 - nl:768], ACT.Exp, bias=negm, scale=SCALE,
                                           accum_out=s4[:, 4, a.h:a.h + 1]).then_inc(ex, 1)
                    for o in items_at[l, i]:
                        if o.eng != "act":
                            continue
                        act.wait_ge(p_tp, o.index + 1)
                        tb = bank(4 + o.n % 2)
                        if o.kind == "p":
                            if o.a.g - au[0].g >= 2:
                                act.wait_ge(o_pv, o.a.g - 1)
                            act.activation(PT[o.a.g % 2][:, o.lo * P:o.hi * P], tb[:, 0:(o.hi - o.lo) * P],
                                           ACT.Copy).then_inc(pt_act, 1)
                        else:
                            k0 = {"A": 0, "B": 2, "D": 6}[o.a.grp]
                            act.activation(x3[:, k0:k0 + 2, o.a.t * P:(o.a.t + 1) * P],
                                           tb[:, 0:256].rearrange("p (k t) -> p k t", k=2),
                                           ACT.Copy).then_inc(pt_act, 1)

            def gates(m):
                l, i = res[m]
                base = ga_before(m)
                n = 0
                for v in range(2 if has_ctx(l) else 1):
                    for hf in range(2):
                        act.wait_ge(ga_sum, base + n + 1)
                        if n == 0:
                            act.dma_start(lnp, ln_rows[2 * l + i].partition_broadcast(P)).then_inc(ln_in, 16)
                        act.activation(gav[:, v, hf * 512:(hf + 1) * 512], bank(2 * v + hf), ACT.Copy).then_inc(ga_in, 1)
                        n += 1
                src = (x3, g3)[i]
                if i == 0:
                    wait_all(act, (pt_act, flat_end(l)[0]), (ro_in, ro_parts(l + 1)))
                for q in k_tiles[m]:
                    if q.k % KDN == 0:
                        act.wait_ge(w_arrived[PLAN[SLOT_AT[q.key]][0]], 16 * PLAN[SLOT_AT[q.key]][1])
                    if q.before:
                        act.wait_ge(*q.before)
                    acts, rows = split_parts(q, tiles(l))
                    act.activation(acts[0], src[:, q.k, 0:tiles(l) * P], ACT.Copy).then_inc(tile_high, 1)
                    act.activation(rows[0], rows_of(q), ACT.Copy).then_inc(tile_high, 1)

            def ffn(l):
                n = TOK if has_ctx(l) else SEQ

                def gate(j):
                    jg = FT * l + j
                    act.wait_ge(conv_done, 2 * jg + 1)
                    if jg >= 2:
                        act.wait_ge(hid_ready, jg - 1)
                    act.activation(sl[jg % 2][:, 0:n], at[jg % 2][:, 0:n], ACT.Silu).then_inc(gate_ready, 1)

                act.wait_ge(*before_up(l))
                real = [u for u in ups_of[l] if u.kind == "up"]

                def high_part(u):
                    if u.half == 0:
                        act.wait_ge(w_arrived[PLAN[SLOT_AT[u.key]][0]], 16 * PLAN[SLOT_AT[u.key]][1])
                    if u.c >= 2:
                        act.wait_ge(up_sum, u.c - 1)
                    act.activation(ws5[:, u.c % 2, 0], half_slot(u), ACT.Copy).then_inc(w_high, 1)

                high_part(real[0])
                high_part(real[1])
                for n_u, u in enumerate(real):
                    jg = FT * l + u.j
                    dst = (at, vt)[u.half][jg % 2]
                    act.wait_ge(up_sum, u.c + 1)
                    if jg >= 2:
                        act.wait_ge(hid_ready, jg - 1)
                    jj = u.half * FT + u.j
                    act.activation(dst[:, 0:n], PS[u.pos][:, 0:n], ACT.Identity, bias=convp[:, l, 3, jj:jj + 1],
                                   scale=convp[:, l, 1, jj:jj + 1]).then_inc(base_ready, 1)
                    if n_u + 2 < len(real):
                        high_part(real[n_u + 2])
                    if u.half == 1 and u.j >= 1:
                        gate(u.j - 1)
                gate(FT - 1)

            for l in range(DEPTH):
                modulate_latent(2 * l)
                take_projections(l, own_of[l])
                hgrn(l)
                attention(l)
                gates(2 * l)
                modulate_latent(2 * l + 1)
                ffn(l)
                gates(2 * l + 1)
            for t in range(NLT):
                act.wait_ge(ln_done, tiles_before[3] + t + 1)
                act.dma_start(out[t * P:(t + 1) * P, :], h3[:, t, :]).then_inc(out_stored, 16)
            act.wait_ge(out_stored, 16 * NLT)

        @block.vector
        def _(dve):
            steps = [0]

            def mark(ins):
                steps[0] += 1
                ins.then_inc(dve_step, 1)

            def step(ins):
                mark(ins)
                dve.wait_ge(dve_step, steps[0])

            dve.wait_ge(consts_in, 48)
            step(dve.tensor_tensor(lbt[:, 0, :], lbl[:, 0, :], lbl[:, 1, :], ALU.max))
            step(dve.tensor_tensor(cexp[:, 0:8].rearrange("p (l e) -> p l e", l=2), lbl,
                                   lbt[:, 0:1, :].broadcast_to([P, 2, 4]), ALU.subtract))
            dve.wait_ge(e_lb, 1)
            e2 = cexp[:, 8:16].rearrange("p (l e) -> p l e", l=2)
            step(dve.tensor_tensor(lbt[:, 1, :], e2[:, 0, :], e2[:, 1, :], ALU.add))
            step(dve.reciprocal(lbt[:, 1, :], lbt[:, 1, :]))
            step(dve.tensor_tensor(e2, e2, lbt[:, 1:2, :].broadcast_to([P, 2, 4]), ALU.mult))
            step(dve.tensor_tensor(lb4[:, 0, :], e2[:, 0, :], e2[:, 0, :], ALU.subtract))
            step(dve.tensor_tensor(lbt[:, 2, :], e2[:, 0, :], e2[:, 1, :], ALU.add))
            step(dve.tensor_tensor(lb4[:, 1, :], lbt[:, 2, :], e2[:, 0, :], ALU.subtract))
            step(dve.tensor_scalar(oml4, lb4, -1.0, 1.0, ALU.mult, ALU.add))
            dve.memset(ones, 1.0)
            step(dve.memset(sel, 0.0))
            dve.memset(sel[0:64, 0:1], 1.0)
            step(dve.memset(sel[64:P, 1:2], 1.0))
            dve.memset(mhalf, -0.5).then_inc(halves, 1)

            def mod_macs(key, mac):
                place, count, _ = PLAN[SLOT_AT[key]]
                wk = ring[:, place, :].rearrange("p (k c) -> p k c", k=KT)
                if mac >= 3:
                    dve.wait_ge(mod_sum, MOD_FIRST + mac - 2)
                dve.wait_ge(w_arrived[place], 16 * count)
                if mac == 1:
                    dve.wait_ge(sc_ready, 1)
                for k in range(KT):
                    for v in range(2):
                        acc = macc_of(mac)[:, v, :]
                        if k == 0:
                            ins = dve.tensor_scalar(acc, wk[:, k, :], scv[:, k, v:v + 1], None, ALU.mult)
                        else:
                            ins = dve.scalar_tensor_tensor(acc, wk[:, k, :], scv[:, k, v:v + 1], acc, ALU.mult, ALU.add)
                        if k < KT - 1:
                            mark(ins)
                    if k < KT - 1:
                        dve.wait_ge(dve_step, steps[0])
                ins.then_inc(mac_done, 1)
            step(dve.tensor_copy(MK[:, :], W[:, 0:2 * LEVELS * 64]))

            def mod_out(l, i, src):
                b = bmod[:, l, 2 * i:2 * i + 2].unsqueeze(2).broadcast_to([P, 2, 2])
                o = mod3[:, l, 2 * i:2 * i + 2, :]
                s3 = src[:, 0:4].rearrange("p (j v) -> p j v", j=2)
                if 4 <= i < 8 or 16 <= i < 20:
                    step(dve.tensor_tensor(o, s3, b, ALU.add))
                    dve.tensor_scalar(o, o, 1.0, None, ALU.add).then_inc(mod_done, 1)
                else:
                    dve.tensor_tensor(o, s3, b, ALU.add).then_inc(mod_done, 1)

            for i in range(MOD_FIRST):
                dve.wait_ge(mod_sum, i + 1)
                mod_out(0, i, bank(i))

            def modulate_context(m):
                l, j0, with_ctx = stages[m]
                if m % 2:
                    for k in range(KT):
                        dve.wait_ge(x_lat, KT * m + k + 1)
                        dve.tensor_copy(xh3[:, k, 0:SEQ], xv[:, k % 2, :]).then_inc(x_high, 1)
                if with_ctx:
                    for k in range(KT):
                        if k == 0:
                            dve.wait_ge(mod_done, MOD_FIRST if m == 0 else mods_done(l))
                        dve.wait_ge(tp_ctx, ctx_before[m] + k + 1)
                        if m % 2:
                            v = xvc[:, k % 2, :]
                            step(dve.tensor_scalar(v, bank(2 + k % 2, 256), mod3[:, l, j0 + 8 + k, 1:2],
                                                   mod3[:, l, j0 + k, 1:2], ALU.mult, ALU.add))
                            step(dve.tensor_copy(xh3[:, k, SEQ:TOK], v))
                            dve.tensor_tensor(xl3[:, k, SEQ:TOK], v, xh3[:, k, SEQ:TOK], ALU.subtract).then_inc(x_ctx, 1)
                            continue
                        dve.tensor_scalar(x3[:, k, SEQ:TOK], bank(2 + k % 2, 256), mod3[:, l, j0 + 8 + k, 1:2],
                                          mod3[:, l, j0 + k, 1:2], ALU.mult, ALU.add).then_inc(x_ctx, 1)

            def rotate(j):
                l, heads = j.l, 4 if j.slot in (QA, QB) else 2
                rw = raw[:, j.r % 3, :]
                ro = rot[:, j.r % 3, :]
                dve.wait_ge(job_act, j.after[0])
                if j.r >= 1:
                    dve.wait_ge(roped, j.r)
                if j.r >= 3:
                    dve.wait_ge(rot_tp, j.r - 2)
                src4 = rw.rearrange("p (i h d) -> p i h d", i=2, d=HD)[:, :, 0:heads, :]
                if j.slot in (QB, KVB):
                    nh = 2 * heads
                    ra4 = ra.rearrange("p (i h d) -> p i h d", i=2, d=HD)[:, :, 0:heads, :]
                    step(dve.tensor_tensor(ra4, src4, src4, ALU.mult))
                    for i in range(2):
                        ins = dve.tensor_reduce(rss[:, 4 * i:4 * i + heads], ra4[:, i], AX, ALU.add)
                        mark(ins) if i == 0 else step(ins)
                    r8 = rss[:, 0:8]
                    if heads == 2:
                        for i in range(2):
                            ins = dve.tensor_scalar(rss[:, 4 * i:4 * i + 2], rss[:, 4 * i:4 * i + 2], 1.0 / HD, EPS,
                                                    ALU.mult, ALU.add)
                    else:
                        ins = dve.tensor_scalar(r8, r8, 1.0 / HD, EPS, ALU.mult, ALU.add)
                    ins.then_inc(ss_ready, 1)
                    rs[0] += 1
                    dve.wait_ge(root_ready, rs[0])
                    for i in range(2):
                        ins = dve.tensor_tensor(ra4[:, i], src4[:, i],
                                                rss[:, 8 + 4 * i:8 + 4 * i + heads].unsqueeze(2).broadcast_to([P, heads, HD]),
                                                ALU.mult)
                        mark(ins) if i == 0 else step(ins)
                    gain = qkn[:, l, 0 if j.slot == QB else 1, :].unsqueeze(1).broadcast_to([P, heads, HD])
                    plain = j.a * 2 >= NLT
                    dst = ro.rearrange("p (i h d) -> p i h d", i=2, d=HD)[:, :, 0:heads, :] if plain else src4
                    for i in range(2):
                        ins = dve.tensor_tensor(dst[:, i], ra4[:, i], gain, ALU.mult)
                        if plain and i == 1:
                            ins.then_inc(roped, 1)
                        elif i == 0:
                            mark(ins)
                        else:
                            step(ins)
                    if plain:
                        return
                elif j.a * 2 >= NLT:
                    dve.tensor_copy(ro, rw).then_inc(roped, 1)
                    return
                for i in range(2):
                    t = 2 * j.a + i
                    s = rw[:, i * 256:i * 256 + heads * HD]
                    o = ro[:, i * 256:i * 256 + heads * HD]
                    a_ = ra[:, i * 256:i * 256 + heads * HD]
                    b_ = rb[:, i * 256:i * 256 + heads * HD]
                    mark(dve.tensor_tensor(a_.rearrange("p (h d) -> p h d", d=HD), s.rearrange("p (h d) -> p h d", d=HD),
                                           cosv[:, t, :].unsqueeze(1).broadcast_to([P, heads, HD]), ALU.mult))
                    s5 = s.rearrange("p (h a f d) -> p h a f d", a=2, f=2, d=HD // 4)
                    b5 = b_.rearrange("p (h a f d) -> p h a f d", a=2, f=2, d=HD // 4)
                    t5 = sinv[:, t, :].rearrange("p (a f d) -> p a f d", a=2, f=2)
                    for f in range(2):
                        ins = dve.tensor_tensor(b5[:, :, :, f, :], s5[:, :, :, 1 - f, :],
                                                t5[:, :, f, :].unsqueeze(1).broadcast_to([P, heads, 2, HD // 4]), ALU.mult)
                        mark(ins)
                dve.wait_ge(dve_step, steps[0])
                v4 = lambda w: w.rearrange("p (i c) -> p i c", i=2)[:, :, 0:heads * HD]
                dve.tensor_tensor(v4(ro), v4(ra), v4(rb), ALU.add).then_inc(roped, 1)

            def project(l):
                mods = [j for j in own_of[l] if j.kind == "mod"]
                for j in own_of[l]:
                    if j.kind != "mod" and j.first:
                        for q in mods[:2]:
                            mod_macs(q.key, q.mac)
                        mods = mods[2:]
                    if j.kind == "mod":
                        dve.wait_ge(mod_sum, MOD_FIRST + j.mac)
                        mod_out(0, j.slot, bank(5))
                    elif j.is_e:
                        lo, hi = (0, SEQ) if j.b == 0 else (SEQ, TOK)
                        d = 0 if j.slot == FCF else 1
                        z = cz[d][:, j.a, lo:hi]
                        e = 2 * d + j.a
                        dve.wait_ge(job_act, j.after[0])
                        step(dve.tensor_scalar(z, z, 1.0, None, ALU.add))
                        step(dve.reciprocal(z, z))
                        dve.tensor_scalar(z, z, oml4[:, l, e:e + 1], lb4[:, l, e:e + 1], ALU.mult,
                                          ALU.add).then_inc(e_in, 1)
                    elif j.rope:
                        rotate(j)

            def later(a, u, w):
                return a.rearrange("p (n f t) -> p n f t", f=2, t=w)[:, :, 1 - u.d, :]

            def hgrn(l):
                us = units_of[l]
                dve.wait_ge(rot_tp, max(j.r for j in jobs_of[l] if j.rope) + 1)
                step(dve.memset(W[:, 2304:4352], 0.0))
                dve.memset(W[:, 8192:9728], 0.0).then_inc(zeroed, 1)
                dve.wait_ge(zeroed, l + 1)
                for i in range(-2, len(us) + 1):
                    if 0 <= i + 2 < len(us):
                        u = us[i + 2]
                        E, cb, ln = EX[u.g % 2], CB[u.g % 2], YB[u.g % 2]
                        dve.wait_ge(lnr, u.g + 1)
                        if u.g >= 2:
                            dve.wait_ge(expd, u.g - 1)
                            dve.wait_ge(ke, u.g - 1)
                            dve.wait_ge(subs, u.g)
                            if units[u.g - 2].out:
                                dve.wait_ge(qe, units[u.g - 2].no + 1)
                        r = slice(None, None, 1 - 2 * u.d)
                        scan = dve.tensor_tensor_scan(cb[:, r], ln[:, 0:P][:, r], ln[:, P:2 * P][:, r], 0.0,
                                                      ALU.add, ALU.add)
                        if not u.out:
                            scan.then_inc(subs, 1)
                        else:
                            step(scan)
                            for m in range(ACT_LEVELS, LEVELS):
                                half = P >> (m + 1)
                                ref = half - 1 + u.d
                                c3 = cb.rearrange("p (n w) -> p n w", w=2 * half)
                                ins = dve.tensor_tensor(E[:, 1 + m, :].rearrange("p (n w) -> p n w", w=2 * half), c3,
                                                        c3[:, :, ref:ref + 1].broadcast_to([P, P // (2 * half), 2 * half]),
                                                        ALU.subtract)
                            ins.then_inc(subs, 1)
                    nxt = us[i + 1] if 0 <= i + 1 < len(us) and us[i + 1].out else None
                    cur = us[i] if 0 <= i < len(us) and us[i].out else None
                    if nxt:
                        u = nxt
                        dve.wait_ge(expd, u.g + 1)
                        if u.no >= 2:
                            dve.wait_ge(o_sum, u.no - 1)
                        dve.tensor_tensor(QE[u.g % 2][:, 0:P], EX[u.g % 2][:, 0, :], cq[:, u.b, u.t * P:(u.t + 1) * P],
                                          ALU.mult)
                    if cur:
                        u = cur
                        if u.no >= 2:
                            dve.wait_ge(o_sum, u.no - 1)
                        dve.wait_ge(maps, u.no + 1)
                        maps4 = PS[1 + u.g % 2][:, 0:LEVELS * P].rearrange("p (m h c) -> p m h c", m=LEVELS, h=2)
                    for m in range(LEVELS):
                        w = P >> (m + 1)
                        if nxt:
                            for hh in range(2):
                                rows = slice(64 * hh, 64 * hh + 64)
                                ins = dve.tensor_tensor(
                                    QL[nxt.g % 2][rows, m, hh, :].rearrange("p (n t) -> p n t", t=w),
                                    later(EX[nxt.g % 2][rows, 1 + m, :], nxt, w),
                                    later(cq[rows, nxt.b, nxt.t * P:(nxt.t + 1) * P], nxt, w), ALU.mult)
                            if m == LEVELS - 1:
                                ins.then_inc(qe, 1)
                        if cur:
                            if m >= 1:
                                dve.wait_ge(dve_step, steps[0])
                            if (m + 1) * P > 512 >= m * P and u.state:
                                dve.wait_ge(kd_in, u.ns + 1)
                            dst = AT[u.d][u.no % 2].rearrange("p h (n f t) -> p h n f t", f=2, t=w)[:, :, :, 1 - u.d, :]
                            src = maps4[:, m, :, :].rearrange("p h (n t) -> p h n t", t=w)
                            msk = mk4[:, u.d, m, :].rearrange("p (n t) -> p n t", t=w).unsqueeze(1)
                            ins = dve.copy_predicated(dst, msk.broadcast_to([P, 2, 64 // w, w]), src)
                            if m < LEVELS - 1:
                                mark(ins)
                            else:
                                ins.then_inc(atd, 1)
                    if cur:
                        dve.wait_ge(atd, u.no + 1)
                    if i >= 1:
                        u = us[i - 1]
                        if u.out:
                            dve.wait_ge(o_sum, u.no + 1)
                            o = cz[0][:, u.b, u.t * P:(u.t + 1) * P]
                            ob = bank(7)
                            if u.no:
                                dve.wait_ge(o_out, u.no)
                            base = ob[:, 0:P]
                            if u.d == 1:
                                step(dve.tensor_tensor(o, base, o, ALU.add))
                                base = o
                            for hh in range(2):
                                c = slice(64 * hh, 64 * hh + 64)
                                ins = dve.scalar_tensor_tensor(o[:, c], ci[:, u.t, u.b * P + 64 * hh:u.b * P + 64 * hh + 64],
                                                               ob[:, P + hh:P + hh + 1], base[:, c], ALU.mult, ALU.add)
                            ins.then_inc(o_out, 1)
                        if u.state:
                            dve.wait_ge(kv_sum, u.ns + 1)
                            if u.ns >= 1:
                                dve.wait_ge(s_new, u.ns)
                            for hh in range(2):
                                rows, cols = slice(64 * hh, 64 * hh + 64), slice(64 * hh, 64 * hh + 64)
                                s = SS[rows, u.d, u.b, cols]
                                ins = dve.scalar_tensor_tensor(s, s, DEC[rows, u.g % 4:u.g % 4 + 1], bank(6)[rows, cols],
                                                               ALU.mult, ALU.add)
                            ins.then_inc(s_new, 1)
                nt = tiles(l)
                dve.wait_ge(o_out, unit_end(l)[1])
                o3 = cz[0][:, :, 0:nt * P]
                n = 2 * nt * 2
                step(dve.tensor_tensor(osq[:, 0:n * HD].rearrange("p (b c) -> p b c", b=2), o3, o3, ALU.mult))
                dve.tensor_reduce(ross[:, 0:n], osq[:, 0:n * HD].rearrange("p (n d) -> p n d", d=HD), AX,
                                  ALU.add).then_inc(ro_sq, 1)
                dve.wait_ge(ro_rstd, l + 1)
                for b in range(2):
                    ob3 = cz[0][:, b, 0:nt * P].rearrange("p (n d) -> p n d", d=HD)
                    rr = ross[:, b * 2 * nt:(b + 1) * 2 * nt].unsqueeze(2).broadcast_to([P, 2 * nt, HD])
                    ins = dve.tensor_tensor(ob3, ob3, rr, ALU.mult)
                    mark(ins) if b == 0 else step(ins)
                for b in range(2):
                    obt = cz[0][:, b, 0:nt * P].rearrange("p (t c) -> p t c", c=P)
                    on = onorm[:, l, b * P:(b + 1) * P].unsqueeze(1).broadcast_to([P, nt, P])
                    ins = dve.tensor_tensor(obt, obt, on, ALU.mult)
                    mark(ins) if b == 0 else step(ins)
                for b in range(2):
                    obt = cz[0][:, b, 0:nt * P].rearrange("p (t c) -> p t c", c=P)
                    ins = dve.tensor_tensor(obt, obt, cg[:, 0:nt, b * P:(b + 1) * P], ALU.mult)
                ins.then_inc(ro_out, 1)

            def attention(l):
                au = atts_of[l]
                for i in range(len(au) + LAG + 3):
                    if i < len(au):
                        a = au[i]
                        sbk, pb = PS[a.g % 2], PB[a.g % 3]
                        nl = (a.hi - a.lo) * P
                        s4 = stat[:, a.quad % 4]
                        m1, m2, m3, negm = [s4[:, w, a.h:a.h + 1] for w in range(4)]
                        sink = sinkv[:, l, a.h:a.h + 1]
                        if a.grp == "D" and a.t == 0 and a.h == 0:
                            dve.wait_ge(bias_in, 16 * (l + 1))
                            step(dve.tensor_scalar(U[:, 0:HEADS * BIAS_ROWS * 64], U[:, 0:HEADS * BIAS_ROWS * 64],
                                                   1.0 / SCALE, None, ALU.mult))
                        dve.wait_ge(sc_sum, a.g + 1)
                        if i == 0:
                            dve.wait_ge(ro_in, ro_parts(l + 1))
                        if nl and a.grp != "B":
                            if i >= 3:
                                dve.wait_ge(p_tp, au[i - 3].p_items[-1].index + 1)
                            mark(dve.tensor_reduce(m1, sbk[:, 512:768], AX, ALU.max))
                            if a.grp == "A":
                                at0 = P * (1 - (a.t - a.lo))
                                add = amask[:, at0:at0 + nl]
                            else:
                                e0 = 64 * (6 - 2 * a.t)
                                add = biasv[:, a.h, e0:e0 + nl]
                            step(dve.tensor_tensor_reduce(pb[:, 0:nl], sbk[:, 0:nl], add, SCALE, NEG * 8, ALU.add, ALU.max, m2))
                            step(dve.scalar_tensor_tensor(m3, m1, SCALE, m2, ALU.mult, ALU.max))
                            if a.grp == "A":
                                ins = dve.tensor_scalar(negm, m3, sink, -1.0, ALU.max, ALU.mult)
                            else:
                                ins = dve.tensor_scalar(negm, m3, -1.0, None, ALU.mult)
                            ins.then_inc(mx, 1)
                        else:
                            step(dve.tensor_reduce(m1, sbk[:, 512 - nl:768], AX, ALU.max))
                            if a.grp == "A":
                                step(dve.tensor_scalar(m3, m1, SCALE, sink, ALU.mult, ALU.max))
                                dve.tensor_scalar(negm, m3, -1.0, None, ALU.mult).then_inc(mx, 1)
                            else:
                                dve.tensor_scalar(negm, m1, -SCALE, None, ALU.mult).then_inc(mx, 1)
                    for o in items_at[l, i]:
                        if o.eng == "dve":
                            dve.wait_ge(p_tp, o.index + 1)
                            if o.a.g - au[0].g >= 2:
                                dve.wait_ge(o_pv, o.a.g - 1)
                            dve.tensor_copy(PT[o.a.g % 2][:, o.lo * P:o.hi * P],
                                            bank(4 + o.n % 2)[:, 0:(o.hi - o.lo) * P]).then_inc(pt_dve, 1)
                    if LAG + 1 <= i < len(au) + LAG + 1 and au[i - LAG - 1].h == HEADS - 1:
                        a = au[i - LAG - 1]
                        s4 = stat[:, a.quad % 4]
                        den = s4[:, 4, :]
                        dve.wait_ge(o_pv, a.g + 1)
                        dve.wait_ge(ex, a.g + 1)
                        if a.hi > a.lo and a.grp != "B":
                            step(dve.tensor_tensor(den, den, s4[:, 5, :], ALU.add))
                        if a.grp == "A":
                            step(dve.tensor_tensor(den, den, s4[:, 6, :], ALU.add))
                        step(dve.reciprocal(s4[:, 7, :], den))
                        if a.quad - au[0].quad >= 2:
                            dve.wait_ge(p_tp, quads[a.quad - 2].index + 1)
                        dve.tensor_tensor(OB[a.quad % 2].rearrange("p (h d) -> p h d", d=HD),
                                          bank(6 + a.quad % 2)[:, 0:256].rearrange("p (h d) -> p h d", d=HD),
                                          s4[:, 7, :].unsqueeze(2).broadcast_to([P, HEADS, HD]),
                                          ALU.mult).then_inc(o_norm, 1)

            def residual(m):
                l, i = res[m]
                nt, tb = tiles(l), tiles_before[m]

                def normalise(t):
                    b = bnb[:, (tb + t) % 3, :]
                    dve.wait_ge(rstd_ready, tb + t + 1)
                    step(dve.scalar_tensor_tensor(h3[:, t, :], h3[:, t, :], b[:, 12:13], lnp[:, 0:1024], ALU.subtract,
                                                  ALU.mult))
                    dve.scalar_tensor_tensor(h3[:, t, :], h3[:, t, :], b[:, 14:15], lnp[:, 1024:2048], ALU.mult,
                                             ALU.add).then_inc(ln_done, 1)

                def low_parts(qs):
                    for q in qs:
                        dve.wait_ge(tile_high, 2 * q.q + 1)
                        high, low = split_parts(q, nt)[0]
                        dve.tensor_tensor(low, (x3, g3)[i][:, q.k, 0:nt * P], high, ALU.subtract).then_inc(acts_low, 1)

                ahead = len(k_tiles[m]) // 2 + 4
                for n in range(2):
                    low_parts(k_tiles[m][:ahead] if n == 0 else k_tiles[m][ahead:])
                    for t in range(nt):
                        job = n * nt + t
                        if job == 0:
                            dve.wait_ge(ga_in, ga_before(m + 1))
                            dve.wait_ge(ln_in, 16 * (m + 1))
                        dve.wait_ge(acc_sum, 2 * tb + job + 1)
                        tmp = gtmp[:, job % 2, :]
                        hs = h3[:, t, n * 512:(n + 1) * 512]
                        dve.tensor_tensor(tmp, bank((job + 4) % 8), gav[:, int(t >= NLT), n * 512:(n + 1) * 512],
                                          ALU.mult).then_inc(acc_read, 1)
                        dve.wait_ge(acc_read, 2 * tb + job + 1)
                        step(dve.scalar_tensor_tensor(hs, hs, ALPHA, tmp, ALU.mult, ALU.add))
                        if n == 1:
                            b = bnb[:, (tb + t) % 3, :]
                            if tb + t >= 3:
                                dve.wait_ge(ln_done, tb + t - 2)
                            mark(dve.bn_stats(b[:, 0:6], h3[:, t, 0:512]))
                            step(dve.bn_stats(b[:, 6:12], h3[:, t, 512:1024]))
                            dve.bn_aggr(b[:, 12:14], b[:, 0:12]).then_inc(bn_ready, 1)
                            if t >= 1:
                                normalise(t - 1)
                normalise(nt - 1)

            def ffn(l):
                segs = ((0, SEQ), (SEQ, TOK)) if has_ctx(l) else ((0, SEQ),)
                dve.wait_ge(x_low, KT * (l + 1))
                if has_ctx(l):
                    dve.wait_ge(x_ctx, ctx_before[2 * l + 2])
                mods = [u for u in ups_of[l] if u.kind == "mod"]
                for u in ups_of[l]:
                    if u.kind == "up" and u.half == 0:
                        for q in mods[:2 if u.j < 2 else 1]:
                            mod_macs(q.key, q.mac)
                        mods = mods[2 if u.j < 2 else 1:]
                    if u.kind == "mod":
                        dve.wait_ge(mod_sum, MOD_FIRST + u.mac)
                        mod_out(u.l + 1, u.j, PS[u.pos][:, 0:4])
                        continue
                    jg = FT * l + u.j
                    y = (at, vt)[u.half][jg % 2]
                    jj = u.half * FT + u.j
                    ps = PS[u.pos]
                    dve.wait_ge(base_ready, u.c + 1)
                    for lo, hi in segs:
                        ins = dve.scalar_tensor_tensor(y[:, lo + 1:hi], ps[:, lo:hi - 1], convp[:, l, 0, jj:jj + 1],
                                                       y[:, lo + 1:hi], ALU.mult, ALU.add)
                        mark(ins)
                    dve.wait_ge(dve_step, steps[0])
                    for lo, hi in segs:
                        ins = dve.scalar_tensor_tensor(y[:, lo:hi - 1], ps[:, lo + 1:hi], convp[:, l, 2, jj:jj + 1],
                                                       y[:, lo:hi - 1], ALU.mult, ALU.add)
                    ins.then_inc(conv_done, 1)

            rs = [0]
            for l in range(DEPTH):
                modulate_context(2 * l)
                project(l)
                hgrn(l)
                attention(l)
                residual(2 * l)
                modulate_context(2 * l + 1)
                ffn(l)
                residual(2 * l + 1)

        @block.gpsimd
        def _(pool):
            steps = [0]

            def step(ins):
                steps[0] += 1
                ins.then_inc(pool_step, 1)
                pool.wait_ge(pool_step, steps[0])

            roots = [0]
            pool.wait_ge(halves, 1)

            def head_roots(l):
                for j in jobs_of[l]:
                    if j.rope and j.slot in (QB, KVB):
                        heads = 4 if j.slot == QB else 2
                        pool.wait_ge(ss_ready, roots[0] + 1)
                        for i in range(2):
                            ins = pool.tensor_tensor(rss[:, 8 + 4 * i:8 + 4 * i + heads], rss[:, 4 * i:4 * i + heads],
                                                     mhalf[:, 0:heads], ALU.pow)
                        ins.then_inc(root_ready, 1)
                        roots[0] += 1

            def hgrn(l):
                us = units_of[l]
                pool.wait_ge(e_in, e_end[l])
                for i in range(-3, len(us)):
                    if 0 <= i + 3 < len(us):
                        u = us[i + 3]
                        f = cz[u.d][:, u.b, u.t * P:(u.t + 1) * P]
                        y = YB[u.g % 2]
                        if u.g >= 2:
                            pool.wait_ge(subs, u.g - 1)
                        if u.g >= 4:
                            pool.wait_ge(ke, u.g - 3)
                        pool.tensor_scalar(y[:, 0:P], f, 2.0 ** -60, None, ALU.max)
                        step(pool.tensor_scalar(y[:, P:2 * P], f, 2.0 ** -60, 2.0 ** 60, ALU.min, ALU.mult))
                        pool.tensor_scalar(y[:, P:2 * P], y[:, P:2 * P], 2.0 ** -63, None, ALU.max)
                        pool.tensor_scalar(KB[u.g % 4], f, -1.0, 1.0, ALU.mult, ALU.add).then_inc(yk, 1)
                    if 0 <= i + 1 < len(us):
                        u = us[i + 1]
                        pool.wait_ge(expd, u.g + 1)
                        pool.wait_ge(yk, u.g + 1)
                        if u.g >= 2:
                            w = units[u.g - 2]
                            if w.out:
                                pool.wait_ge(o_sum, w.no + 1)
                            if w.state:
                                pool.wait_ge(kdt, w.ns + 1)
                        lo = 0 if u.out else 7
                        if u.out:
                            pool.tensor_tensor(QK[u.g % 2], cq[:, u.b, u.t * P:(u.t + 1) * P], KB[u.g % 4], ALU.mult)
                        pool.tensor_tensor(KE[u.g % 2][:, lo:8, :], EX[u.g % 2][:, 1 + lo:9, :],
                                           KB[u.g % 4].unsqueeze(1).broadcast_to([P, 8 - lo, P]), ALU.mult).then_inc(ke, 1)
                n = 2 * tiles(l) * 2
                pool.wait_ge(ro_sq, l + 1)
                step(pool.tensor_scalar(ross[:, 0:n], ross[:, 0:n], 1.0 / HD, EPS, ALU.mult, ALU.add))
                pool.tensor_tensor(ross[:, 0:n], ross[:, 0:n], mhalf[:, 0:n], ALU.pow).then_inc(ro_rstd, 1)

            def layer_norm(m):
                l, i = res[m]
                nt, tb = tiles(l), tiles_before[m]
                for q in k_tiles[m]:
                    pool.wait_ge(tile_high, 2 * q.q + 2)
                    high, low = split_parts(q, nt)[1]
                    pool.tensor_tensor(low, rows_of(q), high, ALU.subtract).then_inc(rows_low, 1)
                for t in range(nt):
                    b = bnb[:, (tb + t) % 3, :]
                    pool.wait_ge(bn_ready, tb + t + 1)
                    step(pool.tensor_scalar(b[:, 14:15], b[:, 13:14], EPS, None, ALU.add))
                    pool.tensor_tensor(b[:, 14:15], b[:, 14:15], mhalf[:, 0:1], ALU.pow).then_inc(rstd_ready, 1)

            def gated(l):
                n = TOK if has_ctx(l) else SEQ
                m = 2 * l + 1
                for k in range(KT):
                    pool.wait_ge(x_high, KT * l + k + 1)
                    pool.tensor_tensor(xl3[:, k, 0:SEQ], xv[:, k % 2, :], xh3[:, k, 0:SEQ],
                                       ALU.subtract).then_inc(x_low, 1)
                real = [u for u in ups_of[l] if u.kind == "up"]

                def low_part(u):
                    pool.wait_ge(w_high, u.c + 1)
                    pool.tensor_tensor(ws5[:, u.c % 2, 1], half_slot(u), ws5[:, u.c % 2, 0],
                                       ALU.subtract).then_inc(w_low, 1)

                low_part(real[0])
                low_part(real[1])
                for j in range(FT):
                    jg = FT * l + j
                    for u in real[2 * j + 4:2 * j + 6] if j else real[2:6]:
                        low_part(u)
                    pool.wait_ge(gate_ready, jg + 1)
                    pool.wait_ge(conv_done, 2 * jg + 2)
                    pool.tensor_tensor(g3[:, j, 0:n], sl[jg % 2][:, 0:n], vt[jg % 2][:, 0:n], ALU.mult).then_inc(hid_ready, 1)

            def pad_keys(l):
                if l:
                    pool.wait_ge(acc_sum, 2 * tiles_before[2 * l])
                    pool.wait_ge(rstd_ready, tiles_before[2 * l])
                for g in "ABD":
                    for hh in range(2):
                        ins = pool.memset(kT[g][64 * (1 - hh):64 * (1 - hh) + 64, hh::2, :], 0.0)
                ins.then_inc(padded, 1)

            for l in range(DEPTH):
                pad_keys(l)
                head_roots(l)
                hgrn(l)
                layer_norm(2 * l)
                gated(l)
                layer_norm(2 * l + 1)


def constants():
    import numpy as np

    f = np.float32
    t = np.arange(SEQ)
    pos = np.stack([t // GRID_W, t % GRID_W], -1).astype(f)
    nf = HD // 4
    inv = (f(10000.0) ** (-np.arange(nf, dtype=f) / f(nf))).astype(f)
    ang = (pos[:, :, None] * inv).astype(f)
    cos, sin = np.cos(ang), np.sin(ang)
    c = np.stack([cos, cos], 2).reshape(SEQ, HD)
    s = np.stack([-sin, sin], 2).reshape(SEQ, HD)
    rows = lambda a: a.reshape(NLT, P, HD).transpose(1, 0, 2).reshape(P, -1)
    i, j = np.arange(P)[:, None], np.arange(P)[None, :]
    am = np.concatenate([np.where(j >= i, 0, NEG), np.zeros((P, P)), np.where(j <= i, 0, NEG)], 1)
    cn = np.concatenate([np.eye(P), rows(c), rows(s), am], 1).astype(f)
    mk = np.zeros((P, 2, LEVELS, 64), f)
    for m in range(LEVELS):
        h = P >> (m + 1)
        same = (i // (2 * h)) == (j // (2 * h))
        late = (np.arange(P) % (2 * h)) >= h
        mk[:, 0, m, :] = (same & (i % (2 * h) < h))[:, late]
        mk[:, 1, m, :] = (same & (i % (2 * h) >= h))[:, ~late]
    return cn, mk.reshape(P, -1)


def kernel(x, c, ctx, c_ctx, w_mod, b_mod, w_in, w_out, ln_g, ln_b, attn_sink, qk_norm, hgrn_lb_logits,
           hgrn_onorm, na_rpb, ffn_w_up, ffn_conv_w, ffn_conv_b, ffn_w_down):
    import numpy as np
    import concourse.bacc as bacc
    from concourse.bass_utils import run_bass_kernel_spmd

    A = np.asarray
    f = np.float32
    w_mod, w_in, w_out, w_up, w_down = A(w_mod), A(w_in), A(w_out), A(ffn_w_up), A(ffn_w_down)
    weights = np.zeros((len(STREAM), P, SLOT), f)
    for n, (kind, l, i, g) in enumerate(STREAM):
        if kind == "up":
            w = w_up[l].reshape(KT, P, 2, FT, P)[:, :, :, i, :].transpose(1, 0, 2, 3)
        elif kind in ("mod", "in"):
            w = (w_mod if kind == "mod" else w_in)[l][:, i * 256:(i + 1) * 256].reshape(KT, P, 256).transpose(1, 0, 2)
            if kind == "in" and i in (QA, QB):
                w = w.reshape(P, KT, 2, 2, HD).transpose(0, 1, 3, 2, 4)
        else:
            w = (w_out if kind == "out" else w_down)[l][g * KDN * P:(g + 1) * KDN * P, i * 512:(i + 1) * 512]
            w = w.reshape(-1, P, 512).transpose(1, 0, 2)
        w = w.reshape(P, -1)
        weights[n, :, :w.shape[1]] = w
    cn, mk = constants()
    per = lambda a: np.moveaxis(a.reshape(a.shape[:-1] + (-1, P)), -1, 0)
    every = lambda a: np.broadcast_to(a.reshape(1, -1), (P, a.size))
    cv = np.stack([per(A(c)[0]), per(A(c_ctx))], -1)
    conv = np.concatenate([A(ffn_conv_w), A(ffn_conv_b)[:, None, :]], 1)
    lbl = per(A(hgrn_lb_logits)).transpose(0, 2, 1, 3)
    params = np.concatenate([q.reshape(P, -1) for q in (
        cv, per(A(b_mod)), per(conv), lbl, every(A(qk_norm)), every(A(hgrn_onorm)), every(A(attn_sink)))], 1)
    rpb = A(na_rpb)
    bias = np.full((DEPTH, 2, GRID_W, HEADS, BIAS_ROWS, GRID_W), NEG, f)
    for col in range(GRID_W):
        c0 = min(max(col - NA_COLS // 2, 0), GRID_W - NA_COLS)
        o0 = c0 - col + NA_COLS - 1
        for a in range(2):
            bias[:, a, col, :, :, c0:c0 + NA_COLS] = rpb[:, :, 1 - a:1 - a + BIAS_ROWS, o0:o0 + NA_COLS]
    bias = bias.reshape(DEPTH, P, HEADS, BIAS_ROWS * GRID_W)
    ln_rows = np.concatenate([A(ln_g), A(ln_b)], -1).reshape(2 * DEPTH, 2 * D_MODEL)
    arrays = {"weights": weights, "x": A(x)[0], "ctx": A(ctx)[0], "consts": cn, "masks": mk,
              "params": params, "bias": bias, "ln_rows": ln_rows}
    arrays = {k: np.ascontiguousarray(v) for k, v in arrays.items()}
    nc = bacc.Bacc("TRN2", target_bir_lowering=False, num_devices=1)
    aps = [nc.dram_tensor(f"in_{k}", v.shape, mybir.dt.from_np(v.dtype), kind="ExternalInput").ap()
           for k, v in arrays.items()]
    out = nc.dram_tensor("out_h", (SEQ, D_MODEL), mybir.dt.float32, kind="ExternalOutput").ap()
    hybrid_backbone(nc, *aps, out)
    r = run_bass_kernel_spmd(nc, [{f"in_{k}": v for k, v in arrays.items()}], core_ids=[0])
    return r.results[0]["out_h"].reshape(1, SEQ, D_MODEL)
```
